# Optimizing a Trainium2 kernel written in Bass

```python
import jax, jax.numpy as jnp
from jax import lax
import numpy as np

D_MODEL = 1024
BATCH = 1
SEQ = 2048
DEPTH = 2
DEC_BATCH = 8
DEC_SEQ = 4
PAST_LEN = 2048
PAGE_SIZE = 128

N_A_LAYERS = DEPTH // 2
N_B_LAYERS = DEPTH - N_A_LAYERS
GLA_HEADS = 4
GLA_DK = D_MODEL // 2
GLA_DV = D_MODEL
GLA_DK_HEAD = GLA_DK // GLA_HEADS
GLA_DV_HEAD = GLA_DV // GLA_HEADS
GLA_GATE_RANK = 16
GLA_TAU = 16.0
GLA_CHUNK = 64
SB_HEADS = 16
SB_HEAD_DIM = D_MODEL // SB_HEADS
SB_WIDTH = SB_HEADS * SB_HEAD_DIM
SB_BIAS_INIT = -7.0
Q_BLOCK = 128
RMS_EPS = 1e-6

kernel_name = "yoco_gla_stickbreaking_step"

def rmsnorm(x, g):
    xf = x.astype(jnp.float32)
    y = xf * lax.rsqrt(jnp.mean(xf * xf, axis=-1, keepdims=True) + RMS_EPS)
    return (y * g.astype(jnp.float32)).astype(x.dtype)

def gla_mixer(hn, s0, w_in, w_a2, b_a, g_head, w_out):
    Bn, T, _ = hn.shape
    f32 = jnp.float32
    proj = hn @ w_in
    q, k, v, g, lr = jnp.split(
        proj, [GLA_DK, 2 * GLA_DK, 2 * GLA_DK + GLA_DV, 2 * GLA_DK + 2 * GLA_DV], axis=-1)
    log_a = jax.nn.log_sigmoid((lr @ w_a2 + b_a).astype(f32)) / GLA_TAU
    L = min(GLA_CHUNK, T)
    nc = -(-T // L)
    pad = nc * L - T

    def chunks(a, dh):
        a = jnp.pad(a.astype(f32), ((0, 0), (0, pad), (0, 0)))
        return a.reshape(Bn, nc, L, GLA_HEADS, dh)

    qc = chunks(q, GLA_DK_HEAD) * (GLA_DK_HEAD ** -0.5)
    kc = chunks(k, GLA_DK_HEAD)
    vc = chunks(v, GLA_DV_HEAD)
    b = jnp.cumsum(chunks(log_a, GLA_DK_HEAD), axis=2)
    b_last = b[:, :, -1:]
    q_t = qc * jnp.exp(b)
    k_t = kc * jnp.exp(-b)
    k_e = kc * jnp.exp(b_last - b)
    causal = jnp.tril(jnp.ones((L, L), dtype=bool))
    p = jnp.einsum('bnihd,bnjhd->bnhij', q_t, k_t)
    p = jnp.where(causal, p, 0.0)
    o_intra = jnp.einsum('bnhij,bnjhe->bnihe', p, vc)
    ds = jnp.einsum('bnjhd,bnjhe->nbhde', k_e, vc)
    decay = jnp.exp(b_last[:, :, 0]).transpose(1, 0, 2, 3)

    def step(s, inp):
        d, dsn = inp
        return d[..., None] * s + dsn, s

    s_fin, s_entry = lax.scan(step, s0.astype(f32), (decay, ds))
    o_inter = jnp.einsum('bnihd,nbhde->bnihe', q_t, s_entry)
    o = (o_intra + o_inter).reshape(Bn, nc * L, GLA_HEADS, GLA_DV_HEAD)[:, :T]
    o = rmsnorm(o, g_head).reshape(Bn, T, GLA_DV) * jax.nn.silu(g.astype(f32))
    return o.astype(hn.dtype) @ w_out, s_fin.astype(s0.dtype)

def sb_block(q_blk, q_start, k, v, bias):
    qb = q_blk.shape[1]
    s_len = k.shape[1]
    q_pos = q_start + jnp.arange(qb)
    k_pos = jnp.arange(s_len)
    valid = k_pos[None, :] < q_pos[:, None]
    z = jnp.einsum('bqhd,bkhd->bhqk', q_blk, k) + bias[None, :, None, None]
    lneg = jnp.where(valid, jax.nn.log_sigmoid(-z), 0.0)
    suffix = lax.cumsum(lneg, axis=3, reverse=True) - lneg
    w = jnp.where(valid, jnp.exp(jax.nn.log_sigmoid(z) + suffix), 0.0)
    return jnp.einsum('bhqk,bkhd->bqhd', w, v)

def sb_attention(q, k, v, bias, q_offset):
    Bn, T, H, dh = q.shape
    qb = min(Q_BLOCK, T)
    nb = T // qb
    q_blocks = q.reshape(Bn, nb, qb, H, dh).transpose(1, 0, 2, 3, 4)
    starts = q_offset + qb * jnp.arange(nb, dtype=jnp.int32)
    bias = bias.astype(jnp.float32)
    out = lax.map(lambda a: sb_block(a[0], a[1], k, v, bias), (q_blocks, starts))
    return out.transpose(1, 0, 2, 3, 4).reshape(Bn, T, H, dh)

def run_trunk(x, s_init, past_k, past_v, pos0, g_norm_a, w_in_a, w_alpha2, b_alpha, g_head_a,
              w_out_a, g_kv, w_kv, g_norm_b, w_in_b, b_sb, w_out_b, g_final):
    Bn, T, _ = x.shape
    f32 = jnp.float32
    h = x
    new_s = []
    k_sh = v_sh = keys = vals = None
    for layer in range(DEPTH):
        if layer < N_A_LAYERS:
            i = layer
            out, s_new = gla_mixer(rmsnorm(h, g_norm_a[i]), s_init[i], w_in_a[i], w_alpha2[i],
                                   b_alpha[i], g_head_a[i], w_out_a[i])
            h = h + out
            new_s.append(s_new)
        else:
            if layer == N_A_LAYERS:
                kv = rmsnorm(h, g_kv) @ w_kv
                k_sh = kv[..., :SB_WIDTH].reshape(Bn, T, SB_HEADS, SB_HEAD_DIM)
                v_sh = kv[..., SB_WIDTH:].reshape(Bn, T, SB_HEADS, SB_HEAD_DIM)
                if past_k is None:
                    keys, vals = k_sh.astype(f32), v_sh.astype(f32)
                else:
                    keys = jnp.concatenate([past_k.astype(f32), k_sh.astype(f32)], axis=1)
                    vals = jnp.concatenate([past_v.astype(f32), v_sh.astype(f32)], axis=1)
            i = layer - N_A_LAYERS
            proj = rmsnorm(h, g_norm_b[i]) @ w_in_b[i]
            q = proj[..., :SB_WIDTH].reshape(Bn, T, SB_HEADS, SB_HEAD_DIM).astype(f32) * (SB_HEAD_DIM ** -0.5)
            gate = proj[..., SB_WIDTH:].astype(f32)
            o = sb_attention(q, keys, vals, b_sb[i], pos0).reshape(Bn, T, SB_WIDTH) * jax.nn.silu(gate)
            h = h + o.astype(h.dtype) @ w_out_b[i]
    return rmsnorm(h, g_final), jnp.stack(new_s), k_sh, v_sh

def setup_inputs(seed: int = 0) -> dict:
    key = jax.random.key(seed)
    ks = jax.random.split(key, 20)
    n_pages = PAST_LEN // PAGE_SIZE
    n_used = DEC_BATCH * n_pages
    n_phys = n_used + n_used // 4
    a_in = 2 * GLA_DK + 2 * GLA_DV + GLA_GATE_RANK
    nrm = jax.random.normal
    f32 = jnp.float32
    page_table = jax.random.permutation(ks[5], n_phys)[:n_used].reshape(DEC_BATCH, n_pages).astype(jnp.int32)
    return {
        "x_prompt": nrm(ks[0], (BATCH, SEQ, D_MODEL), f32),
        "x_sample": nrm(ks[1], (DEC_BATCH, DEC_SEQ, D_MODEL), f32),
        "state_gla": nrm(ks[2], (N_A_LAYERS, DEC_BATCH, GLA_HEADS, GLA_DK_HEAD, GLA_DV_HEAD), f32),
        "cache_k": nrm(ks[3], (n_phys, PAGE_SIZE, SB_HEADS, SB_HEAD_DIM), f32),
        "cache_v": nrm(ks[4], (n_phys, PAGE_SIZE, SB_HEADS, SB_HEAD_DIM), f32),
        "page_table": page_table,
        "g_norm_a": 1.0 + 0.05 * nrm(ks[6], (N_A_LAYERS, D_MODEL), f32),
        "w_in_a": nrm(ks[7], (N_A_LAYERS, D_MODEL, a_in), f32) * D_MODEL ** -0.5,
        "w_alpha2": nrm(ks[8], (N_A_LAYERS, GLA_GATE_RANK, GLA_DK), f32) * GLA_GATE_RANK ** -0.5,
        "b_alpha": 0.1 * nrm(ks[9], (N_A_LAYERS, GLA_DK), f32),
        "g_head_a": 1.0 + 0.05 * nrm(ks[10], (N_A_LAYERS, GLA_DV_HEAD), f32),
        "w_out_a": nrm(ks[11], (N_A_LAYERS, GLA_DV, D_MODEL), f32) * GLA_DV ** -0.5,
        "g_kv": 1.0 + 0.05 * nrm(ks[12], (D_MODEL,), f32),
        "w_kv": nrm(ks[13], (D_MODEL, 2 * SB_WIDTH), f32) * D_MODEL ** -0.5,
        "g_norm_b": 1.0 + 0.05 * nrm(ks[14], (N_B_LAYERS, D_MODEL), f32),
        "w_in_b": nrm(ks[15], (N_B_LAYERS, D_MODEL, 2 * SB_WIDTH), f32) * D_MODEL ** -0.5,
        "b_sb": SB_BIAS_INIT + 0.5 * nrm(ks[18], (N_B_LAYERS, SB_HEADS), f32),
        "w_out_b": nrm(ks[16], (N_B_LAYERS, SB_WIDTH, D_MODEL), f32) * SB_WIDTH ** -0.5,
        "g_final": 1.0 + 0.05 * nrm(ks[17], (D_MODEL,), f32),
    }

def reference(x_prompt, x_sample, state_gla, cache_k, cache_v, page_table, g_norm_a, w_in_a, w_alpha2,
              b_alpha, g_head_a, w_out_a, g_kv, w_kv, g_norm_b, w_in_b, b_sb, w_out_b, g_final):
    weights = (g_norm_a, w_in_a, w_alpha2, b_alpha, g_head_a, w_out_a, g_kv, w_kv, g_norm_b, w_in_b, b_sb,
               w_out_b, g_final)
    s_zero = jnp.zeros((N_A_LAYERS, x_prompt.shape[0], GLA_HEADS, GLA_DK_HEAD, GLA_DV_HEAD), x_prompt.dtype)
    y_prompt, state_gla_prompt, k_prompt, v_prompt = run_trunk(x_prompt, s_zero, None, None, 0, *weights)
    n_seq, n_pages = page_table.shape
    past_len = n_pages * cache_k.shape[1]
    past_k = cache_k[page_table].reshape(n_seq, past_len, SB_HEADS, SB_HEAD_DIM)
    past_v = cache_v[page_table].reshape(n_seq, past_len, SB_HEADS, SB_HEAD_DIM)
    y_sample, state_gla_sample, k_sample, v_sample = run_trunk(x_sample, state_gla, past_k, past_v, past_len, *weights)
    return (y_prompt, y_sample, state_gla_prompt, state_gla_sample, k_prompt, v_prompt, k_sample, v_sample)


_drawn_inputs = setup_inputs


def setup_inputs(seed=0):
    import zlib

    import numpy as np

    out = dict(_drawn_inputs(seed))
    spreads = {}
    factors = {'cache_k': 2.708, 'g_norm_b': 8.0, 'b_sb': 7.609}
    for name, (base, spread) in spreads.items():
        noise = np.random.default_rng([zlib.crc32(name.encode()), seed]).standard_normal(out[name].shape)
        drawn = base * np.exp(spread * noise) if base else spread * noise
        out[name] = __import__('jax').numpy.asarray(drawn.astype(out[name].dtype))
    for name, factor in factors.items():
        out[name] = (out[name] * factor).astype(out[name].dtype)
    return out
```

```python
from contextlib import ExitStack

import numpy as np

import concourse.bass as bass
from concourse import mybir

ALU = mybir.AluOpType
ACT = mybir.ActivationFunctionType
F32 = mybir.dt.float32
F32R = mybir.dt.float32r
BF16 = mybir.dt.bfloat16
I32 = mybir.dt.int32
ds = bass.ds

P = 128
D = 1024
KD = D // P
SEQ = 2048
NSEQ, TSEQ = 8, 4
SMP = NSEQ * TSEQ
TOK = SEQ + SMP
NT = SEQ // P
BANK = 512
NCH = SEQ // BANK
GH, DK, DV = 4, 128, 256
RANK = 16
CHUNK = 64
NCK = SEQ // CHUNK
TAU = 16.0
NH, HD = 16, 64
PAIRS = NH // 2
PAGE = 128
EPS = 1e-6
MASKED = -1e30


def over_tiles(engine, step):
    step(0, 0, 0)
    step(1, 0, 1)
    with engine.Fori(1, NT // 2) as i:
        step(i * 2, i, 0)
        step(i * 2 + 1, i, 1)
    step(NT, NT // 2, 0)


def is_sample(t):
    return isinstance(t, int) and t == NT


def rows_of(t):
    return SMP if is_sample(t) else P


def from_tile(t, n):
    return not isinstance(t, int) or t >= n


class Scope:

    def __init__(self, nc, stack, prefix):
        self.nc, self.stack, self.prefix, self.used = nc, stack, prefix, []
        stack.callback(self.close)

    def close(self):
        self.nc.clear_and_free_semaphores(self.used)
        self.nc.all_engine_barrier()

    def sb(self, name, shape, dt=F32):
        return self.stack.enter_context(self.nc.sbuf_tensor(f"{self.prefix}_{name}", shape, dt))

    def ps(self, name, shape, dt=F32):
        return self.stack.enter_context(self.nc.psum_tensor(f"{self.prefix}_{name}", shape, dt))

    def sem(self, name):
        sem = self.nc.alloc_semaphore(f"{self.prefix}_{name}")
        self.used.append(sem)
        return sem

    def sems(self, name, n):
        return [self.sem(f"{name}{i}") for i in range(n)]


def build_constants(nc, c):
    zeroed, c.consts_ready = c.scope.sem("zeroed"), c.scope.sem("consts_ready")
    c.ident = c.scope.sb("ident", [P, P])
    c.ident_bf = c.scope.sb("ident_bf", [P, P], BF16)
    c.diag_mask = c.scope.sb("diag_mask", [P, P], BF16)
    with nc.Block() as block:

        @block.gpsimd
        def _(pool):
            for t in (c.ident, c.ident_bf, c.diag_mask):
                pool.memset(t[:, :], 0.0).then_inc(zeroed, 1)
            pool.wait_ge(zeroed, 3)
            for t in (c.ident, c.ident_bf):
                pool.affine_select(out=t[:, :], in_=t[:, :], compare_op=ALU.not_equal, fill=1.0, base=0,
                                   pattern=[[-1, P]], channel_multiplier=1).then_inc(c.consts_ready, 1)
            pool.affine_select(out=c.diag_mask[:, :], in_=c.diag_mask[:, :], compare_op=ALU.is_gt, fill=MASKED,
                               base=0, pattern=[[-1, P]], channel_multiplier=1).then_inc(c.consts_ready, 1)


def normalise(nc, c, x_tile, xnT):
    with ExitStack() as stack:
        s = Scope(nc, stack, "norm")
        h = s.sb("h", [P, 2, D])
        square = s.sb("square", [P, D])
        xn = s.sb("xn", [P, 2, D])
        xT = s.sb("xT", [P, 2, KD, P])
        sumsq, root, rstd = (s.sb(n, [P, 2]) for n in ("sumsq", "root", "rstd"))
        eps = s.sb("eps", [P, 1])
        turned_ps = s.ps("turned", [P, 2, KD * P])
        h_in, xT_stored = s.sems("h_in", 2), s.sems("xT_stored", 2)
        eps_set, sumsq_made, root_made, rstd_made, xn_made, turned, act_copied, dve_copied = (
            s.sem(n) for n in ("eps_set", "sumsq_made", "root_made", "rstd_made", "xn_made", "turned",
                               "act_copied", "dve_copied"))
        block = stack.enter_context(nc.Block())
        half = KD // 2

        @block.sync
        def _(sp):
            def step(t, i, b):
                n = rows_of(t)
                if from_tile(t, 2):
                    sp.wait_ge(xn_made, t - 1)
                sp.dma_start(h[0:n, b, :], x_tile(t)).then_inc(h_in[b], 16)
            over_tiles(sp, step)

        @block.scalar
        def _(act):
            def copy(t, i, b):
                n = rows_of(t)
                act.wait_ge(turned, t + 1)
                if from_tile(t, 2):
                    act.wait_ge(xT_stored[b], 16 * i)
                act.activation(xT[:, b, 0:half, 0:n],
                               turned_ps[:, b, 0:half * P].rearrange("p (k n) -> p k n", n=P)[:, :, 0:n],
                               ACT.Copy).then_inc(act_copied, 1)

            def step(t, i, b):
                n = rows_of(t)
                act.wait_ge(h_in[b], 16 * i + 16)
                if from_tile(t, 2):
                    act.wait_ge(rstd_made, t - 1)
                act.activation(square[0:n, :], h[0:n, b, :], ACT.Square,
                               accum_out=sumsq[0:n, b:b + 1]).then_inc(sumsq_made, 1)
                act.wait_ge(sumsq_made, t + 1)
                act.activation(root[0:n, b:b + 1], sumsq[0:n, b:b + 1], ACT.Sqrt, scale=1.0 / D,
                               bias=eps[0:n, :]).then_inc(root_made, 1)
                if from_tile(t, 1):
                    copy(t - 1, i if b else i - 1, 1 - b)
            act.wait_ge(eps_set, 1)
            over_tiles(act, step)
            copy(NT, NT // 2, 0)

        @block.vector
        def _(dve):
            def copy(t, i, b):
                n = rows_of(t)
                dve.wait_ge(turned, t + 1)
                if from_tile(t, 2):
                    dve.wait_ge(xT_stored[b], 16 * i)
                dve.tensor_scalar(xT[:, b, half:KD, 0:n],
                                  turned_ps[:, b, half * P:].rearrange("p (k n) -> p k n", n=P)[:, :, 0:n],
                                  1.0, None, ALU.mult).then_inc(dve_copied, 1)

            def step(t, i, b):
                n = rows_of(t)
                dve.wait_ge(root_made, t + 1)
                dve.reciprocal(rstd[0:n, b:b + 1], root[0:n, b:b + 1]).then_inc(rstd_made, 1)
                dve.wait_ge(rstd_made, t + 1)
                if from_tile(t, 2):
                    dve.wait_ge(turned, t - 1)
                dve.tensor_scalar(xn[0:n, b, :], h[0:n, b, :], rstd[0:n, b:b + 1], None,
                                  ALU.mult).then_inc(xn_made, 1)
                if from_tile(t, 1):
                    copy(t - 1, i if b else i - 1, 1 - b)
            dve.memset(eps[:, :], EPS).then_inc(eps_set, 1)
            over_tiles(dve, step)
            copy(NT, NT // 2, 0)

        @block.tensor
        def _(pe):
            def step(t, i, b):
                n = rows_of(t)
                pe.wait_ge(xn_made, t + 1)
                if from_tile(t, 2):
                    pe.wait_ge(act_copied, t - 1)
                    pe.wait_ge(dve_copied, t - 1)
                for k in range(KD):
                    mm = pe.transpose(turned_ps[:, b, k * P:k * P + n], xn[0:n, b, k * P:(k + 1) * P],
                                      c.ident[0:n, 0:n])
                mm.then_inc(turned, 1)
            over_tiles(pe, step)

        @block.gpsimd
        def _(pool):
            def step(t, i, b):
                n = rows_of(t)
                pool.wait_ge(act_copied, t + 1)
                pool.wait_ge(dve_copied, t + 1)
                pool.wait_ge(eps_set, 1)
                col = ds(t * P, n)
                pool.dma_start(xnT.rearrange("(k p) n -> p k n", p=P)[:, :, col],
                               xT[:, b, :, 0:n]).then_inc(xT_stored[b], 16)
            over_tiles(pool, step)
            pool.wait_ge(xT_stored[0], 16 * (NT // 2 + 1))
            pool.wait_ge(xT_stored[1], 16 * (NT // 2))


def project(nc, c, name, xnT, jobs, tail=None):
    with ExitStack() as stack:
        s = Scope(nc, stack, name)
        slab = s.sb("slab", [P, 2, TOK])
        x_hi, x_lo = (s.sb(n, [P, KD, TOK], F32R) for n in ("x_hi", "x_lo"))
        w_raw = s.sb("w_raw", [P, 2, KD, P])
        w_scaled = s.sb("w_scaled", [P, KD, P])
        w_hi, w_lo = (s.sb(n, [P, 2, KD, P], F32R) for n in ("w_hi", "w_lo"))
        gain = s.sb("gain", [P, len(jobs), KD])
        out = s.sb("out", [P, 2, TOK])
        acc = s.ps("acc", [P, NCH + 1, BANK])
        slab_in, w_in, stored = s.sems("slab_in", 2), s.sems("w_in", 2), s.sems("stored", 2)
        gain_in = s.sem("gain_in")
        x_hi_made, x_lo_made, w_scaled_made, w_hi_made, w_lo_made, chunk_done, copied = (
            s.sem(n) for n in ("x_hi_made", "x_lo_made", "w_scaled_made", "w_hi_made", "w_lo_made",
                               "chunk_done", "copied"))
        block = stack.enter_context(nc.Block())
        spans = [(q * BANK, BANK) for q in range(NCH)] + [(SEQ, SMP)]
        n_spans = len(spans)

        def over_blocks(engine, step):
            done = 0
            for j, (_, _, blocks, _, _) in enumerate(jobs):
                first = 0
                if done == 0:
                    step(j, 0, 0, 0, 0, P)
                    step(j, 1, 1, 0, 1, P)
                    first = 1
                with engine.Fori(first, blocks // 2) as i:
                    step(j, i * 2, i * 2 + done, i + done // 2, 0, P)
                    step(j, i * 2 + 1, i * 2 + 1 + done, i + done // 2, 1, P)
                done += blocks
            if tail:
                step(len(jobs) - 1, jobs[-1][2], done, done // 2, 0, tail)

        @block.sync
        def _(sp):
            for j, (_, g, _, _, _) in enumerate(jobs):
                sp.dma_start(gain[:, j, :], g.rearrange("(k p) -> p k", p=P), allow_slow_non_contiguous=True).then_inc(gain_in, 16)
            for k in range(KD):
                if k >= 2:
                    sp.wait_ge(x_lo_made, k - 1)
                sp.dma_start(slab[:, k % 2, :], xnT[k * P:(k + 1) * P, :]).then_inc(slab_in[k % 2], 16)

            def step(j, jb, n, i, b, width):
                if from_tile(n, 2):
                    sp.wait_ge(w_scaled_made, n - 1)
                src = jobs[j][0].rearrange("(k p) n -> p k n", p=P)[:, :, ds(jb * P, width)]
                sp.dma_start(w_raw[:, b, :, 0:width], src).then_inc(w_in[b], 16)
            over_blocks(sp, step)

        @block.scalar
        def _(act):
            for k in range(KD):
                act.wait_ge(slab_in[k % 2], 16 * (k // 2 + 1))
                act.activation(x_hi[:, k, :], slab[:, k % 2, :], ACT.Copy).then_inc(x_hi_made, 1)

            def step(j, jb, n, i, b, width):
                for q, (at, size) in enumerate(spans):
                    act.wait_ge(chunk_done, n * n_spans + (q + 1))
                    if q == 0 and from_tile(n, 2):
                        act.wait_ge(stored[b], 16 * i)
                    act.activation(out[:, b, at:at + size], acc[:, q, 0:size], ACT.Copy).then_inc(copied, 1)
            over_blocks(act, step)

        @block.vector
        def _(dve):
            for k in range(KD):
                dve.wait_ge(x_hi_made, k + 1)
                dve.tensor_tensor(x_lo[:, k, :], slab[:, k % 2, :], x_hi[:, k, :].bitcast(F32),
                                  ALU.subtract).then_inc(x_lo_made, 1)
            dve.wait_ge(gain_in, 16 * len(jobs))

            def step(j, jb, n, i, b, width):
                dve.wait_ge(w_in[b], 16 * i + 16)
                if from_tile(n, 1):
                    dve.wait_ge(w_lo_made, n)
                dve.tensor_tensor(w_scaled[:, :, 0:width], w_raw[:, b, :, 0:width],
                                  gain[:, j, :].unsqueeze(2).broadcast_to([P, KD, width]),
                                  ALU.mult).then_inc(w_scaled_made, 1)
                dve.wait_ge(w_scaled_made, n + 1)
                if from_tile(n, 2):
                    dve.wait_ge(chunk_done, (n - 1) * n_spans)
                dve.tensor_copy(w_hi[:, b, :, 0:width], w_scaled[:, :, 0:width]).then_inc(w_hi_made, 1)
                dve.wait_ge(w_hi_made, n + 1)
                dve.tensor_tensor(w_lo[:, b, :, 0:width], w_scaled[:, :, 0:width],
                                  w_hi[:, b, :, 0:width].bitcast(F32), ALU.subtract).then_inc(w_lo_made, 1)
            over_blocks(dve, step)

        @block.tensor
        def _(pe):
            pe.wait_ge(x_lo_made, KD)

            def step(j, jb, n, i, b, width):
                pe.wait_ge(w_lo_made, n + 1)
                for q, (at, size) in enumerate(spans):
                    if from_tile(n, 1):
                        pe.wait_ge(copied, (n - 1) * n_spans + (q + 1))
                    for k in range(KD):
                        for w, x in ((w_hi, x_hi), (w_lo, x_hi), (w_hi, x_lo)):
                            mm = pe.matmul(acc[:, q, 0:size], w[:, b, k, :], x[:, k, at:at + size],
                                           start=(k == 0 and w is w_hi and x is x_hi),
                                           stop=(k == KD - 1 and x is x_lo))
                    mm.then_inc(chunk_done, 1)
            over_blocks(pe, step)

        @block.gpsimd
        def _(pool):
            def step(j, jb, n, i, b, width):
                pool.wait_ge(copied, n * n_spans + n_spans)
                pool.wait_ge(gain_in, 16 * len(jobs))
                _, _, _, dst, row = jobs[j]
                pool.dma_start(dst[ds(jb * P + row, width), :], out[0:width, b, :]).then_inc(stored[b], 16)
            over_blocks(pool, step)
            total = sum(j[2] for j in jobs)
            pool.wait_ge(stored[0], 16 * (total // 2 + (1 if tail else 0)))
            pool.wait_ge(stored[1], 16 * (total // 2))


def gla(nc, c, projT, w_alpha2, b_alpha, g_head, state_in, state_prompt, state_sample, o_out):
    q_rows, k_rows, v_rows, g_rows, r_rows = 0, GH * DK, 2 * GH * DK, 2 * GH * DK + GH * DV, 2 * GH * DK + 2 * GH * DV
    scale = float(np.float32(DK ** -0.5))
    spans = [(i * BANK, BANK) for i in range(NCH)] + [(SEQ, SMP)]
    with ExitStack() as stack:
        s = Scope(nc, stack, "gla")
        qT, kT, ktT = (s.sb(n, [P, TOK]) for n in ("qT", "kT", "ktT"))
        vgT = s.sb("vgT", [P, 4, TOK])
        rT = s.sb("rT", [RANK, TOK])
        logit, work, b_sum, gap = (s.sb(n, [P, TOK]) for n in ("logit", "work", "b_sum", "gap"))
        keep = s.sb("keep", [P, TOK])
        w2, bias = s.sb("w2", [RANK, DK]), s.sb("bias", [P, 1])
        decay = s.sb("decay", [P, NCK])
        decay_smp = s.sb("decay_smp", [P, NSEQ])
        vg = s.sb("vg", [P, NT + 1, 2 * DV])
        o = s.sb("o", [P, NT + 1, DV])
        square = s.sb("square", [P, DV])
        ke = s.sb("ke", [P, 2, P])
        pT = s.sb("pT", [P, 2, P])
        S = s.sb("S", [P, 4, DV])
        s_in, s_new = s.sb("s_in", [P, NSEQ, DV]), s.sb("s_new", [P, NSEQ, DV])
        ke_smp, pT_smp = s.sb("ke_smp", [SMP, NSEQ, P]), s.sb("pT_smp", [SMP, SMP])
        q_smp = s.sb("q_smp", [P, NSEQ, SMP])
        tok_mask = s.sb("tok_mask", [P, NSEQ, SMP])
        row_mask = s.sb("row_mask", [SMP, NSEQ])
        may, may_smp = s.sb("may", [P, P], I32), s.sb("may_smp", [SMP, SMP], I32)
        mask_work = s.sb("mask_work", [P, P])
        g_gain = s.sb("g_gain", [P, DV])
        sumsq, root, rstd = (s.sb(n, [P, NT + 1]) for n in ("sumsq", "root", "rstd"))
        eps = s.sb("eps", [P, 1])
        tok_ps, kp_ps, o_ps, ds_ps = (s.ps(n, [P, 2, BANK]) for n in ("tok", "kp", "o_acc", "ds"))
        gate = s.sem("head_gate")
        loads = ("q", "k", "v", "g", "w2", "b", "s0")
        ld = {n: s.sem(f"in_{n}") for n in loads}
        once = s.sem("once_in")
        masks, logit_mm, logit_cp, prep, expd, tok_t, tok_cp, kp_t, ke_cp, pt_cp, ds_mm, s_made, o_mm, o_cp, \
            smp_made, ds_smp, s_smp, sum_made, root_made, rstd_made, normed, gated, st = (s.sem(n) for n in (
                "masks", "logit_mm", "logit_cp", "prep", "expd", "tok_t", "tok_cp", "kp_t", "ke_cp", "pt_cp", "ds_mm",
                "s_made", "o_mm", "o_cp", "smp_made", "ds_smp", "s_smp", "sum_made", "root_made", "rstd_made",
                "normed", "gated", "stored"))
        s_zero = s.sem("s_zero")
        N_PREP, N_EXP = 9, 8
        n_stores = 4

        with nc.Block() as block:
            @block.gpsimd
            def _(pool):
                pool.memset(keep[:, :], 1.0).then_inc(masks, 1)
                pool.memset(tok_mask[:, :, :], 1.0).then_inc(masks, 1)
                pool.memset(row_mask[:, :], 1.0).then_inc(masks, 1)
                pool.memset(mask_work[:, :], 1.0).then_inc(masks, 1)
                pool.memset(may[:, :], 0).then_inc(masks, 1)
                pool.wait_ge(masks, 5)
                pool.affine_select(out=keep[:, 0:SEQ], in_=keep[:, 0:SEQ], compare_op=ALU.not_equal, fill=0.0, base=0,
                                   pattern=[[0, NCK], [1, CHUNK]], channel_multiplier=0).then_inc(masks, 1)
                pool.affine_select(out=keep[:, SEQ:], in_=keep[:, SEQ:], compare_op=ALU.not_equal, fill=0.0, base=0,
                                   pattern=[[0, NSEQ], [1, TSEQ]], channel_multiplier=0).then_inc(masks, 1)
                pool.affine_select(out=tok_mask[:, :, :], in_=tok_mask[:, :, :], compare_op=ALU.is_ge, fill=0.0,
                                   base=0, pattern=[[-TSEQ, NSEQ], [1, SMP]], channel_multiplier=0).then_inc(masks, 1)
                pool.affine_select(out=row_mask[:, :], in_=row_mask[:, :], compare_op=ALU.is_ge, fill=0.0,
                                   base=0, pattern=[[-TSEQ, NSEQ]], channel_multiplier=1).then_inc(masks, 1)
                pool.affine_select(out=mask_work[:, :], in_=mask_work[:, :], compare_op=ALU.is_ge, fill=0.0,
                                   base=0, pattern=[[1, P]], channel_multiplier=-1).then_inc(masks, 1)
                pool.wait_ge(masks, 10)
                pool.affine_select(out=tok_mask[:, :, :], in_=tok_mask[:, :, :], compare_op=ALU.is_gt, fill=0.0,
                                   base=TSEQ, pattern=[[TSEQ, NSEQ], [-1, SMP]], channel_multiplier=0).then_inc(masks, 1)
                pool.affine_select(out=row_mask[:, :], in_=row_mask[:, :], compare_op=ALU.is_gt, fill=0.0,
                                   base=TSEQ, pattern=[[TSEQ, NSEQ]], channel_multiplier=-1).then_inc(masks, 1)
                pool.memset(mask_work[0:CHUNK, CHUNK:], 0.0).then_inc(masks, 1)

            @block.vector
            def _(dve):
                dve.memset(pT[:, :, :], 0.0)
                dve.memset(pT_smp[:, :], 0.0)
                dve.memset(eps[:, :], EPS)
                dve.wait_ge(masks, 13)
                dve.tensor_copy(may[:, :], mask_work[:, :]).then_inc(prep, 1)
                dve.wait_ge(prep, 1)
                dve.tensor_tensor(ke_smp[:, :, 0:SMP], tok_mask[0:SMP, :, :],
                                  row_mask[:, :].unsqueeze(2).broadcast_to([SMP, NSEQ, SMP]), ALU.mult).then_inc(prep, 1)
                dve.wait_ge(prep, 2)
                dve.tensor_reduce(mask_work[0:SMP, 0:SMP], ke_smp[:, :, 0:SMP].rearrange("p s n -> p n s"),
                                  mybir.AxisListType.X, ALU.add).then_inc(prep, 1)
                dve.wait_ge(prep, 3)
                dve.tensor_tensor(mask_work[0:SMP, SMP:2 * SMP], mask_work[0:SMP, 0:SMP], may[0:SMP, 0:SMP],
                                  ALU.mult).then_inc(prep, 1)
                dve.wait_ge(prep, 4)
                dve.tensor_copy(may_smp[:, :], mask_work[0:SMP, SMP:2 * SMP]).then_inc(prep, 1)

            @block.sync
            def _(sp):
                sp.dma_start(rT[:, :], projT[r_rows:r_rows + RANK, :]).then_inc(once, 16)
                sp.dma_start(g_gain[:, :], g_head.unsqueeze(0).broadcast_to([P, DV])).then_inc(once, 16)
                sp.wait_ge(once, 32)
        PREP0 = 5

        def out_of(act, h, t):
            n, b = rows_of(t), t % 2
            act.wait_ge(o_mm, h * (NT + 1) + (t + 1))
            if t >= 1:
                act.wait_ge(sum_made, h * (NT + 1) + t)
            act.activation(square[0:n, :], o_ps[0:n, b, 0:DV], ACT.Square,
                           accum_out=sumsq[0:n, t:t + 1]).then_inc(sum_made, 1)
            act.activation(o[0:n, t, :], o_ps[0:n, b, 0:DV], ACT.Copy).then_inc(o_cp, 1)

        def states(dve, h, t):
            for half in range(2):
                ck = 2 * t + half
                dve.wait_ge(ds_mm, h * NCK + (ck + 1))
                if t >= 1:
                    dve.wait_ge(o_mm, h * (NT + 1) + t)
                if ck >= 1:
                    dve.wait_ge(s_made, h * NCK + ck)
                else:
                    dve.wait_ge(s_zero, h + 1)
                dve.scalar_tensor_tensor(out=S[:, (ck + 1) % 4, :], in0=S[:, ck % 4, :], scalar=decay[:, ck:ck + 1],
                                         in1=ds_ps[:, half, 0:DV], op0=ALU.mult, op1=ALU.add).then_inc(s_made, 1)

        block = stack.enter_context(nc.Block())

        @block.sync
        def _(sp):
            sp.sem_inc(gate, 1)
            with sp.Fori(0, GH) as h:
                sp.wait_ge(gate, h * 4 + 4)
                sp.wait_ge(once, 32)
                sp.dma_start(w2[:, :], w_alpha2[:, ds(h * DK, DK)]).then_inc(ld["w2"], 16)
                sp.dma_start(bias[:, :], b_alpha.rearrange("(n o) -> n o", o=1)[ds(h * DK, DK), :]).then_inc(ld["b"], 16)
                sp.dma_start(qT[:, :], projT[ds(h * DK + q_rows, DK), :]).then_inc(ld["q"], 16)
                sp.dma_start(kT[:, :], projT[ds(h * DK + k_rows, DK), :]).then_inc(ld["k"], 16)
                sp.dma_start(vgT[:, 2:4, :], projT[ds(h * DV + g_rows, DV), :].rearrange("(b p) n -> p b n", p=P)
                             ).then_inc(ld["g"], 16)
                sp.dma_start(vgT[:, 0:2, :], projT[ds(h * DV + v_rows, DV), :].rearrange("(b p) n -> p b n", p=P)
                             ).then_inc(ld["v"], 16)
                sp.dma_start(s_in[:, :, :].unsqueeze(2), state_in.rearrange("s h k v -> k s h v")[:, :, ds(h, 1), :]).then_inc(ld["s0"], 16)
                sp.wait_ge(s_made, h * NCK + NCK)
                sp.dma_start(state_prompt.rearrange("h k v -> k h v")[:, ds(h, 1), :], S[:, 0:1, :]).then_inc(st, 16)
                sp.wait_ge(gated, h * 2 + 2)
                sp.wait_ge(s_smp, h * NSEQ + NSEQ)
                sp.dma_start(state_sample.rearrange("s h k v -> k s h v")[:, :, ds(h, 1), :],
                             s_new[:, :, :].unsqueeze(2)).then_inc(st, 16)
                sp.dma_start(o_out[0:SEQ, :].rearrange("(t p) n -> p t n", p=P)[:, :, ds(h * DV, DV)],
                             o[:, 0:NT, :]).then_inc(st, 16)
                sp.dma_start(o_out[SEQ:TOK, ds(h * DV, DV)], o[0:SMP, NT, :]).then_inc(st, 16)
                sp.wait_ge(st, h * (16 * n_stores) + 16 * n_stores)
                sp.sem_inc(gate, 1)

        @block.tensor
        def _(pe):
            pe.sem_inc(gate, 1)
            logit_banks = [tok_ps[:, 0], tok_ps[:, 1], o_ps[:, 0], o_ps[:, 1], kp_ps[:, 0]]
            with pe.Fori(0, GH) as h:
                pe.wait_ge(gate, h * 4 + 4)
                pe.wait_ge(ld["w2"], h * 16 + 16)
                for (at, n), bank in zip(spans, logit_banks):
                    pe.matmul(bank[:, 0:n], w2[:, :], rT[:, at:at + n], start=True, stop=True).then_inc(logit_mm, 1)

                def to_tokens(t):
                    n, at = rows_of(t), t * P
                    b = t % 2
                    if t >= 2:
                        pe.wait_ge(tok_cp, h * (NT + 1) + (t - 1))
                    for j in range(4):
                        mm = pe.transpose(tok_ps[0:n, b, j * P:(j + 1) * P], vgT[:, j, at:at + n], c.ident[:, :])
                    mm.then_inc(tok_t, 1)
                    if t >= 2:
                        pe.wait_ge(ke_cp, h * (NT + 1) + (t - 1))
                        pe.wait_ge(pt_cp, h * (NT + 1) + (t - 1))
                    pe.transpose(kp_ps[0:n, b, 0:P], kT[:, at:at + n], c.ident[:, :])
                    pe.matmul(kp_ps[0:n, b, P:P + n], ktT[:, at:at + n], qT[:, at:at + n],
                              start=True, stop=True).then_inc(kp_t, 1)

                pe.wait_ge(prep, h * N_PREP + (PREP0 + N_PREP))
                pe.wait_ge(ld["v"], h * 16 + 16)
                pe.wait_ge(logit_cp, h * 5 + 5)
                to_tokens(0)
                for t in range(NT):
                    to_tokens(t + 1)
                    b = t % 2
                    pe.wait_ge(tok_cp, h * (NT + 1) + (t + 1))
                    pe.wait_ge(ke_cp, h * (NT + 1) + (t + 1))
                    pe.wait_ge(pt_cp, h * (NT + 1) + (t + 1))
                    if t >= 1:
                        pe.wait_ge(s_made, h * NCK + 2 * t)
                    for half in range(2):
                        r = slice(half * CHUNK, (half + 1) * CHUNK)
                        pe.matmul(ds_ps[:, half, 0:DV], ke[r, b, :], vg[r, t, 0:DV], start=True,
                                  stop=True).then_inc(ds_mm, 1)
                    if t >= 2:
                        pe.wait_ge(o_cp, h * (NT + 1) + (t - 1))
                    pe.matmul(o_ps[:, b, 0:DV], pT[:, b, :], vg[:, t, 0:DV], start=True, stop=True)
                    for half in range(2):
                        ck = 2 * t + half
                        if ck >= 1:
                            pe.wait_ge(s_made, h * NCK + ck)
                        else:
                            pe.wait_ge(s_zero, h + 1)
                        r = slice(half * CHUNK, (half + 1) * CHUNK)
                        mm = pe.matmul(o_ps[r, b, 0:DV], qT[:, ck * CHUNK:(ck + 1) * CHUNK], S[:, ck % 4, :],
                                       start=False, stop=True, skip_group_check=True)
                    mm.then_inc(o_mm, 1)
                t, b = NT, NT % 2
                pe.wait_ge(tok_cp, h * (NT + 1) + (t + 1))
                pe.wait_ge(pt_cp, h * (NT + 1) + (t + 1))
                pe.wait_ge(o_cp, h * (NT + 1) + (t - 1))
                pe.wait_ge(smp_made, h * 2 + 2)
                pe.wait_ge(ld["s0"], h * 16 + 16)
                for q in range(NSEQ):
                    pe.matmul(o_ps[0:SMP, b, 0:DV], q_smp[:, q, :], s_in[:, q, :], start=(q == 0), stop=False)
                mm = pe.matmul(o_ps[0:SMP, b, 0:DV], pT_smp[:, :], vg[0:SMP, t, 0:DV], start=False, stop=True)
                mm.then_inc(o_mm, 1)
                pe.wait_ge(s_made, h * NCK + NCK)
                for q in range(NSEQ):
                    if q >= 2:
                        pe.wait_ge(s_smp, h * NSEQ + (q - 1))
                    pe.matmul(ds_ps[:, q % 2, 0:DV], ke_smp[:, q, :], vg[0:SMP, t, 0:DV], start=True,
                              stop=True).then_inc(ds_smp, 1)
                pe.wait_ge(ds_smp, h * NSEQ + NSEQ)
                pe.wait_ge(o_mm, h * (NT + 1) + (NT + 1))
                pe.sem_inc(gate, 1)

        @block.scalar
        def _(act):
            act.sem_inc(gate, 1)
            with act.Fori(0, GH) as h:
                act.wait_ge(gate, h * 4 + 4)
                e0 = h * N_EXP
                act.wait_ge(prep, h * N_PREP + (PREP0 + 1))
                act.activation(work[:, :], work[:, :], ACT.Exp, scale=-1.0).then_inc(expd, 1)
                act.wait_ge(expd, e0 + 1)
                act.activation(work[:, :], work[:, :], ACT.Ln, bias=1.0).then_inc(expd, 1)
                act.wait_ge(prep, h * N_PREP + (PREP0 + 3))
                act.activation(work[:, :], b_sum[:, :], ACT.Exp, scale=1.0 / TAU).then_inc(expd, 1)
                act.activation(logit[:, :], b_sum[:, :], ACT.Exp, scale=-1.0 / TAU).then_inc(expd, 1)
                act.activation(decay[:, :], b_sum[:, CHUNK - 1:SEQ:CHUNK], ACT.Exp, scale=1.0 / TAU)
                act.activation(decay_smp[:, :], b_sum[:, SEQ + TSEQ - 1:TOK:TSEQ], ACT.Exp,
                               scale=1.0 / TAU).then_inc(expd, 1)
                act.wait_ge(prep, h * N_PREP + (PREP0 + 5))
                act.activation(gap[:, :], gap[:, :], ACT.Exp, scale=1.0 / TAU).then_inc(expd, 1)
                act.wait_ge(ld["g"], h * 16 + 16)
                for j, (dst, ready) in enumerate(((work, 6), (b_sum, 5))):
                    act.wait_ge(prep, h * N_PREP + (PREP0 + ready))
                    act.wait_ge(expd, e0 + 5)
                    act.activation(dst[:, :], vgT[:, 2 + j, :], ACT.Sigmoid).then_inc(expd, 1)
                for t in range(NT + 1):
                    n, b = rows_of(t), t % 2
                    act.wait_ge(tok_t, h * (NT + 1) + (t + 1))
                    act.activation(vg[0:n, t, :], tok_ps[0:n, b, :], ACT.Copy).then_inc(tok_cp, 1)
                    if t >= 1:
                        out_of(act, h, t - 1)
                out_of(act, h, NT)
                act.wait_ge(sum_made, h * (NT + 1) + (NT + 1))
                act.activation(root[:, 0:NT], sumsq[:, 0:NT], ACT.Sqrt, scale=1.0 / DV, bias=eps[:, :])
                act.activation(root[0:SMP, NT:], sumsq[0:SMP, NT:], ACT.Sqrt, scale=1.0 / DV,
                               bias=eps[0:SMP, :]).then_inc(root_made, 1)
                act.wait_ge(root_made, h + 1)
                act.sem_inc(gate, 1)

        @block.vector
        def _(dve):
            dve.sem_inc(gate, 1)
            with dve.Fori(0, GH) as h:
                dve.wait_ge(gate, h * 4 + 4)
                dve.wait_ge(ld["b"], h * 16 + 16)
                banks = [tok_ps[:, 0], tok_ps[:, 1], o_ps[:, 0], o_ps[:, 1], kp_ps[:, 0]]
                for j, ((at, n), bank) in enumerate(zip(spans, banks)):
                    dve.wait_ge(logit_mm, h * 5 + (j + 1))
                    dve.tensor_scalar(logit[:, at:at + n], bank[:, 0:n], bias[:, 0:1], None,
                                      ALU.add).then_inc(logit_cp, 1)
                p0, e0 = h * N_PREP, h * N_EXP
                dve.wait_ge(logit_cp, h * 5 + 5)
                dve.scalar_tensor_tensor(out=work[:, :], in0=logit[:, :], scalar=-1.0, in1=logit[:, :], op0=ALU.mult,
                                         op1=ALU.max).then_inc(prep, 1)
                dve.wait_ge(expd, e0 + 2)
                dve.wait_ge(prep, p0 + (PREP0 + 1))
                dve.scalar_tensor_tensor(out=logit[:, :], in0=logit[:, :], scalar=0.0, in1=work[:, :], op0=ALU.min,
                                         op1=ALU.subtract).then_inc(prep, 1)
                dve.wait_ge(prep, p0 + (PREP0 + 2))
                dve.tensor_tensor_scan(b_sum[:, :], keep[:, :], logit[:, :], 0.0, ALU.mult, ALU.add).then_inc(prep, 1)
                dve.wait_ge(prep, p0 + (PREP0 + 3))
                for lo, n, size in ((0, NCK, CHUNK), (SEQ, NSEQ, TSEQ)):
                    v = b_sum[:, lo:lo + n * size].rearrange("p (c l) -> p c l", l=size)
                    dve.tensor_tensor(gap[:, lo:lo + n * size].rearrange("p (c l) -> p c l", l=size),
                                      v[:, :, size - 1:size].broadcast_to([P, n, size]), v,
                                      ALU.subtract).then_inc(prep, 1)
                dve.wait_ge(ld["q"], h * 16 + 16)
                dve.wait_ge(expd, e0 + 5)
                dve.scalar_tensor_tensor(out=qT[:, :], in0=qT[:, :], scalar=scale, in1=work[:, :], op0=ALU.mult,
                                         op1=ALU.mult).then_inc(prep, 1)
                dve.wait_ge(ld["k"], h * 16 + 16)
                dve.tensor_tensor(ktT[:, :], kT[:, :], logit[:, :], ALU.mult).then_inc(prep, 1)
                dve.wait_ge(expd, e0 + 6)
                dve.wait_ge(prep, p0 + (PREP0 + 7))
                dve.tensor_tensor(kT[:, :], kT[:, :], gap[:, :], ALU.mult).then_inc(prep, 1)
                dve.wait_ge(expd, e0 + 8)
                dve.tensor_tensor(vgT[:, 2, :], vgT[:, 2, :], work[:, :], ALU.mult)
                dve.tensor_tensor(vgT[:, 3, :], vgT[:, 3, :], b_sum[:, :], ALU.mult).then_inc(prep, 1)
                dve.memset(S[:, 0, :], 0.0).then_inc(s_zero, 1)
                for t in range(NT + 1):
                    n, b = rows_of(t), t % 2
                    dve.wait_ge(kp_t, h * (NT + 1) + (t + 1))
                    if 2 <= t < NT:
                        dve.wait_ge(o_mm, h * (NT + 1) + (t - 1))
                        dve.wait_ge(ds_mm, h * NCK + 2 * (t - 1))
                    if t == NT:
                        dve.wait_ge(ds_mm, h * NCK + 2 * (t - 1))
                    dve.tensor_copy(ke[0:n, b, :], kp_ps[0:n, b, 0:P]).then_inc(ke_cp, 1)
                    if t < NT:
                        dve.copy_predicated(pT[:, b, :], may[:, :], kp_ps[:, b, P:2 * P]).then_inc(pt_cp, 1)
                        if t >= 1:
                            states(dve, h, t - 1)
                    else:
                        dve.copy_predicated(pT_smp[:, :], may_smp[:, :], kp_ps[0:SMP, b, P:P + SMP]).then_inc(pt_cp, 1)
                        states(dve, h, t - 1)
                        dve.wait_ge(ke_cp, h * (NT + 1) + (NT + 1))
                        dve.tensor_tensor(ke_smp[:, :, :], ke[0:SMP, b, :].unsqueeze(1).broadcast_to([SMP, NSEQ, P]),
                                          row_mask[:, :].unsqueeze(2).broadcast_to([SMP, NSEQ, P]),
                                          ALU.mult).then_inc(smp_made, 1)
                        dve.tensor_tensor(q_smp[:, :, :], qT[:, SEQ:TOK].unsqueeze(1).broadcast_to([P, NSEQ, SMP]),
                                          tok_mask[:, :, :], ALU.mult).then_inc(smp_made, 1)
                dve.wait_ge(ld["s0"], h * 16 + 16)
                for q in range(NSEQ):
                    dve.wait_ge(ds_smp, h * NSEQ + (q + 1))
                    dve.scalar_tensor_tensor(out=s_new[:, q, :], in0=s_in[:, q, :], scalar=decay_smp[:, q:q + 1],
                                             in1=ds_ps[:, q % 2, 0:DV], op0=ALU.mult, op1=ALU.add).then_inc(s_smp, 1)
                dve.wait_ge(root_made, h + 1)
                dve.reciprocal(rstd[:, 0:NT], root[:, 0:NT])
                dve.reciprocal(rstd[0:SMP, NT:], root[0:SMP, NT:]).then_inc(rstd_made, 1)
                dve.wait_ge(rstd_made, h + 1)
                dve.wait_ge(o_cp, h * (NT + 1) + (NT + 1))
                for t in range(NT + 1):
                    n = rows_of(t)
                    last = dve.scalar_tensor_tensor(out=o[0:n, t, :], in0=o[0:n, t, :], scalar=rstd[0:n, t:t + 1],
                                                    in1=g_gain[0:n, :], op0=ALU.mult, op1=ALU.mult)
                last.then_inc(normed, 1)
                dve.wait_ge(normed, h + 1)
                dve.wait_ge(tok_cp, h * (NT + 1) + (NT + 1))
                dve.tensor_tensor(o[:, 0:NT, :], o[:, 0:NT, :], vg[:, 0:NT, DV:], ALU.mult).then_inc(gated, 1)
                dve.tensor_tensor(o[0:SMP, NT, :], o[0:SMP, NT, :], vg[0:SMP, NT, DV:], ALU.mult).then_inc(gated, 1)
                dve.wait_ge(gated, h * 2 + 2)
                dve.sem_inc(gate, 1)


def out_project(nc, c, name, o_in, transposed, w_out, residual, h_out, xnT=None, gain=None, y_out=None):
    with ExitStack() as stack:
        s = Scope(nc, stack, name)
        w_raw = s.sb("w_raw", [P, 2, D])
        w_hi, w_lo = (s.sb(n, [P, KD, D], F32R) for n in ("w_hi", "w_lo"))
        o = s.sb("o", [P, 2, D])
        oT_hi, oT_lo = (s.sb(n, [P, 2, KD, P], F32R) for n in ("oT_hi", "oT_lo"))
        res, h, xn = (s.sb(n, [P, 2, D]) for n in ("res", "h", "xn"))
        square = s.sb("square", [P, D])
        xT = s.sb("xT", [P, 2, KD, P])
        gains = s.sb("gains", [P, D])
        sumsq, root, rstd = (s.sb(n, [P, 2]) for n in ("sumsq", "root", "rstd"))
        eps = s.sb("eps", [P, 1])
        oT_ps, y_ps, t_ps = s.ps("oT", [P, KD * P]), s.ps("y", [P, 2, D]), s.ps("t", [P, KD * P])
        w_in, o_in_sem, res_in = s.sems("w_in", 2), s.sems("o_in", 2), s.sems("res_in", 2)
        h_stored, x_stored = s.sems("h_stored", 2), s.sems("x_stored", 2)
        gain_in, eps_set, w_hi_made, w_lo_made, o_turned, hi_made, lo_made, y_made, h_made, sumsq_made, root_made, \
            rstd_made, xn_made, x_turned, x_copied = (s.sem(n) for n in (
                "gain_in", "eps_set", "w_hi_made", "w_lo_made", "o_turned", "hi_made", "lo_made", "y_made", "h_made",
                "sumsq_made", "root_made", "rstd_made", "xn_made", "x_turned", "x_copied"))
        block = stack.enter_context(nc.Block())

        def lagged(i, b):
            return i if b else i - 1

        @block.sync
        def _(sp):
            if gain is not None:
                sp.dma_start(gains[:, :], gain.unsqueeze(0).broadcast_to([P, D])).then_inc(gain_in, 16)
            for k in range(KD):
                if k >= 2:
                    sp.wait_ge(w_lo_made, k - 1)
                sp.dma_start(w_raw[:, k % 2, :], w_out[k * P:(k + 1) * P, :]).then_inc(w_in[k % 2], 16)

            def step(t, i, b):
                n = rows_of(t)
                if from_tile(t, 2):
                    if transposed:
                        sp.wait_ge(lo_made, t - 1)
                    else:
                        sp.wait_ge(o_turned, t - 1)
                if transposed:
                    sp.dma_start(o[:, b, :].rearrange("p (k n) -> p k n", n=P)[:, :, 0:n],
                                 o_in.rearrange("(k p) n -> p k n", p=P)[:, :, ds(t * P, n)]).then_inc(o_in_sem[b], 16)
                else:
                    sp.dma_start(o[0:n, b, :], o_in[ds(t * P, n), :]).then_inc(o_in_sem[b], 16)
                if from_tile(t, 2):
                    sp.wait_ge(h_made, t - 1)
                sp.dma_start(res[0:n, b, :], residual(t)).then_inc(res_in[b], 16)
            over_tiles(sp, step)

        @block.scalar
        def _(act):
            for k in range(KD):
                act.wait_ge(w_in[k % 2], 16 * (k // 2 + 1))
                act.activation(w_hi[:, k, :], w_raw[:, k % 2, :], ACT.Copy).then_inc(w_hi_made, 1)
            act.wait_ge(eps_set, 1)

            def norm(t, i, b):
                n = rows_of(t)
                act.wait_ge(h_made, t + 1)
                if from_tile(t, 2):
                    act.wait_ge(rstd_made, t - 1)
                act.activation(square[0:n, :], h[0:n, b, :], ACT.Square,
                               accum_out=sumsq[0:n, b:b + 1]).then_inc(sumsq_made, 1)
                act.wait_ge(sumsq_made, t + 1)
                act.activation(root[0:n, b:b + 1], sumsq[0:n, b:b + 1], ACT.Sqrt, scale=1.0 / D,
                               bias=eps[0:n, :]).then_inc(root_made, 1)

            def step(t, i, b):
                n = rows_of(t)
                if from_tile(t, 2):
                    act.wait_ge(y_made, t - 1)
                if transposed:
                    act.wait_ge(o_in_sem[b], 16 * i + 16)
                    act.activation(oT_hi[:, b, :, 0:n], o[:, b, :].rearrange("p (k n) -> p k n", n=P)[:, :, 0:n],
                                   ACT.Copy).then_inc(hi_made, 1)
                else:
                    act.wait_ge(o_turned, t + 1)
                    act.activation(oT_hi[:, b, :, 0:n], oT_ps[:, :].rearrange("p (k n) -> p k n", n=P)[:, :, 0:n],
                                   ACT.Copy).then_inc(hi_made, 1)
                if from_tile(t, 1):
                    norm(t - 1, lagged(i, b), 1 - b)
            over_tiles(act, step)
            norm(NT, NT // 2, 0)

        @block.vector
        def _(dve):
            for k in range(KD):
                dve.wait_ge(w_hi_made, k + 1)
                dve.tensor_tensor(w_lo[:, k, :], w_raw[:, k % 2, :], w_hi[:, k, :].bitcast(F32),
                                  ALU.subtract).then_inc(w_lo_made, 1)
            dve.memset(eps[:, :], EPS).then_inc(eps_set, 1)
            if gain is not None:
                dve.wait_ge(gain_in, 16)

            def after(t, i, b):
                n = rows_of(t)
                dve.wait_ge(y_made, t + 1)
                dve.wait_ge(res_in[b], 16 * i + 16)
                if from_tile(t, 2):
                    if h_out is not None:
                        dve.wait_ge(h_stored[b], 16 * i)
                    dve.wait_ge(xn_made, t - 1)
                dve.tensor_tensor(h[0:n, b, :], y_ps[0:n, b, :], res[0:n, b, :], ALU.add).then_inc(h_made, 1)

            def finish(t, i, b):
                n = rows_of(t)
                dve.wait_ge(root_made, t + 1)
                dve.reciprocal(rstd[0:n, b:b + 1], root[0:n, b:b + 1]).then_inc(rstd_made, 1)
                dve.wait_ge(rstd_made, t + 1)
                if xnT is not None:
                    if from_tile(t, 2):
                        dve.wait_ge(x_turned, t - 1)
                    dve.tensor_scalar(xn[0:n, b, :], h[0:n, b, :], rstd[0:n, b:b + 1], None,
                                      ALU.mult).then_inc(xn_made, 1)
                else:
                    if from_tile(t, 2):
                        dve.wait_ge(x_stored[b], 16 * i)
                    dve.scalar_tensor_tensor(out=xn[0:n, b, :], in0=h[0:n, b, :], scalar=rstd[0:n, b:b + 1],
                                             in1=gains[0:n, :], op0=ALU.mult, op1=ALU.mult).then_inc(xn_made, 1)

            def copy_x(t, i, b):
                n = rows_of(t)
                dve.wait_ge(x_turned, t + 1)
                if from_tile(t, 2):
                    dve.wait_ge(x_stored[b], 16 * i)
                dve.tensor_scalar(xT[:, b, :, 0:n], t_ps[:, :].rearrange("p (k n) -> p k n", n=P)[:, :, 0:n],
                                  1.0, None, ALU.mult).then_inc(x_copied, 1)

            def step(t, i, b):
                n = rows_of(t)
                dve.wait_ge(hi_made, t + 1)
                if from_tile(t, 2):
                    dve.wait_ge(y_made, t - 1)
                src = (o[:, b, :] if transposed else oT_ps[:, :]).rearrange("p (k n) -> p k n", n=P)[:, :, 0:n]
                dve.tensor_tensor(oT_lo[:, b, :, 0:n], src, oT_hi[:, b, :, 0:n].bitcast(F32),
                                  ALU.subtract).then_inc(lo_made, 1)
                if from_tile(t, 1):
                    after(t - 1, lagged(i, b), 1 - b)
                    finish(t - 1, lagged(i, b), 1 - b)
                if xnT is not None and from_tile(t, 2):
                    copy_x(t - 2, i - 1, b)
            over_tiles(dve, step)
            after(NT, NT // 2, 0)
            finish(NT, NT // 2, 0)
            if xnT is not None:
                copy_x(NT - 1, NT // 2 - 1, 1)
                copy_x(NT, NT // 2, 0)

        @block.tensor
        def _(pe):
            def turn(t, i, b):
                n = rows_of(t)
                pe.wait_ge(o_in_sem[b], 16 * i + 16)
                if from_tile(t, 1):
                    pe.wait_ge(lo_made, t)
                for k in range(KD):
                    mm = pe.transpose(oT_ps[:, k * P:k * P + n], o[0:n, b, k * P:(k + 1) * P], c.ident[0:n, 0:n])
                mm.then_inc(o_turned, 1)

            def turn_x(t, i, b):
                n = rows_of(t)
                pe.wait_ge(xn_made, t + 1)
                if from_tile(t, 1):
                    pe.wait_ge(x_copied, t)
                for k in range(KD):
                    mm = pe.transpose(t_ps[:, k * P:k * P + n], xn[0:n, b, k * P:(k + 1) * P], c.ident[0:n, 0:n])
                mm.then_inc(x_turned, 1)

            def products(t, i, b):
                pe.wait_ge(lo_made, t + 1)
                if from_tile(t, 2):
                    pe.wait_ge(h_made, t - 1)
                for j in range(D // BANK):
                    for k in range(KD):
                        for w, x in ((w_hi, oT_hi), (w_lo, oT_hi), (w_hi, oT_lo)):
                            mm = pe.matmul(y_ps[:, b, j * BANK:(j + 1) * BANK], x[:, b, k, :],
                                           w[:, k, j * BANK:(j + 1) * BANK],
                                           start=(k == 0 and w is w_hi and x is oT_hi),
                                           stop=(k == KD - 1 and x is oT_lo))
                mm.then_inc(y_made, 1)

            def step(t, i, b):
                if not transposed:
                    turn(t, i, b)
                if from_tile(t, 1):
                    products(t - 1, lagged(i, b), 1 - b)
                if xnT is not None and from_tile(t, 2):
                    turn_x(t - 2, i - 1, b)
            pe.wait_ge(w_lo_made, KD)
            over_tiles(pe, step)
            products(NT, NT // 2, 0)
            if xnT is not None:
                turn_x(NT - 1, NT // 2 - 1, 1)
                turn_x(NT, NT // 2, 0)

        @block.gpsimd
        def _(pool):
            def step(t, i, b):
                n = rows_of(t)
                if h_out is not None:
                    pool.wait_ge(h_made, t + 1)
                    pool.wait_ge(eps_set, 1)
                    pool.dma_start(h_out(t), h[0:n, b, :]).then_inc(h_stored[b], 16)
                pool.wait_ge(x_copied if xnT is not None else xn_made, t + 1)
                pool.wait_ge(eps_set, 1)
                if xnT is not None:
                    pool.dma_start(xnT.rearrange("(k p) n -> p k n", p=P)[:, :, ds(t * P, n)],
                                   xT[:, b, :, 0:n]).then_inc(x_stored[b], 16)
                else:
                    pool.dma_start(y_out(t), xn[0:n, b, :]).then_inc(x_stored[b], 16)
            over_tiles(pool, step)
            for stored in ([h_stored] if h_out is not None else []) + [x_stored]:
                pool.wait_ge(stored[0], 16 * (NT // 2 + 1))
                pool.wait_ge(stored[1], 16 * (NT // 2))


def chunks_of(tile):
    n, out = (tile + 1) * P, []
    while n > 0:
        out.append((max(0, n - 1024), n))
        n -= 1024
    return out


def attention_schedule():
    def logits(e, g):
        return [("z", e, t, j) for t in range(4 * g, 4 * g + 4) for j in range(len(chunks_of(t)))]

    groups = [(e, g) for e in range(2) for g in range(4)]
    order = list(logits(*groups[0]))
    for n, (e, g) in enumerate(groups):
        values = [("a", e, g, j) for j in reversed(range(4 * g + 4))]
        nxt = logits(*groups[n + 1]) if n + 1 < len(groups) else []
        done = 0
        for m, v in enumerate(values):
            want = -(-len(nxt) * (m + 1) // len(values))
            order += nxt[done:want]
            done = want
            order.append(v)
    return order


def prompt_attention(nc, c, projT, b_sb, k_out, v_out, oT):
    k_rows, v_rows, q_rows, g_rows = 0, D, 2 * D, 3 * D
    order = attention_schedule()
    n_z, n_a = (sum(x[0] == kind for x in order) for kind in "za")
    z_index = {x: n for n, x in enumerate(x for x in order if x[0] == "z")}
    a_index = {x: n for n, x in enumerate(x for x in order if x[0] == "a")}

    def last_z(e, t):
        return z_index[("z", e, t, len(chunks_of(t)) - 1)]

    def last_a(e, g):
        return a_index[("a", e, g, 0)]

    with ExitStack() as stack:
        s = Scope(nc, stack, "att")
        qT, kT, vT, gT, silu = (s.sb(n, [P, SEQ]) for n in ("qT", "kT", "vT", "gT", "silu"))
        k_tok, v_tok = (s.sb(n, [P, NT, P]) for n in ("k_tok", "v_tok"))
        w = s.sb("w", [P, 8, SEQ])
        pass_on = s.sb("pass_on", [P, 2, SEQ])
        rest = s.sb("rest", [P, 2, SEQ + 1])
        zeros = s.sb("zeros", [P, 1024])
        wT = s.sb("wT", [P, 2, BANK])
        out = s.sb("out", [P, SEQ])
        bias_all = s.sb("bias_all", [P, 2, NH])
        bias = s.sb("bias", [P, 2, 2])
        z_ps = s.ps("z", [P, 2, 1024])
        wT_ps = s.ps("wT_acc", [P, 2, BANK])
        o_ps = s.ps("o_acc", [P, 2, BANK])
        gate = s.sem("pair_gate")
        in_q, in_k, in_v, in_g, bias_in = (s.sem(n) for n in ("in_q", "in_k", "in_v", "in_g", "bias_in"))
        setup, bias_set, sig_made, silu_made, kv_turned, kv_copied, z_made, sigmoids, scanned, w_made, w_turned, \
            wT_copied, av_done, o_made, o_gated, st = (s.sem(n) for n in (
                "setup", "bias_set", "sig_made", "silu_made", "kv_turned", "kv_copied", "z_made", "sigmoids",
                "scanned", "w_made", "w_turned", "wT_copied", "av_done", "o_made", "o_gated", "stored"))
        block = stack.enter_context(nc.Block())

        def group_no(e, g):
            return 4 * e + g

        @block.sync
        def _(sp):
            sp.sem_inc(gate, 1)
            sp.dma_start(bias_all[:, 0, :], b_sb.unsqueeze(0).broadcast_to([P, NH])).then_inc(bias_in, 16)
            with sp.Fori(0, PAIRS) as pr:
                sp.wait_ge(gate, pr * 4 + 4)
                sp.wait_ge(bias_in, 16)
                for dst, row, sem in ((kT, k_rows, in_k), (vT, v_rows, in_v), (gT, g_rows, in_g), (qT, q_rows, in_q)):
                    sp.dma_start(dst[:, :], projT[ds(pr * P + row, P), 0:SEQ]).then_inc(sem, 16)
                sp.wait_ge(kv_copied, pr * 8 + 8)
                sp.wait_ge(o_gated, pr * 8 + 8)
                sp.dma_start(oT[ds(pr * P, P), 0:SEQ], out[:, :]).then_inc(st, 16)
                for dst, src in ((k_out, k_tok), (v_out, v_tok)):
                    sp.dma_start(dst.rearrange("(t p) n -> p t n", p=P)[:, :, ds(pr * P, P)],
                                 src[:, :, :]).then_inc(st, 16)
                sp.wait_ge(st, pr * 48 + 48)
                sp.sem_inc(gate, 1)

        @block.tensor
        def _(pe):
            pe.sem_inc(gate, 1)
            with pe.Fori(0, PAIRS) as pr:
                pe.wait_ge(gate, pr * 4 + 4)
                for n in range(8):
                    src = kT if n < 4 else vT
                    pe.wait_ge(in_k if n < 4 else in_v, pr * 16 + 16)
                    if n >= 2:
                        pe.wait_ge(kv_copied, pr * 8 + (n - 1))
                    for j in range(4):
                        at = ((n % 4) * 4 + j) * P
                        mm = pe.transpose(wT_ps[:, n % 2, j * P:(j + 1) * P], src[:, at:at + P], c.ident[:, :])
                    mm.then_inc(kv_turned, 1)
                pe.wait_ge(in_q, pr * 16 + 16)

                def value_product(e, g, j):
                    a = a_index[("a", e, g, j)]
                    lo = max(0, j - 4 * g) * P
                    pe.wait_ge(wT_copied, pr * n_a + (a + 1))
                    r = slice(HD * e, HD * (e + 1))
                    mm = pe.matmul(o_ps[r, group_no(e, g) % 2, lo:BANK], v_tok[:, j, r], wT[:, a % 2, lo:BANK],
                                   start=(j == 4 * g + 3), stop=(j == 0), skip_group_check=True)
                    mm.then_inc(av_done, 1)

                for kind, e, x, j in order:
                    r = slice(HD * e, HD * (e + 1))
                    if kind == "z":
                        lo, hi = chunks_of(x)[j]
                        n = z_index[(kind, e, x, j)]
                        if n >= 2:
                            pe.wait_ge(sigmoids, pr * n_z + (n - 1))
                        for at in range(lo, hi, BANK):
                            size = min(BANK, hi - at)
                            dst = z_ps[:, n % 2, at - lo:at - lo + size]
                            diagonal = at + size == (x + 1) * P
                            if diagonal:
                                pe.matmul(dst[:, size - P:size], c.ident_bf[:, :], c.diag_mask[:, :], start=True,
                                          stop=False, skip_group_check=True)
                            mm = pe.matmul(dst, qT[r, x * P:(x + 1) * P], kT[r, at:at + size], start=not diagonal,
                                           stop=True, skip_group_check=True)
                        mm.then_inc(z_made, 1)
                    else:
                        a, gn = a_index[(kind, e, x, j)], group_no(e, x)
                        first = j == 4 * x + 3
                        if first:
                            pe.wait_ge(w_made, pr * n_z + (last_z(e, j) + 1))
                            if gn >= 2:
                                pe.wait_ge(o_gated, pr * 8 + (gn - 1))
                        if a >= 2:
                            pe.wait_ge(wT_copied, pr * n_a + (a - 1))
                        elif a < 2:
                            pe.wait_ge(kv_copied, pr * 8 + 8)
                        for t in range(max(4 * x, j), 4 * x + 4):
                            at = SEQ - (t + 1) * P + j * P
                            mm = pe.transpose(wT_ps[:, a % 2, (t % 4) * P:(t % 4 + 1) * P],
                                              w[:, 4 * (gn % 2) + t % 4, at:at + P], c.ident[:, :])
                        mm.then_inc(w_turned, 1)
                        if not first:
                            value_product(e, x, j + 1)
                        if j == 0:
                            value_product(e, x, 0)
                pe.wait_ge(av_done, pr * n_a + n_a)
                pe.sem_inc(gate, 1)

        @block.scalar
        def _(act):
            act.sem_inc(gate, 1)
            act.wait_ge(setup, 1)
            with act.Fori(0, PAIRS) as pr:
                act.wait_ge(gate, pr * 4 + 4)
                for n in range(8):
                    dst = k_tok if n < 4 else v_tok
                    act.wait_ge(kv_turned, pr * 8 + (n + 1))
                    act.activation(dst[:, (n % 4) * 4:(n % 4) * 4 + 4, :],
                                   wT_ps[:, n % 2, :].rearrange("p (t n) -> p t n", n=P), ACT.Copy
                                   ).then_inc(kv_copied, 1)
                act.wait_ge(in_g, pr * 16 + 16)
                act.activation(silu[:, :], gT[:, :], ACT.Sigmoid).then_inc(sig_made, 1)
                act.wait_ge(bias_set, pr + 1)
                for kind, e, x, j in order:
                    if kind == "z":
                        lo, hi = chunks_of(x)[j]
                        n, gn = z_index[(kind, e, x, j)], group_no(e, x // 4)
                        at = SEQ - (x + 1) * P
                        if gn >= 2 and j == 0:
                            pe_, pg = divmod(gn - 2, 4)
                            act.wait_ge(w_turned, pr * n_a + (last_a(pe_, pg) + 1))
                        if j == 0 and (e, x) not in ((0, 0), (0, 1)):
                            ze, zx = (e, x - 2) if x >= 2 else (e - 1, x + 14)
                            act.wait_ge(scanned, pr * n_z + (last_z(ze, zx) + 1))
                        act.wait_ge(z_made, pr * n_z + (n + 1))
                        act.activation(w[:, 4 * (gn % 2) + x % 4, at + lo:at + hi], z_ps[:, n % 2, 0:hi - lo],
                                       ACT.Sigmoid, bias=bias[:, 0, e:e + 1], scale=HD ** -0.5)
                        act.activation(pass_on[:, x % 2, at + lo:at + hi], z_ps[:, n % 2, 0:hi - lo],
                                       ACT.Sigmoid, bias=bias[:, 1, e:e + 1], scale=-HD ** -0.5).then_inc(sigmoids, 1)
                    else:
                        a = a_index[(kind, e, x, j)]
                        lo = max(0, j - 4 * x) * P
                        act.wait_ge(w_turned, pr * n_a + (a + 1))
                        if a >= 2:
                            act.wait_ge(av_done, pr * n_a + (a - 1))
                        act.activation(wT[:, a % 2, lo:BANK], wT_ps[:, a % 2, lo:BANK], ACT.Copy).then_inc(wT_copied, 1)
                act.wait_ge(wT_copied, pr * n_a + n_a)
                act.sem_inc(gate, 1)

        @block.vector
        def _(dve):
            dve.sem_inc(gate, 1)
            dve.memset(zeros[:, :], 0.0)
            dve.memset(rest[:, :, SEQ:], 1.0).then_inc(setup, 1)
            dve.wait_ge(bias_in, 16)
            dve.tensor_scalar(bias_all[:, 1, :], bias_all[:, 0, :], -1.0, None, ALU.mult).then_inc(setup, 1)
            dve.wait_ge(setup, 2)
            with dve.Fori(0, PAIRS) as pr:
                dve.wait_ge(gate, pr * 4 + 4)
                dve.wait_ge(setup, 2)
                dve.tensor_scalar(bias[:, :, :], bias_all[:, :, ds(pr * 2, 2)], 1.0, None, ALU.mult).then_inc(bias_set, 1)
                dve.wait_ge(sig_made, pr + 1)
                dve.tensor_tensor(silu[:, :], silu[:, :], gT[:, :], ALU.mult).then_inc(silu_made, 1)
                for kind, e, x, j in order:
                    if kind == "z":
                        lo, hi = chunks_of(x)[j]
                        n, gn = z_index[(kind, e, x, j)], group_no(e, x // 4)
                        at, b, size = SEQ - (x + 1) * P, x % 2, hi - lo
                        dve.wait_ge(sigmoids, pr * n_z + (n + 1))
                        if n >= 1:
                            dve.wait_ge(w_made, pr * n_z + n)
                        dve.tensor_tensor_scan(rest[:, b, at + lo:at + hi][:, ::-1],
                                               pass_on[:, b, at + lo:at + hi][:, ::-1], zeros[:, 0:size],
                                               rest[:, b, at + hi:at + hi + 1], ALU.mult, ALU.add).then_inc(scanned, 1)
                        dve.wait_ge(scanned, pr * n_z + (n + 1))
                        weights = w[:, 4 * (gn % 2) + x % 4, at + lo:at + hi]
                        dve.tensor_tensor(weights, weights, rest[:, b, at + lo + 1:at + hi + 1],
                                          ALU.mult).then_inc(w_made, 1)
                    elif j == 0:
                        gn, r = group_no(e, x), slice(HD * e, HD * (e + 1))
                        dve.wait_ge(av_done, pr * n_a + (a_index[(kind, e, x, j)] + 1))
                        dve.wait_ge(silu_made, pr + 1)
                        dve.tensor_tensor(out[r, x * BANK:(x + 1) * BANK], o_ps[r, gn % 2, :],
                                          silu[r, x * BANK:(x + 1) * BANK], ALU.mult).then_inc(o_gated, 1)
                dve.wait_ge(o_gated, pr * 8 + 8)
                dve.sem_inc(gate, 1)


def sample_attention(nc, c, projT, b_sb, cache_k, cache_v, page_table, k_out, v_out, oT):
    n_phys = cache_k.shape[0]
    n_pages = page_table.shape[1]
    past = n_pages * PAGE
    groups = n_pages // 4
    rows = NH * TSEQ
    k_ring, v_ring = 8, n_pages
    blocks = D // P
    with ExitStack() as stack:
        s = Scope(nc, stack, "smp")
        newT = s.sb("newT", [P, 4 * blocks, SMP])
        silu = s.sb("silu", [P, blocks, SMP])
        new_k, new_v = s.sb("new_k", [SMP, D]), s.sb("new_v", [P, D])
        q_rows = s.sb("q_rows", [P, 2, 9 * rows])
        mask_all = s.sb("mask_all", [P, NSEQ, SMP], BF16)
        mask_tokens = s.sb("mask_tokens", [TSEQ, NSEQ, SMP], BF16)
        mask = s.sb("mask", [P, 2, SMP], BF16)
        mask_dram = nc.dram_tensor("mask_dram", (TSEQ, NSEQ * SMP), BF16).ap()
        table = s.sb("table", [1, NSEQ * n_pages], I32)
        k_pages, v_pages = s.sb("k_pages", [P, k_ring, D]), s.sb("v_pages", [P, v_ring, D])
        kT = s.sb("kT", [P, 2, blocks, BANK])
        w = s.sb("w", [P, past + P])
        pass_on = s.sb("pass_on", [rows, 2, BANK])
        rest = s.sb("rest", [rows, past + SMP + 1])
        zeros = s.sb("zeros", [rows, BANK])
        wT = s.sb("wT", [P, 2, 4 * rows])
        o = s.sb("o", [P, D])
        out = s.sb("out", [P, blocks, SMP])
        bias = s.sb("bias", [rows, 2])
        kT_ps = s.ps("kT_acc", [P, 2, D])
        z_ps, wT_ps, o_ps = s.ps("z", [P, BANK]), s.ps("wT_acc", [P, BANK]), s.ps("o_acc", [rows, D])
        once, table_in, mask_moved, kv_stored, out_stored = (s.sem(n) for n in (
            "once_in", "table_in", "mask_moved", "kv_stored", "out_stored"))
        k_in, v_in = s.sems("k_in", k_ring), s.sems("v_in", v_ring)
        setup, masks, new_turned, new_copied, q_made, k_turned, act_copied, dve_copied, z_made, sigmoids, scanned, \
            w_made, w_turned, wT_copied, v_used, o_made, o_copied, folded, gated, seq_done = (s.sem(n) for n in (
                "setup", "masks", "new_turned", "new_copied", "q_made", "k_turned", "act_copied", "dve_copied",
                "z_made", "sigmoids", "scanned", "w_made", "w_turned", "wT_copied", "v_used", "o_made", "o_copied",
                "folded", "gated", "seq_done"))
        n_w = groups + 1
        half = blocks // 2

        with nc.Block() as block:
            @block.sync
            def _(sp):
                sp.dma_start(newT[:, :, :], projT.rearrange("(b p) n -> p b n", p=P)[:, :, SEQ:TOK]).then_inc(once, 16)
                sp.dma_start(bias[:, 0:1], b_sb.unsqueeze(1).unsqueeze(1).broadcast_to([NH, TSEQ, 1]),
                             allow_slow_non_contiguous=True).then_inc(once, 16)
                sp.dma_start(table[:, :], page_table.rearrange("(o s) n -> o (s n)", o=1)).then_inc(table_in, 16)
                sp.wait_ge(masks, 4)
                sp.dma_start(mask_dram, mask_tokens[:, :, :].rearrange("p s n -> p (s n)")).then_inc(mask_moved, 16)
                sp.wait_ge(mask_moved, 16)
                sp.dma_start(mask_all[0:rows, :, :].rearrange("p s n -> p (s n)"),
                             mask_dram.unsqueeze(0).broadcast_to([NH, TSEQ, NSEQ * SMP])).then_inc(mask_moved, 16)
                sp.wait_ge(new_copied, 4)
                sp.dma_start(k_out, new_k[:, :]).then_inc(kv_stored, 16)
                sp.dma_start(v_out, new_v[0:SMP, :]).then_inc(kv_stored, 16)
                sp.wait_ge(kv_stored, 32)
                sp.wait_ge(table_in, 16)
                sp.wait_ge(mask_moved, 32)

            @block.gpsimd
            def _(pool):
                pool.memset(mask_tokens[:, :, :], 0.0).then_inc(masks, 1)
                pool.memset(mask_all[:, :, :], 0.0).then_inc(masks, 1)
                pool.wait_ge(masks, 2)
                pool.affine_select(out=mask_tokens[:, :, :], in_=mask_tokens[:, :, :], compare_op=ALU.is_ge,
                                   fill=MASKED, base=0, pattern=[[-TSEQ, NSEQ], [1, SMP]],
                                   channel_multiplier=0).then_inc(masks, 1)
                pool.wait_ge(masks, 3)
                pool.affine_select(out=mask_tokens[:, :, :], in_=mask_tokens[:, :, :], compare_op=ALU.is_gt,
                                   fill=MASKED, base=0, pattern=[[TSEQ, NSEQ], [-1, SMP]],
                                   channel_multiplier=1).then_inc(masks, 1)

            @block.vector
            def _(dve):
                dve.memset(q_rows[:, :, :], 0.0)
                dve.memset(new_v[:, :], 0.0)
                dve.memset(w[:, :], 0.0)
                dve.memset(o[:, :], 0.0)
                dve.memset(zeros[:, :], 0.0)
                dve.memset(rest[:, past + SMP:], 1.0).then_inc(setup, 1)
                dve.wait_ge(once, 32)
                dve.tensor_scalar(bias[:, 1:2], bias[:, 0:1], -1.0, None, ALU.mult).then_inc(setup, 1)
                dve.wait_ge(setup, 2)
                for n in range(4):
                    dve.wait_ge(new_turned, n + 1)
                    dst = (new_k if n < 2 else new_v)[0:SMP, (n % 2) * BANK:(n % 2 + 1) * BANK]
                    dve.tensor_copy(dst, kT_ps[0:SMP, n // 2, (n % 2) * BANK:(n % 2 + 1) * BANK]).then_inc(new_copied, 1)
                dve.wait_ge(setup, 3)
                dve.tensor_tensor(silu[:, :, :], silu[:, :, :], newT[:, 3 * blocks:, :], ALU.mult).then_inc(setup, 1)

            @block.scalar
            def _(act):
                act.wait_ge(once, 32)
                act.wait_ge(setup, 2)
                act.activation(silu[:, :, :], newT[:, 3 * blocks:, :], ACT.Sigmoid).then_inc(setup, 1)

            @block.tensor
            def _(pe):
                pe.wait_ge(once, 32)
                for n in range(4):
                    for j in range(4):
                        mm = pe.transpose(kT_ps[0:SMP, n // 2, (n % 2) * BANK + j * P:(n % 2) * BANK + (j + 1) * P],
                                          newT[:, 4 * n + j, :], c.ident[:, :])
                    mm.then_inc(new_turned, 1)

        block = stack.enter_context(nc.Block())

        def over_sequences(engine, step):
            with engine.Fori(0, NSEQ // 2) as i:
                step(i * 2, i, 0)
                step(i * 2 + 1, i, 1)

        def half_read(g):
            return g + 2 if g >= 2 else g + 1

        def page_of(m):
            return (groups - 1 - m // 4) * 4 + m % 4

        @block.sync
        def _(sp):
            def step(q, i, b):
                for m in range(n_pages):
                    page = sp.value_load(table[0:1, ds(q * n_pages + page_of(m), 1)], min_val=0, max_val=n_phys - 1)
                    sp.wait_ge(k_turned, q * n_pages + (m + 1))
                    sp.wait_ge(table_in, 16)
                    sp.dma_start(k_pages[:, m % k_ring, :], cache_k.rearrange("g t h d -> (g t) (h d)")
                                 [ds(page * PAGE, PAGE), :]).then_inc(k_in[m % k_ring], 16)
                    sp.wait_ge(v_used, q * n_pages + (m + 1))
                    sp.wait_ge(table_in, 16)
                    sp.dma_start(v_pages[:, m % v_ring, :], cache_v.rearrange("g t h d -> (g t) (h d)")
                                 [ds(page * PAGE, PAGE), :]).then_inc(v_in[m % v_ring], 16)
            over_sequences(sp, step)
            sp.wait_ge(gated, NSEQ + 1)
            sp.dma_start(oT.rearrange("(b p) n -> p b n", p=P)[:, :, SEQ:TOK], out[:, :, :]).then_inc(out_stored, 16)
            sp.wait_ge(out_stored, 16)

        @block.tensor
        def _(pe):
            pe.sem_inc(k_turned, k_ring)
            pe.sem_inc(v_used, v_ring)
            pe.sem_inc(z_made, 2)
            pe.sem_inc(folded, 2)
            per_lap = n_pages // k_ring

            def step(q, i, b):
                def turn_keys(g):
                    for p in range(4):
                        m = 4 * g + p
                        pe.wait_ge(k_in[m % k_ring], q * (16 * per_lap) + 16 * (m // k_ring + 1))
                        pe.wait_ge(act_copied, q * n_pages + (m + 1))
                        pe.wait_ge(dve_copied, q * n_pages + (m + 1))
                        for hp in range(blocks):
                            mm = pe.transpose(kT_ps[:, m % 2, hp * P:(hp + 1) * P],
                                              k_pages[:, m % k_ring, hp * P:(hp + 1) * P], c.ident[:, :])
                        mm.then_inc(k_turned, 1)

                def logits(n):
                    pe.wait_ge(sigmoids, q * n_w + (n + 1))
                    if n == 0:
                        pe.wait_ge(gated, q + 1)
                        pe.wait_ge(q_made, q * 3 + 3)
                        pe.matmul(z_ps[0:rows, 0:SMP], c.ident_bf[:, 0:rows], mask[:, b, :], start=True, stop=False)
                        for hp in range(blocks):
                            mm = pe.matmul(z_ps[0:rows, 0:SMP], q_rows[:, b, hp * rows:(hp + 1) * rows], newT[:, hp, :],
                                           start=False, stop=(hp == blocks - 1))
                    else:
                        pe.wait_ge(act_copied, q * n_pages + (4 * n + 2))
                        pe.wait_ge(dve_copied, q * n_pages + (4 * n + 2))
                        for hp in range(blocks):
                            mm = pe.matmul(z_ps[0:rows, :], q_rows[:, b, hp * rows:(hp + 1) * rows],
                                           kT[:, (n - 1) % 2, hp, :], start=(hp == 0), stop=(hp == blocks - 1))
                    mm.then_inc(z_made, 1)

                def turn_weights(n):
                    pe.wait_ge(w_made, q * n_w + (n + 1))
                    pe.wait_ge(wT_copied, q * n_w + (n + 1))
                    if n == 0:
                        mm = pe.transpose(wT_ps[:, 0:P], w[:, past:past + P], c.ident[:, :])
                    else:
                        for p in range(4):
                            at = page_of(4 * (n - 1) + p) * PAGE
                            mm = pe.transpose(wT_ps[:, p * P:(p + 1) * P], w[:, at:at + PAGE], c.ident[:, :])
                    mm.then_inc(w_turned, 1)

                def values(n):
                    pe.wait_ge(wT_copied, q * n_w + (n + 2))
                    if n == 0:
                        pe.wait_ge(o_copied, q + 1)
                    for p in range(1 if n == 0 else 4):
                        m = 4 * (n - 1) + p
                        if n > 0:
                            pe.wait_ge(v_in[m], q * 16 + 16)
                        for j in range(D // BANK):
                            src = new_v if n == 0 else v_pages[:, m, :]
                            mm = pe.matmul(o_ps[:, j * BANK:(j + 1) * BANK], wT[:, (n + b) % 2, p * rows:(p + 1) * rows],
                                           src[:, j * BANK:(j + 1) * BANK], start=(n == 0), stop=(n == groups and p == 3))
                        if n > 0:
                            mm.then_inc(v_used, 1)

                turn_keys(0)
                logits(0)
                for n in range(n_w):
                    if n + 1 < n_w:
                        logits(n + 1)
                    if n + 1 < groups:
                        turn_keys(n + 1)
                    turn_weights(n)
                    values(n)
                pe.wait_ge(v_used, q * n_pages + (n_pages + v_ring))
                pe.wait_ge(o_copied, q + 2)
                for h in range(NH):
                    e, hp = h % 2, h // 2
                    mm = pe.matmul(z_ps[HD * e:HD * (e + 1), hp * TSEQ:(hp + 1) * TSEQ],
                                   o[:, h * HD:(h + 1) * HD], c.ident[:, h * TSEQ:(h + 1) * TSEQ],
                                   start=True, stop=True)
                mm.then_inc(folded, 1)
            over_sequences(pe, step)

        @block.scalar
        def _(act):
            act.sem_inc(act_copied, 2)
            act.sem_inc(sigmoids, 1)
            act.sem_inc(wT_copied, 1)
            act.sem_inc(o_copied, 1)

            def step(q, i, b):
                def copy_keys(g):
                    for p in range(4):
                        m = 4 * g + p
                        act.wait_ge(k_turned, q * n_pages + (m + 1 + k_ring))
                        if p == 0:
                            act.wait_ge(z_made, q * n_w + half_read(g))
                        act.activation(kT[:, g % 2, 0:half, p * P:(p + 1) * P],
                                       kT_ps[:, m % 2, 0:BANK].rearrange("p (h n) -> p h n", n=P),
                                       ACT.Copy).then_inc(act_copied, 1)

                def sigmoid(n):
                    act.wait_ge(z_made, q * n_w + (n + 3))
                    size = SMP if n == 0 else BANK
                    at = past if n == 0 else (groups - n) * BANK
                    act.wait_ge(scanned, q * n_w + (n + 1))
                    act.wait_ge(v_used, q * n_pages + v_ring)
                    act.activation(w[0:rows, at:at + size], z_ps[0:rows, 0:size], ACT.Sigmoid, bias=bias[:, 0:1],
                                   scale=HD ** -0.5)
                    act.activation(pass_on[:, (n + b) % 2, 0:size], z_ps[0:rows, 0:size], ACT.Sigmoid, bias=bias[:, 1:2],
                                   scale=-HD ** -0.5).then_inc(sigmoids, 1)

                def copy_weights(n):
                    act.wait_ge(w_turned, q * n_w + (n + 1))
                    m = 1 if n == 0 else 4
                    act.activation(wT[:, (n + b) % 2, 0:m * rows].rearrange("p (m n) -> p m n", n=rows),
                                   wT_ps[:, 0:m * P].rearrange("p (m n) -> p m n", n=P)[:, :, 0:rows],
                                   ACT.Copy).then_inc(wT_copied, 1)

                copy_keys(0)
                sigmoid(0)
                for n in range(n_w):
                    if n + 1 < n_w:
                        sigmoid(n + 1)
                    if n + 1 < groups:
                        copy_keys(n + 1)
                    copy_weights(n)
                act.wait_ge(v_used, q * n_pages + (n_pages + v_ring))
                act.wait_ge(folded, q + 2)
                act.activation(o[0:rows, :], o_ps[:, :], ACT.Copy).then_inc(o_copied, 1)
            over_sequences(act, step)

        @block.vector
        def _(dve):
            dve.sem_inc(dve_copied, 2)
            dve.sem_inc(scanned, 2)
            dve.sem_inc(gated, 1)

            def step(q, i, b):
                cols = ds(q * TSEQ, TSEQ)

                def queries():
                    dve.wait_ge(folded, q + 1)
                    view = q_rows[:, b, :].rearrange("p (h n) -> p h n", n=rows + 2 * TSEQ)
                    qT = newT[:, 2 * blocks:3 * blocks, :]
                    dve.tensor_scalar(view[0:HD, :, 0:TSEQ], qT[0:HD, :, cols], 1.0, None, ALU.mult).then_inc(q_made, 1)
                    dve.tensor_scalar(view[HD:P, :, TSEQ:2 * TSEQ], qT[HD:P, :, cols], 1.0, None,
                                      ALU.mult).then_inc(q_made, 1)
                    dve.tensor_scalar(mask[:, b, :], mask_all[:, ds(q, 1), :].rearrange("p o n -> p (o n)"), 1.0, None,
                                      ALU.mult).then_inc(q_made, 1)

                def copy_keys(g):
                    for p in range(4):
                        m = 4 * g + p
                        dve.wait_ge(k_turned, q * n_pages + (m + 1 + k_ring))
                        if p == 0:
                            dve.wait_ge(z_made, q * n_w + half_read(g))
                        dve.tensor_copy(kT[:, g % 2, half:blocks, p * P:(p + 1) * P],
                                        kT_ps[:, m % 2, BANK:D].rearrange("p (h n) -> p h n", n=P)
                                        ).then_inc(dve_copied, 1)

                def weights(n):
                    size = SMP if n == 0 else BANK
                    at = past if n == 0 else (groups - n) * BANK
                    dve.wait_ge(sigmoids, q * n_w + (n + 2))
                    if n > 0:
                        dve.wait_ge(w_made, q * n_w + n)
                    dve.tensor_tensor_scan(rest[:, at:at + size][:, ::-1], pass_on[:, (n + b) % 2, 0:size][:, ::-1],
                                           zeros[:, 0:size], rest[:, at + size:at + size + 1], ALU.mult,
                                           ALU.add).then_inc(scanned, 1)
                    dve.wait_ge(scanned, q * n_w + (n + 3))
                    dve.tensor_tensor(w[0:rows, at:at + size], w[0:rows, at:at + size], rest[:, at + 1:at + size + 1],
                                      ALU.mult).then_inc(w_made, 1)

                queries()
                copy_keys(0)
                weights(0)
                for n in range(n_w):
                    if n + 1 < n_w:
                        weights(n + 1)
                    if n + 1 < groups:
                        copy_keys(n + 1)
                dve.wait_ge(folded, q + 3)
                dve.tensor_tensor(out[:, :, cols], z_ps[:, 0:blocks * TSEQ].rearrange("p (h n) -> p h n", n=TSEQ), silu[:, :, cols],
                                  ALU.mult).then_inc(gated, 1)
            over_sequences(dve, step)


def trunk(nc, x_prompt, x_sample, state_gla, cache_k, cache_v, page_table, g_norm_a, w_in_a, w_alpha2, b_alpha,
          g_head_a, w_out_a, g_kv, w_kv, g_norm_b, w_in_b, b_sb, w_out_b, g_final, y_prompt, y_sample,
          state_prompt, state_sample, k_prompt, v_prompt, k_sample, v_sample):
    def rows(a):
        return a.rearrange("a b d -> (a b) d")

    def tile_of(prompt, sample):
        return lambda t: sample if is_sample(t) else prompt[ds(t * P, P), :]

    def heads(a):
        return a.rearrange("a t h d -> (a t) (h d)")

    xnT, oT = (nc.dram_tensor(n, (D, TOK), F32).ap() for n in ("xnT", "oT"))
    o_gla, h_mid = (nc.dram_tensor(n, (TOK, D), F32).ap() for n in ("o_gla", "h_mid"))
    proj_a = nc.dram_tensor("proj_a", (w_in_a.shape[2], TOK), F32).ap()
    proj_b = nc.dram_tensor("proj_b", (4 * D, TOK), F32).ap()
    x_of = tile_of(rows(x_prompt), rows(x_sample))
    h_of = tile_of(h_mid[0:SEQ, :], h_mid[SEQ:TOK, :])

    class Constants:
        pass

    with ExitStack() as stack:
        c = Constants()
        c.scope = Scope(nc, stack, "const")
        build_constants(nc, c)
        normalise(nc, c, x_of, xnT)
        full = w_in_a.shape[2] // P
        project(nc, c, "proja", xnT, [(w_in_a[0], g_norm_a[0], full, proj_a, 0)], tail=w_in_a.shape[2] - full * P)
        gla(nc, c, proj_a, w_alpha2[0], b_alpha[0], g_head_a[0], state_gla[0], state_prompt[0, 0], state_sample[0],
            o_gla)
        out_project(nc, c, "outa", o_gla, False, w_out_a[0], x_of, h_of, xnT=xnT)
        project(nc, c, "projb", xnT, [(w_kv, g_kv, 2 * D // P, proj_b, 0), (w_in_b[0], g_norm_b[0], 2 * D // P,
                                                                           proj_b, 2 * D)])
        prompt_attention(nc, c, proj_b, b_sb[0], heads(k_prompt), heads(v_prompt), oT)
        sample_attention(nc, c, proj_b, b_sb[0], cache_k, cache_v, page_table, heads(k_sample), heads(v_sample), oT)
        out_project(nc, c, "outb", oT, True, w_out_b[0], h_of, None, gain=g_final,
                    y_out=tile_of(rows(y_prompt), rows(y_sample)))


INPUTS = ("x_prompt", "x_sample", "state_gla", "cache_k", "cache_v", "page_table", "g_norm_a", "w_in_a", "w_alpha2",
          "b_alpha", "g_head_a", "w_out_a", "g_kv", "w_kv", "g_norm_b", "w_in_b", "b_sb", "w_out_b", "g_final")
OUTPUTS = (("y_prompt", (1, SEQ, D)), ("y_sample", (NSEQ, TSEQ, D)), ("state_gla_prompt", (1, 1, GH, DK, DV)),
           ("state_gla_sample", (1, NSEQ, GH, DK, DV)), ("k_prompt", (1, SEQ, NH, HD)), ("v_prompt", (1, SEQ, NH, HD)),
           ("k_sample", (NSEQ, TSEQ, NH, HD)), ("v_sample", (NSEQ, TSEQ, NH, HD)))


def kernel(**inputs):
    import concourse.bacc as bacc
    from concourse.bass_utils import run_bass_kernel_spmd

    nc = bacc.Bacc("TRN2", target_bir_lowering=False, num_devices=1)
    arrays, args = {}, []
    for name in INPUTS:
        a = np.ascontiguousarray(inputs[name])
        arrays[f"in_{name}"] = a
        args.append(nc.dram_tensor(f"in_{name}", a.shape, mybir.dt.from_np(a.dtype), kind="ExternalInput").ap())
    for name, shape in OUTPUTS:
        args.append(nc.dram_tensor(f"out_{name}", shape, F32, kind="ExternalOutput").ap())
    trunk(nc, *args)
    result = run_bass_kernel_spmd(nc, [arrays], core_ids=[0])
    return tuple(result.results[0][f"out_{name}"] for name, _ in OUTPUTS)
```

```python
from contextlib import ExitStack

import numpy as np

import concourse.bass as bass
from concourse import mybir

ALU = mybir.AluOpType
ACT = mybir.ActivationFunctionType
F32 = mybir.dt.float32
F32R = mybir.dt.float32r
BF16 = mybir.dt.bfloat16
I32 = mybir.dt.int32
ds = bass.ds

P = 128
D = 1024
KD = D // P
SEQ = 2048
NSEQ, TSEQ = 8, 4
SMP = NSEQ * TSEQ
TOK = SEQ + SMP
NT = SEQ // P
BANK = 512
NCH = SEQ // BANK
GH, DK, DV = 4, 128, 256
RANK = 16
CHUNK = 64
NCK = SEQ // CHUNK
TAU = 16.0
NH, HD = 16, 64
PAIRS = NH // 2
PAGE = 128
EPS = 1e-6
MASKED = -1e30


def over_tiles(engine, step):
    step(0, 0, 0)
    step(1, 0, 1)
    with engine.Fori(1, NT // 2) as i:
        step(i * 2, i, 0)
        step(i * 2 + 1, i, 1)
    step(NT, NT // 2, 0)


def is_sample(t):
    return isinstance(t, int) and t == NT


def rows_of(t):
    return SMP if is_sample(t) else P


def from_tile(t, n):
    return not isinstance(t, int) or t >= n


class Scope:

    def __init__(self, nc, stack, prefix):
        self.nc, self.stack, self.prefix, self.used = nc, stack, prefix, []
        stack.callback(self.close)

    def close(self):
        self.nc.clear_and_free_semaphores(self.used)
        self.nc.all_engine_barrier()

    def sb(self, name, shape, dt=F32):
        return self.stack.enter_context(self.nc.sbuf_tensor(f"{self.prefix}_{name}", shape, dt))

    def ps(self, name, shape, dt=F32):
        return self.stack.enter_context(self.nc.psum_tensor(f"{self.prefix}_{name}", shape, dt))

    def sem(self, name):
        sem = self.nc.alloc_semaphore(f"{self.prefix}_{name}")
        self.used.append(sem)
        return sem

    def sems(self, name, n):
        return [self.sem(f"{name}{i}") for i in range(n)]


def build_constants(nc, c):
    zeroed, c.consts_ready = c.scope.sem("zeroed"), c.scope.sem("consts_ready")
    c.ident = c.scope.sb("ident", [P, P])
    c.ident_bf = c.scope.sb("ident_bf", [P, P], BF16)
    c.diag_mask = c.scope.sb("diag_mask", [P, P], BF16)
    with nc.Block() as block:

        @block.gpsimd
        def _(pool):
            for t in (c.ident, c.ident_bf, c.diag_mask):
                pool.memset(t[:, :], 0.0).then_inc(zeroed, 1)
            pool.wait_ge(zeroed, 3)
            for t in (c.ident, c.ident_bf):
                pool.affine_select(out=t[:, :], in_=t[:, :], compare_op=ALU.not_equal, fill=1.0, base=0,
                                   pattern=[[-1, P]], channel_multiplier=1).then_inc(c.consts_ready, 1)
            pool.affine_select(out=c.diag_mask[:, :], in_=c.diag_mask[:, :], compare_op=ALU.is_gt, fill=MASKED,
                               base=0, pattern=[[-1, P]], channel_multiplier=1).then_inc(c.consts_ready, 1)


def normalise(nc, c, x_tile, xnT):
    with ExitStack() as stack:
        s = Scope(nc, stack, "norm")
        h = s.sb("h", [P, 2, D])
        square = s.sb("square", [P, D])
        xn = s.sb("xn", [P, 2, D])
        xT = s.sb("xT", [P, 2, KD, P])
        sumsq, root, rstd = (s.sb(n, [P, 2]) for n in ("sumsq", "root", "rstd"))
        eps = s.sb("eps", [P, 1])
        turned_ps = s.ps("turned", [P, 2, KD * P])
        h_in, xT_stored = s.sems("h_in", 2), s.sems("xT_stored", 2)
        eps_set, sumsq_made, root_made, rstd_made, xn_made, turned, act_copied, dve_copied = (
            s.sem(n) for n in ("eps_set", "sumsq_made", "root_made", "rstd_made", "xn_made", "turned",
                               "act_copied", "dve_copied"))
        block = stack.enter_context(nc.Block())
        half = KD // 2

        @block.sync
        def _(sp):
            def step(t, i, b):
                n = rows_of(t)
                if from_tile(t, 2):
                    sp.wait_ge(xn_made, t - 1)
                sp.dma_start(h[0:n, b, :], x_tile(t)).then_inc(h_in[b], 16)
            over_tiles(sp, step)

        @block.scalar
        def _(act):
            def copy(t, i, b):
                n = rows_of(t)
                act.wait_ge(turned, t + 1)
                if from_tile(t, 2):
                    act.wait_ge(xT_stored[b], 16 * i)
                act.activation(xT[:, b, 0:half, 0:n],
                               turned_ps[:, b, 0:half * P].rearrange("p (k n) -> p k n", n=P)[:, :, 0:n],
                               ACT.Copy).then_inc(act_copied, 1)

            def step(t, i, b):
                n = rows_of(t)
                act.wait_ge(h_in[b], 16 * i + 16)
                if from_tile(t, 2):
                    act.wait_ge(rstd_made, t - 1)
                act.activation(square[0:n, :], h[0:n, b, :], ACT.Square,
                               accum_out=sumsq[0:n, b:b + 1]).then_inc(sumsq_made, 1)
                act.wait_ge(sumsq_made, t + 1)
                act.activation(root[0:n, b:b + 1], sumsq[0:n, b:b + 1], ACT.Sqrt, scale=1.0 / D,
                               bias=eps[0:n, :]).then_inc(root_made, 1)
                if from_tile(t, 1):
                    copy(t - 1, i if b else i - 1, 1 - b)
            act.wait_ge(eps_set, 1)
            over_tiles(act, step)
            copy(NT, NT // 2, 0)

        @block.vector
        def _(dve):
            def copy(t, i, b):
                n = rows_of(t)
                dve.wait_ge(turned, t + 1)
                if from_tile(t, 2):
                    dve.wait_ge(xT_stored[b], 16 * i)
                dve.tensor_scalar(xT[:, b, half:KD, 0:n],
                                  turned_ps[:, b, half * P:].rearrange("p (k n) -> p k n", n=P)[:, :, 0:n],
                                  1.0, None, ALU.mult).then_inc(dve_copied, 1)

            def step(t, i, b):
                n = rows_of(t)
                dve.wait_ge(root_made, t + 1)
                dve.reciprocal(rstd[0:n, b:b + 1], root[0:n, b:b + 1]).then_inc(rstd_made, 1)
                dve.wait_ge(rstd_made, t + 1)
                if from_tile(t, 2):
                    dve.wait_ge(turned, t - 1)
                dve.tensor_scalar(xn[0:n, b, :], h[0:n, b, :], rstd[0:n, b:b + 1], None,
                                  ALU.mult).then_inc(xn_made, 1)
                if from_tile(t, 1):
                    copy(t - 1, i if b else i - 1, 1 - b)
            dve.memset(eps[:, :], EPS).then_inc(eps_set, 1)
            over_tiles(dve, step)
            copy(NT, NT // 2, 0)

        @block.tensor
        def _(pe):
            def step(t, i, b):
                n = rows_of(t)
                pe.wait_ge(xn_made, t + 1)
                if from_tile(t, 2):
                    pe.wait_ge(act_copied, t - 1)
                    pe.wait_ge(dve_copied, t - 1)
                for k in range(KD):
                    mm = pe.transpose(turned_ps[:, b, k * P:k * P + n], xn[0:n, b, k * P:(k + 1) * P],
                                      c.ident[0:n, 0:n])
                mm.then_inc(turned, 1)
            over_tiles(pe, step)

        @block.gpsimd
        def _(pool):
            def step(t, i, b):
                n = rows_of(t)
                pool.wait_ge(act_copied, t + 1)
                pool.wait_ge(dve_copied, t + 1)
                pool.wait_ge(eps_set, 1)
                col = ds(t * P, n)
                pool.dma_start(xnT.rearrange("(k p) n -> p k n", p=P)[:, :, col],
                               xT[:, b, :, 0:n]).then_inc(xT_stored[b], 16)
            over_tiles(pool, step)
            pool.wait_ge(xT_stored[0], 16 * (NT // 2 + 1))
            pool.wait_ge(xT_stored[1], 16 * (NT // 2))


def project(nc, c, name, xnT, jobs, tail=None):
    with ExitStack() as stack:
        s = Scope(nc, stack, name)
        slab = s.sb("slab", [P, 2, TOK])
        x_hi, x_lo = (s.sb(n, [P, KD, TOK], F32R) for n in ("x_hi", "x_lo"))
        w_raw = s.sb("w_raw", [P, 2, KD, P])
        w_scaled = s.sb("w_scaled", [P, KD, P])
        w_hi, w_lo = (s.sb(n, [P, 2, KD, P], F32R) for n in ("w_hi", "w_lo"))
        gain = s.sb("gain", [P, len(jobs), KD])
        out = s.sb("out", [P, 2, TOK])
        acc = s.ps("acc", [P, NCH + 1, BANK])
        slab_in, w_in, stored = s.sems("slab_in", 2), s.sems("w_in", 2), s.sems("stored", 2)
        gain_in = s.sem("gain_in")
        x_hi_made, x_lo_made, w_scaled_made, w_hi_made, w_lo_made, chunk_done, copied = (
            s.sem(n) for n in ("x_hi_made", "x_lo_made", "w_scaled_made", "w_hi_made", "w_lo_made",
                               "chunk_done", "copied"))
        block = stack.enter_context(nc.Block())
        spans = [(q * BANK, BANK) for q in range(NCH)] + [(SEQ, SMP)]
        n_spans = len(spans)

        def over_blocks(engine, step, skip_first=False):
            done = 0
            for j, (_, _, blocks, _, _) in enumerate(jobs):
                first = 0
                if done == 0:
                    if not skip_first:
                        step(j, 0, 0, 0, 0, P)
                    step(j, 1, 1, 0, 1, P)
                    first = 1
                with engine.Fori(first, blocks // 2) as i:
                    step(j, i * 2, i * 2 + done, i + done // 2, 0, P)
                    step(j, i * 2 + 1, i * 2 + 1 + done, i + done // 2, 1, P)
                done += blocks
            if tail:
                step(len(jobs) - 1, jobs[-1][2], done, done // 2, 0, tail)

        @block.sync
        def _(sp):
            for j, (_, g, _, _, _) in enumerate(jobs):
                sp.dma_start(gain[:, j, :], g.rearrange("(k p) -> p k", p=P), allow_slow_non_contiguous=True).then_inc(gain_in, 16)
            def step(j, jb, n, i, b, width):
                if from_tile(n, 2):
                    sp.wait_ge(w_scaled_made, n - 1)
                src = jobs[j][0].rearrange("(k p) n -> p k n", p=P)[:, :, ds(jb * P, width)]
                sp.dma_start(w_raw[:, b, :, 0:width], src).then_inc(w_in[b], 16)
            step(0, 0, 0, 0, 0, P)
            for k in range(KD):
                if k >= 2:
                    sp.wait_ge(x_lo_made, k - 1)
                sp.dma_start(slab[:, k % 2, :], xnT[k * P:(k + 1) * P, :]).then_inc(slab_in[k % 2], 16)
            over_blocks(sp, step, skip_first=True)

        @block.scalar
        def _(act):
            for k in range(KD):
                act.wait_ge(slab_in[k % 2], 16 * (k // 2 + 1))
                act.activation(x_hi[:, k, :], slab[:, k % 2, :], ACT.Copy).then_inc(x_hi_made, 1)

            def step(j, jb, n, i, b, width):
                for q, (at, size) in enumerate(spans):
                    act.wait_ge(chunk_done, n * n_spans + (q + 1))
                    if q == 0 and from_tile(n, 2):
                        act.wait_ge(stored[b], 16 * i)
                    act.activation(out[:, b, at:at + size], acc[:, q, 0:size], ACT.Copy).then_inc(copied, 1)
            over_blocks(act, step)

        @block.vector
        def _(dve):
            dve.wait_ge(gain_in, 16 * len(jobs))

            def step(j, jb, n, i, b, width):
                dve.wait_ge(w_in[b], 16 * i + 16)
                if from_tile(n, 1):
                    dve.wait_ge(w_lo_made, n)
                dve.tensor_tensor(w_scaled[:, :, 0:width], w_raw[:, b, :, 0:width],
                                  gain[:, j, :].unsqueeze(2).broadcast_to([P, KD, width]),
                                  ALU.mult).then_inc(w_scaled_made, 1)
                dve.wait_ge(w_scaled_made, n + 1)
                if from_tile(n, 2):
                    dve.wait_ge(chunk_done, (n - 1) * n_spans)
                dve.tensor_copy(w_hi[:, b, :, 0:width], w_scaled[:, :, 0:width]).then_inc(w_hi_made, 1)
                dve.wait_ge(w_hi_made, n + 1)
                dve.tensor_tensor(w_lo[:, b, :, 0:width], w_scaled[:, :, 0:width],
                                  w_hi[:, b, :, 0:width].bitcast(F32), ALU.subtract).then_inc(w_lo_made, 1)
            step(0, 0, 0, 0, 0, P)
            for k in range(KD):
                dve.wait_ge(x_hi_made, k + 1)
                dve.tensor_tensor(x_lo[:, k, :], slab[:, k % 2, :], x_hi[:, k, :].bitcast(F32),
                                  ALU.subtract).then_inc(x_lo_made, 1)
            over_blocks(dve, step, skip_first=True)

        @block.tensor
        def _(pe):
            def products(b, width, k, q):
                at, size = spans[q]
                for w, x in ((w_hi, x_hi), (w_lo, x_hi), (w_hi, x_lo)):
                    mm = pe.matmul(acc[:, q, 0:size], w[:, b, k, :], x[:, k, at:at + size],
                                   start=(k == 0 and w is w_hi and x is x_hi), stop=(k == KD - 1 and x is x_lo))
                return mm

            def step(j, jb, n, i, b, width):
                pe.wait_ge(w_lo_made, n + 1)
                if not from_tile(n, 1):
                    for k in range(KD):
                        pe.wait_ge(x_lo_made, k + 1)
                        for q in range(n_spans):
                            mm = products(b, width, k, q)
                            if k == KD - 1:
                                mm.then_inc(chunk_done, 1)
                    return
                for q, (at, size) in enumerate(spans):
                    if from_tile(n, 1):
                        pe.wait_ge(copied, (n - 1) * n_spans + (q + 1))
                    for k in range(KD):
                        mm = products(b, width, k, q)
                    mm.then_inc(chunk_done, 1)
            over_blocks(pe, step)

        @block.gpsimd
        def _(pool):
            def step(j, jb, n, i, b, width):
                pool.wait_ge(copied, n * n_spans + n_spans)
                pool.wait_ge(gain_in, 16 * len(jobs))
                _, _, _, dst, row = jobs[j]
                pool.dma_start(dst[ds(jb * P + row, width), :], out[0:width, b, :]).then_inc(stored[b], 16)
            over_blocks(pool, step)
            total = sum(j[2] for j in jobs)
            pool.wait_ge(stored[0], 16 * (total // 2 + (1 if tail else 0)))
            pool.wait_ge(stored[1], 16 * (total // 2))


def gla(nc, c, projT, w_alpha2, b_alpha, g_head, state_in, state_prompt, state_sample, o_out):
    q_rows, k_rows, v_rows, g_rows, r_rows = 0, GH * DK, 2 * GH * DK, 2 * GH * DK + GH * DV, 2 * GH * DK + 2 * GH * DV
    scale = float(np.float32(DK ** -0.5))
    spans = [(i * BANK, BANK) for i in range(NCH)] + [(SEQ, SMP)]
    with ExitStack() as stack:
        s = Scope(nc, stack, "gla")
        qT, kT, ktT = (s.sb(n, [P, TOK]) for n in ("qT", "kT", "ktT"))
        vgT = s.sb("vgT", [P, 4, TOK])
        rT = s.sb("rT", [RANK, TOK])
        logit, work, b_sum, gap = (s.sb(n, [P, TOK]) for n in ("logit", "work", "b_sum", "gap"))
        keep = s.sb("keep", [P, TOK])
        w2, bias = s.sb("w2", [RANK, DK]), s.sb("bias", [P, 1])
        decay = s.sb("decay", [P, NCK])
        decay_smp = s.sb("decay_smp", [P, NSEQ])
        vg = s.sb("vg", [P, NT + 1, 2 * DV])
        o = s.sb("o", [P, NT + 1, DV])
        square = s.sb("square", [P, DV])
        ke = s.sb("ke", [P, 2, P])
        pT = s.sb("pT", [P, 2, P])
        S = s.sb("S", [P, 4, DV])
        s_in, s_new = s.sb("s_in", [P, NSEQ, DV]), s.sb("s_new", [P, NSEQ, DV])
        ke_smp, pT_smp = s.sb("ke_smp", [SMP, NSEQ, P]), s.sb("pT_smp", [SMP, SMP])
        q_smp = s.sb("q_smp", [P, NSEQ, SMP])
        tok_mask = s.sb("tok_mask", [P, NSEQ, SMP])
        row_mask = s.sb("row_mask", [SMP, NSEQ])
        may, may_smp = s.sb("may", [P, P], I32), s.sb("may_smp", [SMP, SMP], I32)
        mask_work = s.sb("mask_work", [P, P])
        g_gain = s.sb("g_gain", [P, DV])
        sumsq, root, rstd = (s.sb(n, [P, NT + 1]) for n in ("sumsq", "root", "rstd"))
        eps = s.sb("eps", [P, 1])
        tok_ps, kp_ps, o_ps, ds_ps = (s.ps(n, [P, 2, BANK]) for n in ("tok", "kp", "o_acc", "ds"))
        gate = s.sem("head_gate")
        loads = ("q", "k", "v", "g", "w2", "b", "s0")
        ld = {n: s.sem(f"in_{n}") for n in loads}
        once = s.sem("once_in")
        masks, logit_mm, logit_cp, prep, expd, tok_t, tok_cp, kp_t, ke_cp, pt_cp, ds_mm, s_made, o_mm, o_cp, \
            smp_made, ds_smp, s_smp, sum_made, root_made, rstd_made, normed, gated, st = (s.sem(n) for n in (
                "masks", "logit_mm", "logit_cp", "prep", "expd", "tok_t", "tok_cp", "kp_t", "ke_cp", "pt_cp", "ds_mm",
                "s_made", "o_mm", "o_cp", "smp_made", "ds_smp", "s_smp", "sum_made", "root_made", "rstd_made",
                "normed", "gated", "stored"))
        s_zero = s.sem("s_zero")
        N_PREP, N_EXP = 9, 8
        n_stores = 4

        with nc.Block() as block:
            @block.gpsimd
            def _(pool):
                pool.memset(keep[:, :], 1.0).then_inc(masks, 1)
                pool.memset(tok_mask[:, :, :], 1.0).then_inc(masks, 1)
                pool.memset(row_mask[:, :], 1.0).then_inc(masks, 1)
                pool.memset(mask_work[:, :], 1.0).then_inc(masks, 1)
                pool.memset(may[:, :], 0).then_inc(masks, 1)
                pool.wait_ge(masks, 5)
                pool.affine_select(out=keep[:, 0:SEQ], in_=keep[:, 0:SEQ], compare_op=ALU.not_equal, fill=0.0, base=0,
                                   pattern=[[0, NCK], [1, CHUNK]], channel_multiplier=0).then_inc(masks, 1)
                pool.affine_select(out=keep[:, SEQ:], in_=keep[:, SEQ:], compare_op=ALU.not_equal, fill=0.0, base=0,
                                   pattern=[[0, NSEQ], [1, TSEQ]], channel_multiplier=0).then_inc(masks, 1)
                pool.affine_select(out=tok_mask[:, :, :], in_=tok_mask[:, :, :], compare_op=ALU.is_ge, fill=0.0,
                                   base=0, pattern=[[-TSEQ, NSEQ], [1, SMP]], channel_multiplier=0).then_inc(masks, 1)
                pool.affine_select(out=row_mask[:, :], in_=row_mask[:, :], compare_op=ALU.is_ge, fill=0.0,
                                   base=0, pattern=[[-TSEQ, NSEQ]], channel_multiplier=1).then_inc(masks, 1)
                pool.affine_select(out=mask_work[:, :], in_=mask_work[:, :], compare_op=ALU.is_ge, fill=0.0,
                                   base=0, pattern=[[1, P]], channel_multiplier=-1).then_inc(masks, 1)
                pool.wait_ge(masks, 10)
                pool.affine_select(out=tok_mask[:, :, :], in_=tok_mask[:, :, :], compare_op=ALU.is_gt, fill=0.0,
                                   base=TSEQ, pattern=[[TSEQ, NSEQ], [-1, SMP]], channel_multiplier=0).then_inc(masks, 1)
                pool.affine_select(out=row_mask[:, :], in_=row_mask[:, :], compare_op=ALU.is_gt, fill=0.0,
                                   base=TSEQ, pattern=[[TSEQ, NSEQ]], channel_multiplier=-1).then_inc(masks, 1)
                pool.memset(mask_work[0:CHUNK, CHUNK:], 0.0).then_inc(masks, 1)

            @block.vector
            def _(dve):
                dve.memset(pT[:, :, :], 0.0)
                dve.memset(pT_smp[:, :], 0.0)
                dve.memset(eps[:, :], EPS)
                dve.wait_ge(masks, 13)
                dve.tensor_copy(may[:, :], mask_work[:, :]).then_inc(prep, 1)
                dve.wait_ge(prep, 1)
                dve.tensor_tensor(ke_smp[:, :, 0:SMP], tok_mask[0:SMP, :, :],
                                  row_mask[:, :].unsqueeze(2).broadcast_to([SMP, NSEQ, SMP]), ALU.mult).then_inc(prep, 1)
                dve.wait_ge(prep, 2)
                dve.tensor_reduce(mask_work[0:SMP, 0:SMP], ke_smp[:, :, 0:SMP].rearrange("p s n -> p n s"),
                                  mybir.AxisListType.X, ALU.add).then_inc(prep, 1)
                dve.wait_ge(prep, 3)
                dve.tensor_tensor(mask_work[0:SMP, SMP:2 * SMP], mask_work[0:SMP, 0:SMP], may[0:SMP, 0:SMP],
                                  ALU.mult).then_inc(prep, 1)
                dve.wait_ge(prep, 4)
                dve.tensor_copy(may_smp[:, :], mask_work[0:SMP, SMP:2 * SMP]).then_inc(prep, 1)

            @block.sync
            def _(sp):
                sp.dma_start(rT[:, :], projT[r_rows:r_rows + RANK, :]).then_inc(once, 16)
                sp.dma_start(g_gain[:, :], g_head.unsqueeze(0).broadcast_to([P, DV])).then_inc(once, 16)
                sp.wait_ge(once, 32)
        PREP0 = 5

        def out_of(act, h, t):
            n, b = rows_of(t), t % 2
            act.wait_ge(o_mm, h * (NT + 1) + (t + 1))
            if t >= 1:
                act.wait_ge(sum_made, h * (NT + 1) + t)
            act.activation(square[0:n, :], o_ps[0:n, b, 0:DV], ACT.Square,
                           accum_out=sumsq[0:n, t:t + 1]).then_inc(sum_made, 1)
            act.activation(o[0:n, t, :], o_ps[0:n, b, 0:DV], ACT.Copy).then_inc(o_cp, 1)

        def states(dve, h, t):
            for half in range(2):
                ck = 2 * t + half
                dve.wait_ge(ds_mm, h * NCK + (ck + 1))
                if t >= 1:
                    dve.wait_ge(o_mm, h * (NT + 1) + t)
                if ck >= 1:
                    dve.wait_ge(s_made, h * NCK + ck)
                else:
                    dve.wait_ge(s_zero, h + 1)
                dve.scalar_tensor_tensor(out=S[:, (ck + 1) % 4, :], in0=S[:, ck % 4, :], scalar=decay[:, ck:ck + 1],
                                         in1=ds_ps[:, half, 0:DV], op0=ALU.mult, op1=ALU.add).then_inc(s_made, 1)

        block = stack.enter_context(nc.Block())

        @block.sync
        def _(sp):
            sp.sem_inc(gate, 1)
            with sp.Fori(0, GH) as h:
                sp.wait_ge(gate, h * 4 + 4)
                sp.wait_ge(once, 32)
                sp.dma_start(w2[:, :], w_alpha2[:, ds(h * DK, DK)]).then_inc(ld["w2"], 16)
                sp.dma_start(bias[:, :], b_alpha.rearrange("(n o) -> n o", o=1)[ds(h * DK, DK), :]).then_inc(ld["b"], 16)
                sp.dma_start(qT[:, :], projT[ds(h * DK + q_rows, DK), :]).then_inc(ld["q"], 16)
                sp.dma_start(kT[:, :], projT[ds(h * DK + k_rows, DK), :]).then_inc(ld["k"], 16)
                sp.dma_start(vgT[:, 2:4, :], projT[ds(h * DV + g_rows, DV), :].rearrange("(b p) n -> p b n", p=P)
                             ).then_inc(ld["g"], 16)
                sp.dma_start(vgT[:, 0:2, :], projT[ds(h * DV + v_rows, DV), :].rearrange("(b p) n -> p b n", p=P)
                             ).then_inc(ld["v"], 16)
                sp.dma_start(s_in[:, :, :].unsqueeze(2), state_in.rearrange("s h k v -> k s h v")[:, :, ds(h, 1), :]).then_inc(ld["s0"], 16)
                sp.wait_ge(s_made, h * NCK + NCK)
                sp.dma_start(state_prompt.rearrange("h k v -> k h v")[:, ds(h, 1), :], S[:, 0:1, :]).then_inc(st, 16)
                sp.wait_ge(gated, h * 2 + 2)
                sp.wait_ge(s_smp, h * NSEQ + NSEQ)
                sp.dma_start(state_sample.rearrange("s h k v -> k s h v")[:, :, ds(h, 1), :],
                             s_new[:, :, :].unsqueeze(2)).then_inc(st, 16)
                sp.dma_start(o_out[0:SEQ, :].rearrange("(t p) n -> p t n", p=P)[:, :, ds(h * DV, DV)],
                             o[:, 0:NT, :]).then_inc(st, 16)
                sp.dma_start(o_out[SEQ:TOK, ds(h * DV, DV)], o[0:SMP, NT, :]).then_inc(st, 16)
                sp.wait_ge(st, h * (16 * n_stores) + 16 * n_stores)
                sp.sem_inc(gate, 1)

        @block.tensor
        def _(pe):
            pe.sem_inc(gate, 1)
            logit_banks = [tok_ps[:, 0], tok_ps[:, 1], o_ps[:, 0], o_ps[:, 1], kp_ps[:, 0]]
            with pe.Fori(0, GH) as h:
                pe.wait_ge(gate, h * 4 + 4)
                pe.wait_ge(ld["w2"], h * 16 + 16)
                for (at, n), bank in zip(spans, logit_banks):
                    pe.matmul(bank[:, 0:n], w2[:, :], rT[:, at:at + n], start=True, stop=True).then_inc(logit_mm, 1)

                def to_tokens(t):
                    n, at = rows_of(t), t * P
                    b = t % 2
                    if t >= 2:
                        pe.wait_ge(tok_cp, h * (NT + 1) + (t - 1))
                    for j in range(4):
                        mm = pe.transpose(tok_ps[0:n, b, j * P:(j + 1) * P], vgT[:, j, at:at + n], c.ident[:, :])
                    mm.then_inc(tok_t, 1)
                    if t >= 2:
                        pe.wait_ge(ke_cp, h * (NT + 1) + (t - 1))
                        pe.wait_ge(pt_cp, h * (NT + 1) + (t - 1))
                    pe.transpose(kp_ps[0:n, b, 0:P], kT[:, at:at + n], c.ident[:, :])
                    pe.matmul(kp_ps[0:n, b, P:P + n], ktT[:, at:at + n], qT[:, at:at + n],
                              start=True, stop=True).then_inc(kp_t, 1)

                pe.wait_ge(prep, h * N_PREP + (PREP0 + N_PREP))
                pe.wait_ge(ld["v"], h * 16 + 16)
                pe.wait_ge(logit_cp, h * 5 + 5)
                to_tokens(0)
                for t in range(NT):
                    to_tokens(t + 1)
                    b = t % 2
                    pe.wait_ge(tok_cp, h * (NT + 1) + (t + 1))
                    pe.wait_ge(ke_cp, h * (NT + 1) + (t + 1))
                    pe.wait_ge(pt_cp, h * (NT + 1) + (t + 1))
                    if t >= 1:
                        pe.wait_ge(s_made, h * NCK + 2 * t)
                    for half in range(2):
                        r = slice(half * CHUNK, (half + 1) * CHUNK)
                        pe.matmul(ds_ps[:, half, 0:DV], ke[r, b, :], vg[r, t, 0:DV], start=True,
                                  stop=True).then_inc(ds_mm, 1)
                    if t >= 2:
                        pe.wait_ge(o_cp, h * (NT + 1) + (t - 1))
                    pe.matmul(o_ps[:, b, 0:DV], pT[:, b, :], vg[:, t, 0:DV], start=True, stop=True)
                    for half in range(2):
                        ck = 2 * t + half
                        if ck >= 1:
                            pe.wait_ge(s_made, h * NCK + ck)
                        else:
                            pe.wait_ge(s_zero, h + 1)
                        r = slice(half * CHUNK, (half + 1) * CHUNK)
                        mm = pe.matmul(o_ps[r, b, 0:DV], qT[:, ck * CHUNK:(ck + 1) * CHUNK], S[:, ck % 4, :],
                                       start=False, stop=True, skip_group_check=True)
                    mm.then_inc(o_mm, 1)
                t, b = NT, NT % 2
                pe.wait_ge(tok_cp, h * (NT + 1) + (t + 1))
                pe.wait_ge(pt_cp, h * (NT + 1) + (t + 1))
                pe.wait_ge(o_cp, h * (NT + 1) + (t - 1))
                pe.wait_ge(smp_made, h * 2 + 2)
                pe.wait_ge(ld["s0"], h * 16 + 16)
                for q in range(NSEQ):
                    pe.matmul(o_ps[0:SMP, b, 0:DV], q_smp[:, q, :], s_in[:, q, :], start=(q == 0), stop=False)
                mm = pe.matmul(o_ps[0:SMP, b, 0:DV], pT_smp[:, :], vg[0:SMP, t, 0:DV], start=False, stop=True)
                mm.then_inc(o_mm, 1)
                pe.wait_ge(s_made, h * NCK + NCK)
                for q in range(NSEQ):
                    if q >= 2:
                        pe.wait_ge(s_smp, h * NSEQ + (q - 1))
                    pe.matmul(ds_ps[:, q % 2, 0:DV], ke_smp[:, q, :], vg[0:SMP, t, 0:DV], start=True,
                              stop=True).then_inc(ds_smp, 1)
                pe.wait_ge(ds_smp, h * NSEQ + NSEQ)
                pe.wait_ge(o_mm, h * (NT + 1) + (NT + 1))
                pe.sem_inc(gate, 1)

        @block.scalar
        def _(act):
            act.sem_inc(gate, 1)
            with act.Fori(0, GH) as h:
                act.wait_ge(gate, h * 4 + 4)
                e0 = h * N_EXP
                act.wait_ge(prep, h * N_PREP + (PREP0 + 1))
                act.activation(work[:, :], work[:, :], ACT.Exp, scale=-1.0).then_inc(expd, 1)
                act.wait_ge(expd, e0 + 1)
                act.activation(work[:, :], work[:, :], ACT.Ln, bias=1.0).then_inc(expd, 1)
                act.wait_ge(prep, h * N_PREP + (PREP0 + 3))
                act.activation(work[:, :], b_sum[:, :], ACT.Exp, scale=1.0 / TAU).then_inc(expd, 1)
                act.activation(logit[:, :], b_sum[:, :], ACT.Exp, scale=-1.0 / TAU).then_inc(expd, 1)
                act.activation(decay[:, :], b_sum[:, CHUNK - 1:SEQ:CHUNK], ACT.Exp, scale=1.0 / TAU)
                act.activation(decay_smp[:, :], b_sum[:, SEQ + TSEQ - 1:TOK:TSEQ], ACT.Exp,
                               scale=1.0 / TAU).then_inc(expd, 1)
                act.wait_ge(prep, h * N_PREP + (PREP0 + 5))
                act.activation(gap[:, :], gap[:, :], ACT.Exp, scale=1.0 / TAU).then_inc(expd, 1)
                act.wait_ge(ld["g"], h * 16 + 16)
                for j, (dst, ready) in enumerate(((work, 6), (b_sum, 5))):
                    act.wait_ge(prep, h * N_PREP + (PREP0 + ready))
                    act.wait_ge(expd, e0 + 5)
                    act.activation(dst[:, :], vgT[:, 2 + j, :], ACT.Sigmoid).then_inc(expd, 1)
                for t in range(NT + 1):
                    n, b = rows_of(t), t % 2
                    act.wait_ge(tok_t, h * (NT + 1) + (t + 1))
                    act.activation(vg[0:n, t, :], tok_ps[0:n, b, :], ACT.Copy).then_inc(tok_cp, 1)
                    if t >= 1:
                        out_of(act, h, t - 1)
                out_of(act, h, NT)
                act.wait_ge(sum_made, h * (NT + 1) + (NT + 1))
                act.activation(root[:, 0:NT], sumsq[:, 0:NT], ACT.Sqrt, scale=1.0 / DV, bias=eps[:, :])
                act.activation(root[0:SMP, NT:], sumsq[0:SMP, NT:], ACT.Sqrt, scale=1.0 / DV,
                               bias=eps[0:SMP, :]).then_inc(root_made, 1)
                act.wait_ge(root_made, h + 1)
                act.sem_inc(gate, 1)

        @block.vector
        def _(dve):
            dve.sem_inc(gate, 1)
            with dve.Fori(0, GH) as h:
                dve.wait_ge(gate, h * 4 + 4)
                dve.wait_ge(ld["b"], h * 16 + 16)
                banks = [tok_ps[:, 0], tok_ps[:, 1], o_ps[:, 0], o_ps[:, 1], kp_ps[:, 0]]
                for j, ((at, n), bank) in enumerate(zip(spans, banks)):
                    dve.wait_ge(logit_mm, h * 5 + (j + 1))
                    dve.tensor_scalar(logit[:, at:at + n], bank[:, 0:n], bias[:, 0:1], None,
                                      ALU.add).then_inc(logit_cp, 1)
                p0, e0 = h * N_PREP, h * N_EXP
                dve.wait_ge(logit_cp, h * 5 + 5)
                dve.scalar_tensor_tensor(out=work[:, :], in0=logit[:, :], scalar=-1.0, in1=logit[:, :], op0=ALU.mult,
                                         op1=ALU.max).then_inc(prep, 1)
                dve.wait_ge(expd, e0 + 2)
                dve.wait_ge(prep, p0 + (PREP0 + 1))
                dve.scalar_tensor_tensor(out=logit[:, :], in0=logit[:, :], scalar=0.0, in1=work[:, :], op0=ALU.min,
                                         op1=ALU.subtract).then_inc(prep, 1)
                dve.wait_ge(prep, p0 + (PREP0 + 2))
                dve.tensor_tensor_scan(b_sum[:, :], keep[:, :], logit[:, :], 0.0, ALU.mult, ALU.add).then_inc(prep, 1)
                dve.wait_ge(prep, p0 + (PREP0 + 3))
                for lo, n, size in ((0, NCK, CHUNK), (SEQ, NSEQ, TSEQ)):
                    v = b_sum[:, lo:lo + n * size].rearrange("p (c l) -> p c l", l=size)
                    dve.tensor_tensor(gap[:, lo:lo + n * size].rearrange("p (c l) -> p c l", l=size),
                                      v[:, :, size - 1:size].broadcast_to([P, n, size]), v,
                                      ALU.subtract).then_inc(prep, 1)
                dve.wait_ge(ld["q"], h * 16 + 16)
                dve.wait_ge(expd, e0 + 5)
                dve.scalar_tensor_tensor(out=qT[:, :], in0=qT[:, :], scalar=scale, in1=work[:, :], op0=ALU.mult,
                                         op1=ALU.mult).then_inc(prep, 1)
                dve.wait_ge(ld["k"], h * 16 + 16)
                dve.tensor_tensor(ktT[:, :], kT[:, :], logit[:, :], ALU.mult).then_inc(prep, 1)
                dve.wait_ge(expd, e0 + 6)
                dve.wait_ge(prep, p0 + (PREP0 + 7))
                dve.tensor_tensor(kT[:, :], kT[:, :], gap[:, :], ALU.mult).then_inc(prep, 1)
                dve.wait_ge(expd, e0 + 8)
                dve.tensor_tensor(vgT[:, 2, :], vgT[:, 2, :], work[:, :], ALU.mult)
                dve.tensor_tensor(vgT[:, 3, :], vgT[:, 3, :], b_sum[:, :], ALU.mult).then_inc(prep, 1)
                dve.memset(S[:, 0, :], 0.0).then_inc(s_zero, 1)
                for t in range(NT + 1):
                    n, b = rows_of(t), t % 2
                    dve.wait_ge(kp_t, h * (NT + 1) + (t + 1))
                    if 2 <= t < NT:
                        dve.wait_ge(o_mm, h * (NT + 1) + (t - 1))
                        dve.wait_ge(ds_mm, h * NCK + 2 * (t - 1))
                    if t == NT:
                        dve.wait_ge(ds_mm, h * NCK + 2 * (t - 1))
                    dve.tensor_copy(ke[0:n, b, :], kp_ps[0:n, b, 0:P]).then_inc(ke_cp, 1)
                    if t < NT:
                        dve.copy_predicated(pT[:, b, :], may[:, :], kp_ps[:, b, P:2 * P]).then_inc(pt_cp, 1)
                        if t >= 1:
                            states(dve, h, t - 1)
                    else:
                        dve.copy_predicated(pT_smp[:, :], may_smp[:, :], kp_ps[0:SMP, b, P:P + SMP]).then_inc(pt_cp, 1)
                        states(dve, h, t - 1)
                        dve.wait_ge(ke_cp, h * (NT + 1) + (NT + 1))
                        dve.tensor_tensor(ke_smp[:, :, :], ke[0:SMP, b, :].unsqueeze(1).broadcast_to([SMP, NSEQ, P]),
                                          row_mask[:, :].unsqueeze(2).broadcast_to([SMP, NSEQ, P]),
                                          ALU.mult).then_inc(smp_made, 1)
                        dve.tensor_tensor(q_smp[:, :, :], qT[:, SEQ:TOK].unsqueeze(1).broadcast_to([P, NSEQ, SMP]),
                                          tok_mask[:, :, :], ALU.mult).then_inc(smp_made, 1)
                dve.wait_ge(ld["s0"], h * 16 + 16)
                for q in range(NSEQ):
                    dve.wait_ge(ds_smp, h * NSEQ + (q + 1))
                    dve.scalar_tensor_tensor(out=s_new[:, q, :], in0=s_in[:, q, :], scalar=decay_smp[:, q:q + 1],
                                             in1=ds_ps[:, q % 2, 0:DV], op0=ALU.mult, op1=ALU.add).then_inc(s_smp, 1)
                dve.wait_ge(root_made, h + 1)
                dve.reciprocal(rstd[:, 0:NT], root[:, 0:NT])
                dve.reciprocal(rstd[0:SMP, NT:], root[0:SMP, NT:]).then_inc(rstd_made, 1)
                dve.wait_ge(rstd_made, h + 1)
                dve.wait_ge(o_cp, h * (NT + 1) + (NT + 1))
                for t in range(NT + 1):
                    n = rows_of(t)
                    last = dve.scalar_tensor_tensor(out=o[0:n, t, :], in0=o[0:n, t, :], scalar=rstd[0:n, t:t + 1],
                                                    in1=g_gain[0:n, :], op0=ALU.mult, op1=ALU.mult)
                last.then_inc(normed, 1)
                dve.wait_ge(normed, h + 1)
                dve.wait_ge(tok_cp, h * (NT + 1) + (NT + 1))
                dve.tensor_tensor(o[:, 0:NT, :], o[:, 0:NT, :], vg[:, 0:NT, DV:], ALU.mult).then_inc(gated, 1)
                dve.tensor_tensor(o[0:SMP, NT, :], o[0:SMP, NT, :], vg[0:SMP, NT, DV:], ALU.mult).then_inc(gated, 1)
                dve.wait_ge(gated, h * 2 + 2)
                dve.sem_inc(gate, 1)


def out_project(nc, c, name, o_in, transposed, w_out, residual, h_out, xnT=None, gain=None, y_out=None):
    with ExitStack() as stack:
        s = Scope(nc, stack, name)
        w_raw = s.sb("w_raw", [P, 2, D])
        w_hi, w_lo = (s.sb(n, [P, KD, D], F32R) for n in ("w_hi", "w_lo"))
        o = s.sb("o", [P, 2, D])
        oT_hi, oT_lo = (s.sb(n, [P, 2, KD, P], F32R) for n in ("oT_hi", "oT_lo"))
        res, h, xn = (s.sb(n, [P, 2, D]) for n in ("res", "h", "xn"))
        square = s.sb("square", [P, D])
        xT = s.sb("xT", [P, 2, KD, P])
        gains = s.sb("gains", [P, D])
        sumsq, root, rstd = (s.sb(n, [P, 2]) for n in ("sumsq", "root", "rstd"))
        eps = s.sb("eps", [P, 1])
        oT_ps, y_ps, t_ps = s.ps("oT", [P, KD * P]), s.ps("y", [P, 2, D]), s.ps("t", [P, KD * P])
        w_in, o_in_sem, res_in = s.sems("w_in", 2), s.sems("o_in", 2), s.sems("res_in", 2)
        h_stored, x_stored = s.sems("h_stored", 2), s.sems("x_stored", 2)
        gain_in, eps_set, w_hi_made, w_lo_made, o_turned, hi_made, lo_made, y_made, h_made, sumsq_made, root_made, \
            rstd_made, xn_made, x_turned, x_copied = (s.sem(n) for n in (
                "gain_in", "eps_set", "w_hi_made", "w_lo_made", "o_turned", "hi_made", "lo_made", "y_made", "h_made",
                "sumsq_made", "root_made", "rstd_made", "xn_made", "x_turned", "x_copied"))
        block = stack.enter_context(nc.Block())

        def lagged(i, b):
            return i if b else i - 1

        @block.sync
        def _(sp):
            if gain is not None:
                sp.dma_start(gains[:, :], gain.unsqueeze(0).broadcast_to([P, D])).then_inc(gain_in, 16)
            for k in range(KD):
                if k >= 2:
                    sp.wait_ge(w_lo_made, k - 1)
                sp.dma_start(w_raw[:, k % 2, :], w_out[k * P:(k + 1) * P, :]).then_inc(w_in[k % 2], 16)

            def step(t, i, b):
                n = rows_of(t)
                if from_tile(t, 2):
                    if transposed:
                        sp.wait_ge(lo_made, t - 1)
                    else:
                        sp.wait_ge(o_turned, t - 1)
                if transposed:
                    sp.dma_start(o[:, b, :].rearrange("p (k n) -> p k n", n=P)[:, :, 0:n],
                                 o_in.rearrange("(k p) n -> p k n", p=P)[:, :, ds(t * P, n)]).then_inc(o_in_sem[b], 16)
                else:
                    sp.dma_start(o[0:n, b, :], o_in[ds(t * P, n), :]).then_inc(o_in_sem[b], 16)
                if from_tile(t, 2):
                    sp.wait_ge(h_made, t - 1)
                sp.dma_start(res[0:n, b, :], residual(t)).then_inc(res_in[b], 16)
            over_tiles(sp, step)

        @block.scalar
        def _(act):
            for k in range(KD):
                act.wait_ge(w_in[k % 2], 16 * (k // 2 + 1))
                act.activation(w_hi[:, k, :], w_raw[:, k % 2, :], ACT.Copy).then_inc(w_hi_made, 1)
            act.wait_ge(eps_set, 1)

            def norm(t, i, b):
                n = rows_of(t)
                act.wait_ge(h_made, t + 1)
                if from_tile(t, 2):
                    act.wait_ge(rstd_made, t - 1)
                act.activation(square[0:n, :], h[0:n, b, :], ACT.Square,
                               accum_out=sumsq[0:n, b:b + 1]).then_inc(sumsq_made, 1)
                act.wait_ge(sumsq_made, t + 1)
                act.activation(root[0:n, b:b + 1], sumsq[0:n, b:b + 1], ACT.Sqrt, scale=1.0 / D,
                               bias=eps[0:n, :]).then_inc(root_made, 1)

            def step(t, i, b):
                n = rows_of(t)
                if from_tile(t, 2):
                    act.wait_ge(y_made, t - 1)
                if transposed:
                    act.wait_ge(o_in_sem[b], 16 * i + 16)
                    act.activation(oT_hi[:, b, :, 0:n], o[:, b, :].rearrange("p (k n) -> p k n", n=P)[:, :, 0:n],
                                   ACT.Copy).then_inc(hi_made, 1)
                else:
                    act.wait_ge(o_turned, t + 1)
                    act.activation(oT_hi[:, b, :, 0:n], oT_ps[:, :].rearrange("p (k n) -> p k n", n=P)[:, :, 0:n],
                                   ACT.Copy).then_inc(hi_made, 1)
                if from_tile(t, 1):
                    norm(t - 1, lagged(i, b), 1 - b)
            over_tiles(act, step)
            norm(NT, NT // 2, 0)

        @block.vector
        def _(dve):
            for k in range(KD):
                dve.wait_ge(w_hi_made, k + 1)
                dve.tensor_tensor(w_lo[:, k, :], w_raw[:, k % 2, :], w_hi[:, k, :].bitcast(F32),
                                  ALU.subtract).then_inc(w_lo_made, 1)
            dve.memset(eps[:, :], EPS).then_inc(eps_set, 1)
            if gain is not None:
                dve.wait_ge(gain_in, 16)

            def after(t, i, b):
                n = rows_of(t)
                dve.wait_ge(y_made, t + 1)
                dve.wait_ge(res_in[b], 16 * i + 16)
                if from_tile(t, 2):
                    if h_out is not None:
                        dve.wait_ge(h_stored[b], 16 * i)
                    dve.wait_ge(xn_made, t - 1)
                dve.tensor_tensor(h[0:n, b, :], y_ps[0:n, b, :], res[0:n, b, :], ALU.add).then_inc(h_made, 1)

            def finish(t, i, b):
                n = rows_of(t)
                dve.wait_ge(root_made, t + 1)
                dve.reciprocal(rstd[0:n, b:b + 1], root[0:n, b:b + 1]).then_inc(rstd_made, 1)
                dve.wait_ge(rstd_made, t + 1)
                if xnT is not None:
                    if from_tile(t, 2):
                        dve.wait_ge(x_turned, t - 1)
                    dve.tensor_scalar(xn[0:n, b, :], h[0:n, b, :], rstd[0:n, b:b + 1], None,
                                      ALU.mult).then_inc(xn_made, 1)
                else:
                    if from_tile(t, 2):
                        dve.wait_ge(x_stored[b], 16 * i)
                    dve.scalar_tensor_tensor(out=xn[0:n, b, :], in0=h[0:n, b, :], scalar=rstd[0:n, b:b + 1],
                                             in1=gains[0:n, :], op0=ALU.mult, op1=ALU.mult).then_inc(xn_made, 1)

            def copy_x(t, i, b):
                n = rows_of(t)
                dve.wait_ge(x_turned, t + 1)
                if from_tile(t, 2):
                    dve.wait_ge(x_stored[b], 16 * i)
                dve.tensor_scalar(xT[:, b, :, 0:n], t_ps[:, :].rearrange("p (k n) -> p k n", n=P)[:, :, 0:n],
                                  1.0, None, ALU.mult).then_inc(x_copied, 1)

            def step(t, i, b):
                n = rows_of(t)
                dve.wait_ge(hi_made, t + 1)
                if from_tile(t, 2):
                    dve.wait_ge(y_made, t - 1)
                src = (o[:, b, :] if transposed else oT_ps[:, :]).rearrange("p (k n) -> p k n", n=P)[:, :, 0:n]
                dve.tensor_tensor(oT_lo[:, b, :, 0:n], src, oT_hi[:, b, :, 0:n].bitcast(F32),
                                  ALU.subtract).then_inc(lo_made, 1)
                if from_tile(t, 1):
                    after(t - 1, lagged(i, b), 1 - b)
                    finish(t - 1, lagged(i, b), 1 - b)
                if xnT is not None and from_tile(t, 2):
                    copy_x(t - 2, i - 1, b)
            over_tiles(dve, step)
            after(NT, NT // 2, 0)
            finish(NT, NT // 2, 0)
            if xnT is not None:
                copy_x(NT - 1, NT // 2 - 1, 1)
                copy_x(NT, NT // 2, 0)

        @block.tensor
        def _(pe):
            def turn(t, i, b):
                n = rows_of(t)
                pe.wait_ge(o_in_sem[b], 16 * i + 16)
                if from_tile(t, 1):
                    pe.wait_ge(lo_made, t)
                for k in range(KD):
                    mm = pe.transpose(oT_ps[:, k * P:k * P + n], o[0:n, b, k * P:(k + 1) * P], c.ident[0:n, 0:n])
                mm.then_inc(o_turned, 1)

            def turn_x(t, i, b):
                n = rows_of(t)
                pe.wait_ge(xn_made, t + 1)
                if from_tile(t, 1):
                    pe.wait_ge(x_copied, t)
                for k in range(KD):
                    mm = pe.transpose(t_ps[:, k * P:k * P + n], xn[0:n, b, k * P:(k + 1) * P], c.ident[0:n, 0:n])
                mm.then_inc(x_turned, 1)

            def products(t, i, b):
                by_part = not from_tile(t, 1)
                pe.wait_ge(lo_made, t + 1)
                if from_tile(t, 2):
                    pe.wait_ge(h_made, t - 1)
                for j in range(D // BANK):
                    for k in range(KD):
                        if by_part and j == 0:
                            pe.wait_ge(w_lo_made, k + 1)
                        for w, x in ((w_hi, oT_hi), (w_lo, oT_hi), (w_hi, oT_lo)):
                            mm = pe.matmul(y_ps[:, b, j * BANK:(j + 1) * BANK], x[:, b, k, :],
                                           w[:, k, j * BANK:(j + 1) * BANK],
                                           start=(k == 0 and w is w_hi and x is oT_hi),
                                           stop=(k == KD - 1 and x is oT_lo))
                mm.then_inc(y_made, 1)

            def step(t, i, b):
                if not transposed:
                    turn(t, i, b)
                if from_tile(t, 1):
                    products(t - 1, lagged(i, b), 1 - b)
                if xnT is not None and from_tile(t, 2):
                    turn_x(t - 2, i - 1, b)
            over_tiles(pe, step)
            products(NT, NT // 2, 0)
            if xnT is not None:
                turn_x(NT - 1, NT // 2 - 1, 1)
                turn_x(NT, NT // 2, 0)

        @block.gpsimd
        def _(pool):
            def step(t, i, b):
                n = rows_of(t)
                if h_out is not None:
                    pool.wait_ge(h_made, t + 1)
                    pool.wait_ge(eps_set, 1)
                    pool.dma_start(h_out(t), h[0:n, b, :]).then_inc(h_stored[b], 16)
                pool.wait_ge(x_copied if xnT is not None else xn_made, t + 1)
                pool.wait_ge(eps_set, 1)
                if xnT is not None:
                    pool.dma_start(xnT.rearrange("(k p) n -> p k n", p=P)[:, :, ds(t * P, n)],
                                   xT[:, b, :, 0:n]).then_inc(x_stored[b], 16)
                else:
                    pool.dma_start(y_out(t), xn[0:n, b, :]).then_inc(x_stored[b], 16)
            over_tiles(pool, step)
            for stored in ([h_stored] if h_out is not None else []) + [x_stored]:
                pool.wait_ge(stored[0], 16 * (NT // 2 + 1))
                pool.wait_ge(stored[1], 16 * (NT // 2))


def chunks_of(tile):
    n, out = (tile + 1) * P, []
    while n > 0:
        out.append((max(0, n - 1024), n))
        n -= 1024
    return out


def attention_schedule():
    def logits(off, e, g):
        return [("z", off, e, t, j) for t in range(4 * g, 4 * g + 4) for j in range(len(chunks_of(t)))]

    def merge(main, beside):
        out, done = [], 0
        for m, v in enumerate(main):
            want = -(-len(beside) * (m + 1) // len(main))
            out += beside[done:want] + [v]
            done = want
        return out

    split = [[("split", 1, e, c) for c in range(NCH)] for e in range(2)]
    turn = [("turn", 1, m) for m in range(8)]
    silu = [("silu", 1, c) for c in range(NCH - 1)]
    extra = {(0, 0): [("silu", 0, NCH - 1)], (0, 3): split[0], (1, 1): turn[:4], (1, 2): turn[4:],
             (1, 3): split[1] + silu}
    groups = [(0, e, g) for e in range(2) for g in range(4)] + [(1, 0, 0)]
    order = []
    for n, (_, e, g) in enumerate(groups[:-1]):
        values = [("a", 0, e, g, j) for j in reversed(range(4 * g + 4))]
        order += merge(merge(values, logits(*groups[n + 1])), extra.get((e, g), []))
    return split[0] + logits(1, 0, 0) + turn + silu + split[1], order


def prompt_attention(nc, c, projT, b_sb, k_out, v_out, oT):
    k_rows, v_rows, q_rows, g_rows = 0, D, 2 * D, 3 * D
    first, order = attention_schedule()
    every_a = [x for x in order if x[0] == "a"]
    n_z, n_r = (sum(x[0] in kinds for x in order) for kinds in (("z",), ("a", "turn")))
    n_a = len(every_a)
    z_first, ring_first = (sum(x[0] in kinds for x in first) for kinds in (("z",), ("turn",)))
    z_place = {x[1:]: z_first + n for n, x in enumerate(x for x in order if x[0] == "z")}
    ring_place = {x: ring_first + n for n, x in enumerate(x for x in order if x[0] in ("a", "turn"))}
    ring_of_last = {x: ring_first + n for n, x in enumerate(every_a)}
    a_place = {x: n for n, x in enumerate(every_a)}
    LAST = PAIRS - 1
    START = -1
    CREDIT = 2
    last_of = {t: len(chunks_of(t)) - 1 for t in range(NT)}

    def z_at(off, e, t, j):
        if (off, e, t, j) in z_place:
            return z_place[(off, e, t, j)]
        return z_place[(off + 1, e, t, j)] - n_z

    def tile_before(off, e, t, by):
        n = (off * 2 + e) * NT + t - by
        return n // (2 * NT), n // NT % 2, n % NT

    def last_z(off, e, t):
        if off < 0:
            return last_z(off + 1, e, t) - n_z
        return z_at(off, e, t, last_of[t])

    def ring_at(pr, x):
        return (ring_of_last if pr is LAST else ring_place)[x]

    def last_ring(pr, off, e, g):
        return ring_at(None if off < 0 else pr, ("a", 0, e, g, 0)) + off * n_r

    with ExitStack() as stack:
        s = Scope(nc, stack, "att")
        raw_k, raw_v, raw_g, twice_k, twice_q = (s.sb(n, [P, SEQ]) for n in (
            "raw_k", "raw_v", "raw_g", "twice_k", "twice_q"))
        q_parts, k_hi, k_lo = (s.sb(n, [P, 2, SEQ], F32R) for n in ("q_parts", "k_hi", "k_lo"))
        silu = s.sb("silu", [P, SEQ])
        k_tok, v_tok = (s.sb(n, [P, NT, P]) for n in ("k_tok", "v_tok"))
        v_used = s.sb("v_used", [P, 2, NT, HD])
        w_even, w_odd = s.sb("w_even", [P, 4, SEQ - BANK]), s.sb("w_odd", [P, 4, SEQ])
        rest = s.sb("rest", [P, 2, SEQ + 1])
        zero, one = s.sb("zero", [P, 1]), s.sb("one", [P, 1])
        wT = s.sb("wT", [P, 2, BANK])
        out = s.sb("out", [P, SEQ])
        bias_all = s.sb("bias_all", [P, 2, NH])
        bias = s.sb("bias", [P, 2, 2])
        z_ps = s.ps("z", [P, 2, 1024])
        wT_ps = s.ps("wT_acc", [P, 2, BANK])
        o_ps = s.ps("o_acc", [P, 2, BANK])
        in_k, in_v, in_g, in_twice, bias_in, kv_stored = (s.sem(n) for n in (
            "in_k", "in_v", "in_g", "in_twice", "bias_in", "kv_stored"))
        out_stored, one_set = s.sems("out_stored", 2), s.sem("one_set")
        setup, bias_set, sig_made, silu_made, hi_made, lo_made, v_set, z_made, sigmoids, scanned, w_made, ring_turned, \
            ring_copied, av_done, o_gated = (s.sem(n) for n in (
                "setup", "bias_set", "sig_made", "silu_made", "hi_made", "lo_made", "v_set", "z_made", "sigmoids",
                "scanned", "w_made", "ring_turned", "ring_copied", "av_done", "o_gated"))
        block = stack.enter_context(nc.Block())

        def group_no(e, g):
            return 4 * e + g

        def quarter(c):
            return slice(c * BANK, (c + 1) * BANK)

        def turn_at(pr, n):
            if pr is START:
                return n, n % 2
            place = ring_place[("turn", 1, n)]
            return pr * n_r + place, place % 2

        def weights(g, t, at, size):
            if g % 2:
                return w_odd[:, t % 4, at:at + size]
            return w_even[:, t % 4, at - BANK:at - BANK + size]

        def over_pairs(engine, run):
            run(START, first)
            with engine.Fori(0, PAIRS - 1) as pr:
                run(pr, order)
            run(LAST, [x for x in order if x[1] == 0])

        @block.sync
        def _(sp):
            sp.dma_start(bias_all[:, 0, :], b_sb.unsqueeze(0).broadcast_to([P, NH])).then_inc(bias_in, 16)

            def load_head(pair, e):
                for dst, row in ((twice_k, k_rows), (twice_q, q_rows)):
                    for half in range(2):
                        sp.dma_start(dst[half * HD:(half + 1) * HD, :],
                                     projT[ds(pair * P + (row + e * HD), HD), 0:SEQ]).then_inc(in_twice, 16)

            def load(dst, row, pair, sem):
                sp.dma_start(dst[:, :], projT[ds(pair * P + row, P), 0:SEQ]).then_inc(sem, 16)

            def store_out(pair, e):
                sp.wait_ge(o_gated, pair * 8 + (4 * e + 4 + CREDIT))
                sp.dma_start(oT[ds(pair * P + e * HD, HD), 0:SEQ], out[e * HD:(e + 1) * HD, :]
                             ).then_inc(out_stored[e], 16)

            def store_tokens(pair):
                for dst, src in ((k_out, k_tok), (v_out, v_tok)):
                    sp.dma_start(dst.rearrange("(t p) n -> p t n", p=P)[:, :, ds(pair * P, P)],
                                 src[:, :, :]).then_inc(kv_stored, 16)

            load_head(0, 0)
            load(raw_k, k_rows, 0, in_k)
            load(raw_v, v_rows, 0, in_v)
            load(raw_g, g_rows, 0, in_g)
            sp.wait_ge(lo_made, 2 * NCH)
            load_head(0, 1)
            sp.wait_ge(ring_copied, ring_first + CREDIT)
            store_tokens(0)
            with sp.Fori(0, PAIRS - 1) as pr:
                load(raw_k, k_rows + P, pr, in_k)
                load(raw_v, v_rows + P, pr, in_v)
                sp.wait_ge(silu_made, pr * NCH + NCH)
                load(raw_g, g_rows + P, pr, in_g)
                sp.wait_ge(lo_made, pr * (4 * NCH) + 4 * NCH)
                load_head(pr + 1, 0)
                store_out(pr, 0)
                sp.wait_ge(lo_made, pr * (4 * NCH) + 6 * NCH)
                load_head(pr + 1, 1)
                store_out(pr, 1)
                store_tokens(pr + 1)
            store_out(PAIRS - 1, 0)
            store_out(PAIRS - 1, 1)
            sp.wait_ge(kv_stored, 32 * PAIRS)
            for e in range(2):
                sp.wait_ge(out_stored[e], 16 * PAIRS + 1)

        @block.tensor
        def _(pe):
            pe.sem_inc(ring_turned, CREDIT)
            pe.sem_inc(av_done, CREDIT)

            def run(pr, items):
                def value_product(e, g, j):
                    x = ("a", 0, e, g, j)
                    a, lo, r = a_place[x], max(0, j - 4 * g) * P, slice(HD * e, HD * (e + 1))
                    pe.wait_ge(ring_copied, pr * n_r + (ring_at(pr, x) + 1 + CREDIT))
                    mm = pe.matmul(o_ps[r, group_no(e, g) % 2, lo:BANK], v_used[:, e, j, :], wT[:, a % 2, lo:BANK],
                                   start=(j == 4 * g + 3), stop=(j == 0), skip_group_check=True)
                    mm.then_inc(av_done, 1)

                for kind, off, *x in items:
                    if kind == "turn":
                        n, = x
                        ring, bank = turn_at(pr, n)
                        src = raw_k if n < 4 else raw_v
                        pe.wait_ge(in_k if n < 4 else in_v, pr * 16 + 32)
                        pe.wait_ge(ring_copied, ring + (CREDIT - 1))
                        for j in range(4):
                            at = ((n % 4) * 4 + j) * P
                            mm = pe.transpose(wT_ps[:, bank, j * P:(j + 1) * P], src[:, at:at + P], c.ident[:, :])
                        mm.then_inc(ring_turned, 1)
                    elif kind == "z":
                        e, t, j = x
                        lo, hi = chunks_of(t)[j]
                        n = z_at(off, e, t, j)
                        if t == 0:
                            pe.wait_ge(lo_made, pr * (4 * NCH) + (4 * off + 2 * e + 2) * NCH)
                        if not (pr is START and t < 2):
                            pe.wait_ge(sigmoids, pr * n_z + (n - 1))
                        for at in range(lo, hi, BANK):
                            size = min(BANK, hi - at)
                            dst = z_ps[:, n % 2, at - lo:at - lo + size]
                            diagonal = at + size == (t + 1) * P
                            if diagonal:
                                pe.matmul(dst[:, size - P:size], c.ident_bf[:, :], c.diag_mask[:, :], start=True,
                                          stop=False, skip_group_check=True)
                            q = q_parts[:, e, t * P:(t + 1) * P]
                            pe.matmul(dst, q, k_hi[:, e, at:at + size], start=not diagonal,
                                      stop=False, skip_group_check=True)
                            mm = pe.matmul(dst, q, k_lo[:, e, at:at + size], start=False,
                                           stop=True, skip_group_check=True)
                        mm.then_inc(z_made, 1)
                    elif kind == "a":
                        e, g, j = x
                        item = ("a", 0, e, g, j)
                        ring, gn = ring_at(pr, item), group_no(e, g)
                        is_first = j == 4 * g + 3
                        if is_first:
                            pe.wait_ge(w_made, pr * n_z + (last_z(0, e, j) + 1))
                            pe.wait_ge(o_gated, pr * 8 + (gn - 1 + CREDIT))
                            if g == 0:
                                pe.wait_ge(v_set, pr * 2 + (e + 1))
                        pe.wait_ge(ring_copied, pr * n_r + (ring - 1 + CREDIT))
                        for t in range(max(4 * g, j), 4 * g + 4):
                            at = SEQ - (t + 1) * P + j * P
                            mm = pe.transpose(wT_ps[:, ring % 2, (t % 4) * P:(t % 4 + 1) * P],
                                              weights(g, t, at, P), c.ident[:, :])
                        mm.then_inc(ring_turned, 1)
                        if not is_first:
                            value_product(e, g, j + 1)
                        if j == 0:
                            value_product(e, g, 0)
            over_pairs(pe, run)

        @block.scalar
        def _(act):
            act.sem_inc(ring_copied, CREDIT)

            def run(pr, items):
                before = pr is START
                for kind, off, *x in items:
                    if kind == "silu":
                        c, = x
                        act.wait_ge(in_g, pr * 16 + (16 * off + 16))
                        if not before:
                            act.wait_ge(o_gated, pr * 8 + (8 * off - 3 + c + CREDIT))
                        act.activation(silu[:, quarter(c)], raw_g[:, quarter(c)], ACT.Sigmoid).then_inc(sig_made, 1)
                    elif kind == "split":
                        e, c = x
                        if c == 0:
                            act.wait_ge(in_twice, pr * 128 + (128 * off + 64 * e + 64))
                            if not before:
                                act.wait_ge(z_made, pr * n_z + (last_z(0, e, NT - 1) + 1))
                        act.activation(k_hi[:, e, quarter(c)], twice_k[:, quarter(c)], ACT.Copy)
                        act.activation(q_parts[:, e, quarter(c)], twice_q[:, quarter(c)], ACT.Copy).then_inc(hi_made, 1)
                    elif kind == "turn":
                        n, = x
                        dst = k_tok if n < 4 else v_tok
                        ring, bank = turn_at(pr, n)
                        act.wait_ge(ring_turned, ring + (1 + CREDIT))
                        if not before and n == 0:
                            act.wait_ge(kv_stored, pr * 32 + 32)
                        if not before and n == 4:
                            act.wait_ge(v_set, pr * 2 + 2)
                        act.activation(dst[:, (n % 4) * 4:(n % 4) * 4 + 4, :],
                                       wT_ps[:, bank, :].rearrange("p (t n) -> p t n", n=P),
                                       ACT.Copy).then_inc(ring_copied, 1)
                    elif kind == "z":
                        e, t, j = x
                        lo, hi = chunks_of(t)[j]
                        n, at, g = z_at(off, e, t, j), SEQ - (t + 1) * P, t // 4
                        if t == 0:
                            act.wait_ge(bias_set, pr * 2 + (2 * off + e + 1))
                        if j == 0 and not before:
                            g_off, gn = divmod(off * 8 + group_no(e, g) - 2, 8)
                            act.wait_ge(ring_turned, pr * n_r + (last_ring(pr, g_off, gn // 4, gn % 4) + 1 + CREDIT))
                        if j == 0 and not (before and t < 2):
                            act.wait_ge(w_made, pr * n_z + (last_z(*tile_before(off, e, t, 2)) + 1))
                        act.wait_ge(z_made, pr * n_z + (n + 1))
                        act.activation(weights(g, t, at + lo, hi - lo), z_ps[:, n % 2, 0:hi - lo],
                                       ACT.Sigmoid, bias=bias[:, 0, e:e + 1], scale=HD ** -0.5)
                        act.activation(rest[:, t % 2, at + lo:at + hi], z_ps[:, n % 2, 0:hi - lo],
                                       ACT.Sigmoid, bias=bias[:, 1, e:e + 1], scale=-HD ** -0.5).then_inc(sigmoids, 1)
                    else:
                        e, g, j = x
                        item = ("a", 0, e, g, j)
                        a, ring, lo = a_place[item], ring_at(pr, item), max(0, j - 4 * g) * P
                        act.wait_ge(ring_turned, pr * n_r + (ring + 1 + CREDIT))
                        act.wait_ge(av_done, pr * n_a + (a - 1 + CREDIT))
                        act.activation(wT[:, a % 2, lo:BANK], wT_ps[:, ring % 2, lo:BANK], ACT.Copy
                                       ).then_inc(ring_copied, 1)
            over_pairs(act, run)

        @block.vector
        def _(dve):
            dve.sem_inc(o_gated, CREDIT)
            for e in range(2):
                dve.sem_inc(out_stored[e], 1)
            dve.memset(zero[:, :], 0.0)
            dve.memset(rest[:, :, SEQ:], 1.0).then_inc(setup, 1)
            dve.wait_ge(bias_in, 16)
            dve.tensor_scalar(bias_all[:, 1, :], bias_all[:, 0, :], -1.0, None, ALU.mult).then_inc(setup, 1)
            dve.wait_ge(setup, 2)

            def run(pr, items):
                before = pr is START
                for kind, off, *x in items:
                    if kind == "silu":
                        c, = x
                        dve.wait_ge(sig_made, pr * NCH + (NCH * off + c + 1))
                        dve.tensor_tensor(silu[:, quarter(c)], silu[:, quarter(c)], raw_g[:, quarter(c)],
                                          ALU.mult).then_inc(silu_made, 1)
                    elif kind == "split":
                        e, c = x
                        if c == 0:
                            if not before:
                                dve.wait_ge(sigmoids, pr * n_z + (last_z(0, e, NT - 1) + 1))
                            dve.wait_ge(setup, 2)
                            dve.tensor_scalar(bias[:, :, e:e + 1], bias_all[:, :, ds(pr * 2 + (2 + e), 1)], 1.0, None,
                                              ALU.mult).then_inc(bias_set, 1)
                        dve.wait_ge(hi_made, pr * (2 * NCH) + ((2 + e) * NCH + c + 1))
                        dve.tensor_tensor(k_lo[:, e, quarter(c)], twice_k[:, quarter(c)],
                                          k_hi[:, e, quarter(c)].bitcast(F32), ALU.subtract).then_inc(lo_made, 1)
                        dve.tensor_tensor(q_parts[HD:P, e, quarter(c)], twice_q[HD:P, quarter(c)],
                                          q_parts[HD:P, e, quarter(c)].bitcast(F32), ALU.subtract).then_inc(lo_made, 1)
                    elif kind == "z":
                        e, t, j = x
                        lo, hi = chunks_of(t)[j]
                        n, at, b = z_at(off, e, t, j), SEQ - (t + 1) * P, t % 2
                        dve.wait_ge(sigmoids, pr * n_z + (n + 1))
                        if not (before and t == 0):
                            dve.wait_ge(w_made, pr * n_z + n)
                        products = rest[:, b, at + lo:at + hi][:, ::-1]
                        dve.tensor_tensor_scan(products, products, zero[:, 0:1].broadcast_to([P, hi - lo]),
                                               rest[:, b, at + hi:at + hi + 1], ALU.mult, ALU.add).then_inc(scanned, 1)
                        dve.wait_ge(scanned, pr * n_z + (n + 1))
                        these = weights(t // 4, t, at + lo, hi - lo)
                        dve.tensor_tensor(these, these, rest[:, b, at + lo + 1:at + hi + 1],
                                          ALU.mult).then_inc(w_made, 1)
                    elif kind == "a" and x[2] == 0:
                        e, g, _ = x
                        gn, r = group_no(e, g), slice(HD * e, HD * (e + 1))
                        if g == 0:
                            dve.wait_ge(out_stored[e], pr * 16 + 1)
                        dve.wait_ge(silu_made, pr * NCH + (g + 1))
                        dve.wait_ge(av_done, pr * n_a + (a_place[("a", 0, e, g, 0)] + 1 + CREDIT))
                        dve.tensor_tensor(out[r, g * BANK:(g + 1) * BANK], o_ps[r, gn % 2, :],
                                          silu[r, g * BANK:(g + 1) * BANK], ALU.mult).then_inc(o_gated, 1)
            over_pairs(dve, run)

        @block.gpsimd
        def _(pool):
            def use(pair, e, ring):
                pool.wait_ge(ring_copied, ring + (1 + CREDIT))
                pool.tensor_tensor(v_used[:, e, :, :], v_tok[:, :, e * HD:(e + 1) * HD],
                                   one[:, :].unsqueeze(2).broadcast_to([P, NT, HD]), ALU.mult).then_inc(v_set, 1)

            pool.memset(one[:, :], 1.0).then_inc(one_set, 1)
            pool.wait_ge(one_set, 1)
            use(0, 0, 7)
            use(0, 1, 7)
            with pool.Fori(0, PAIRS - 1) as pr:
                for e in range(2):
                    pool.wait_ge(av_done, pr * n_a + ((e + 1) * (n_a // 2) + CREDIT))
                    use(pr + 1, e, pr * n_r + ring_place[("turn", 1, 7)])


def sample_attention(nc, c, projT, b_sb, cache_k, cache_v, page_table, k_out, v_out, oT):
    n_phys = cache_k.shape[0]
    n_pages = page_table.shape[1]
    past = n_pages * PAGE
    groups = n_pages // 4
    rows = NH * TSEQ
    k_ring, v_ring = 8, n_pages
    blocks = D // P
    with ExitStack() as stack:
        s = Scope(nc, stack, "smp")
        newT = s.sb("newT", [P, 4 * blocks, SMP])
        silu = s.sb("silu", [P, blocks, SMP])
        new_k, new_v = s.sb("new_k", [SMP, D]), s.sb("new_v", [P, D])
        q_rows = s.sb("q_rows", [P, 2, 9 * rows])
        mask_all = s.sb("mask_all", [P, NSEQ, SMP], BF16)
        mask_tokens = s.sb("mask_tokens", [TSEQ, NSEQ, SMP], BF16)
        mask = s.sb("mask", [P, 2, SMP], BF16)
        mask_dram = nc.dram_tensor("mask_dram", (TSEQ, NSEQ * SMP), BF16).ap()
        table = s.sb("table", [1, NSEQ * n_pages], I32)
        k_pages, v_pages = s.sb("k_pages", [P, k_ring, D]), s.sb("v_pages", [P, v_ring, D])
        kT = s.sb("kT", [P, 2, blocks, BANK])
        w = s.sb("w", [P, past + P])
        pass_on = s.sb("pass_on", [rows, 2, BANK])
        rest = s.sb("rest", [rows, past + SMP + 1])
        zeros = s.sb("zeros", [rows, BANK])
        wT = s.sb("wT", [P, 2, 4 * rows])
        o = s.sb("o", [P, D])
        out = s.sb("out", [P, blocks, SMP])
        bias = s.sb("bias", [rows, 2])
        kT_ps = s.ps("kT_acc", [P, 2, D])
        z_ps, wT_ps, o_ps = s.ps("z", [P, BANK]), s.ps("wT_acc", [P, BANK]), s.ps("o_acc", [rows, D])
        once, table_in, mask_moved, kv_stored, out_stored = (s.sem(n) for n in (
            "once_in", "table_in", "mask_moved", "kv_stored", "out_stored"))
        k_in, v_in = s.sems("k_in", k_ring), s.sems("v_in", v_ring)
        setup, masks, new_turned, new_copied, q_made, k_turned, act_copied, dve_copied, z_made, sigmoids, scanned, \
            w_made, w_turned, wT_copied, v_used, o_made, o_copied, folded, gated, seq_done = (s.sem(n) for n in (
                "setup", "masks", "new_turned", "new_copied", "q_made", "k_turned", "act_copied", "dve_copied",
                "z_made", "sigmoids", "scanned", "w_made", "w_turned", "wT_copied", "v_used", "o_made", "o_copied",
                "folded", "gated", "seq_done"))
        n_w = groups + 1
        half = blocks // 2

        with nc.Block() as block:
            @block.sync
            def _(sp):
                sp.dma_start(newT[:, :, :], projT.rearrange("(b p) n -> p b n", p=P)[:, :, SEQ:TOK]).then_inc(once, 16)
                sp.dma_start(bias[:, 0:1], b_sb.unsqueeze(1).unsqueeze(1).broadcast_to([NH, TSEQ, 1]),
                             allow_slow_non_contiguous=True).then_inc(once, 16)
                sp.dma_start(table[:, :], page_table.rearrange("(o s) n -> o (s n)", o=1)).then_inc(table_in, 16)
                sp.wait_ge(masks, 4)
                sp.dma_start(mask_dram, mask_tokens[:, :, :].rearrange("p s n -> p (s n)")).then_inc(mask_moved, 16)
                sp.wait_ge(mask_moved, 16)
                sp.dma_start(mask_all[0:rows, :, :].rearrange("p s n -> p (s n)"),
                             mask_dram.unsqueeze(0).broadcast_to([NH, TSEQ, NSEQ * SMP])).then_inc(mask_moved, 16)
                sp.wait_ge(new_copied, 4)
                sp.dma_start(k_out, new_k[:, :]).then_inc(kv_stored, 16)
                sp.dma_start(v_out, new_v[0:SMP, :]).then_inc(kv_stored, 16)
                sp.wait_ge(kv_stored, 32)
                sp.wait_ge(table_in, 16)
                sp.wait_ge(mask_moved, 32)

            @block.gpsimd
            def _(pool):
                pool.memset(mask_tokens[:, :, :], 0.0).then_inc(masks, 1)
                pool.memset(mask_all[:, :, :], 0.0).then_inc(masks, 1)
                pool.wait_ge(masks, 2)
                pool.affine_select(out=mask_tokens[:, :, :], in_=mask_tokens[:, :, :], compare_op=ALU.is_ge,
                                   fill=MASKED, base=0, pattern=[[-TSEQ, NSEQ], [1, SMP]],
                                   channel_multiplier=0).then_inc(masks, 1)
                pool.wait_ge(masks, 3)
                pool.affine_select(out=mask_tokens[:, :, :], in_=mask_tokens[:, :, :], compare_op=ALU.is_gt,
                                   fill=MASKED, base=0, pattern=[[TSEQ, NSEQ], [-1, SMP]],
                                   channel_multiplier=1).then_inc(masks, 1)

            @block.vector
            def _(dve):
                dve.memset(q_rows[:, :, :], 0.0)
                dve.memset(new_v[:, :], 0.0)
                dve.memset(w[:, :], 0.0)
                dve.memset(o[:, :], 0.0)
                dve.memset(zeros[:, :], 0.0)
                dve.memset(rest[:, past + SMP:], 1.0).then_inc(setup, 1)
                dve.wait_ge(once, 32)
                dve.tensor_scalar(bias[:, 1:2], bias[:, 0:1], -1.0, None, ALU.mult).then_inc(setup, 1)
                dve.wait_ge(setup, 2)
                for n in range(4):
                    dve.wait_ge(new_turned, n + 1)
                    dst = (new_k if n < 2 else new_v)[0:SMP, (n % 2) * BANK:(n % 2 + 1) * BANK]
                    dve.tensor_copy(dst, kT_ps[0:SMP, n // 2, (n % 2) * BANK:(n % 2 + 1) * BANK]).then_inc(new_copied, 1)
                dve.wait_ge(setup, 3)
                dve.tensor_tensor(silu[:, :, :], silu[:, :, :], newT[:, 3 * blocks:, :], ALU.mult).then_inc(setup, 1)

            @block.scalar
            def _(act):
                act.wait_ge(once, 32)
                act.wait_ge(setup, 2)
                act.activation(silu[:, :, :], newT[:, 3 * blocks:, :], ACT.Sigmoid).then_inc(setup, 1)

            @block.tensor
            def _(pe):
                pe.wait_ge(once, 32)
                for n in range(4):
                    for j in range(4):
                        mm = pe.transpose(kT_ps[0:SMP, n // 2, (n % 2) * BANK + j * P:(n % 2) * BANK + (j + 1) * P],
                                          newT[:, 4 * n + j, :], c.ident[:, :])
                    mm.then_inc(new_turned, 1)

        block = stack.enter_context(nc.Block())

        def over_sequences(engine, step):
            with engine.Fori(0, NSEQ // 2) as i:
                step(i * 2, i, 0)
                step(i * 2 + 1, i, 1)

        def half_read(g):
            return g + 2 if g >= 2 else g + 1

        def page_of(m):
            return (groups - 1 - m // 4) * 4 + m % 4

        @block.sync
        def _(sp):
            def step(q, i, b):
                for m in range(n_pages):
                    page = sp.value_load(table[0:1, ds(q * n_pages + page_of(m), 1)], min_val=0, max_val=n_phys - 1)
                    sp.wait_ge(k_turned, q * n_pages + (m + 1))
                    sp.wait_ge(table_in, 16)
                    sp.dma_start(k_pages[:, m % k_ring, :], cache_k.rearrange("g t h d -> (g t) (h d)")
                                 [ds(page * PAGE, PAGE), :]).then_inc(k_in[m % k_ring], 16)
                    sp.wait_ge(v_used, q * n_pages + (m + 1))
                    sp.wait_ge(table_in, 16)
                    sp.dma_start(v_pages[:, m % v_ring, :], cache_v.rearrange("g t h d -> (g t) (h d)")
                                 [ds(page * PAGE, PAGE), :]).then_inc(v_in[m % v_ring], 16)
            over_sequences(sp, step)
            sp.wait_ge(gated, NSEQ + 1)
            sp.dma_start(oT.rearrange("(b p) n -> p b n", p=P)[:, :, SEQ:TOK], out[:, :, :]).then_inc(out_stored, 16)
            sp.wait_ge(out_stored, 16)

        @block.tensor
        def _(pe):
            pe.sem_inc(k_turned, k_ring)
            pe.sem_inc(v_used, v_ring)
            pe.sem_inc(z_made, 2)
            pe.sem_inc(folded, 2)
            per_lap = n_pages // k_ring

            def step(q, i, b):
                def turn_keys(g):
                    for p in range(4):
                        m = 4 * g + p
                        pe.wait_ge(k_in[m % k_ring], q * (16 * per_lap) + 16 * (m // k_ring + 1))
                        pe.wait_ge(act_copied, q * n_pages + (m + 1))
                        pe.wait_ge(dve_copied, q * n_pages + (m + 1))
                        for hp in range(blocks):
                            mm = pe.transpose(kT_ps[:, m % 2, hp * P:(hp + 1) * P],
                                              k_pages[:, m % k_ring, hp * P:(hp + 1) * P], c.ident[:, :])
                        mm.then_inc(k_turned, 1)

                def logits(n):
                    pe.wait_ge(sigmoids, q * n_w + (n + 1))
                    if n == 0:
                        pe.wait_ge(gated, q + 1)
                        pe.wait_ge(q_made, q * 3 + 3)
                        pe.matmul(z_ps[0:rows, 0:SMP], c.ident_bf[:, 0:rows], mask[:, b, :], start=True, stop=False)
                        for hp in range(blocks):
                            mm = pe.matmul(z_ps[0:rows, 0:SMP], q_rows[:, b, hp * rows:(hp + 1) * rows], newT[:, hp, :],
                                           start=False, stop=(hp == blocks - 1))
                    else:
                        pe.wait_ge(act_copied, q * n_pages + (4 * n + 2))
                        pe.wait_ge(dve_copied, q * n_pages + (4 * n + 2))
                        for hp in range(blocks):
                            mm = pe.matmul(z_ps[0:rows, :], q_rows[:, b, hp * rows:(hp + 1) * rows],
                                           kT[:, (n - 1) % 2, hp, :], start=(hp == 0), stop=(hp == blocks - 1))
                    mm.then_inc(z_made, 1)

                def turn_weights(n):
                    pe.wait_ge(w_made, q * n_w + (n + 1))
                    pe.wait_ge(wT_copied, q * n_w + (n + 1))
                    if n == 0:
                        mm = pe.transpose(wT_ps[:, 0:P], w[:, past:past + P], c.ident[:, :])
                    else:
                        for p in range(4):
                            at = page_of(4 * (n - 1) + p) * PAGE
                            mm = pe.transpose(wT_ps[:, p * P:(p + 1) * P], w[:, at:at + PAGE], c.ident[:, :])
                    mm.then_inc(w_turned, 1)

                def values(n):
                    pe.wait_ge(wT_copied, q * n_w + (n + 2))
                    if n == 0:
                        pe.wait_ge(o_copied, q + 1)
                    for p in range(1 if n == 0 else 4):
                        m = 4 * (n - 1) + p
                        if n > 0:
                            pe.wait_ge(v_in[m], q * 16 + 16)
                        for j in range(D // BANK):
                            src = new_v if n == 0 else v_pages[:, m, :]
                            mm = pe.matmul(o_ps[:, j * BANK:(j + 1) * BANK], wT[:, (n + b) % 2, p * rows:(p + 1) * rows],
                                           src[:, j * BANK:(j + 1) * BANK], start=(n == 0), stop=(n == groups and p == 3))
                        if n > 0:
                            mm.then_inc(v_used, 1)

                turn_keys(0)
                logits(0)
                for n in range(n_w):
                    if n + 1 < n_w:
                        logits(n + 1)
                    if n + 1 < groups:
                        turn_keys(n + 1)
                    turn_weights(n)
                    values(n)
                pe.wait_ge(v_used, q * n_pages + (n_pages + v_ring))
                pe.wait_ge(o_copied, q + 2)
                for h in range(NH):
                    e, hp = h % 2, h // 2
                    mm = pe.matmul(z_ps[HD * e:HD * (e + 1), hp * TSEQ:(hp + 1) * TSEQ],
                                   o[:, h * HD:(h + 1) * HD], c.ident[:, h * TSEQ:(h + 1) * TSEQ],
                                   start=True, stop=True)
                mm.then_inc(folded, 1)
            over_sequences(pe, step)

        @block.scalar
        def _(act):
            act.sem_inc(act_copied, 2)
            act.sem_inc(sigmoids, 1)
            act.sem_inc(wT_copied, 1)
            act.sem_inc(o_copied, 1)

            def step(q, i, b):
                def copy_keys(g):
                    for p in range(4):
                        m = 4 * g + p
                        act.wait_ge(k_turned, q * n_pages + (m + 1 + k_ring))
                        if p == 0:
                            act.wait_ge(z_made, q * n_w + half_read(g))
                        act.activation(kT[:, g % 2, 0:half, p * P:(p + 1) * P],
                                       kT_ps[:, m % 2, 0:BANK].rearrange("p (h n) -> p h n", n=P),
                                       ACT.Copy).then_inc(act_copied, 1)

                def sigmoid(n):
                    act.wait_ge(z_made, q * n_w + (n + 3))
                    size = SMP if n == 0 else BANK
                    at = past if n == 0 else (groups - n) * BANK
                    act.wait_ge(scanned, q * n_w + (n + 1))
                    act.wait_ge(v_used, q * n_pages + v_ring)
                    act.activation(w[0:rows, at:at + size], z_ps[0:rows, 0:size], ACT.Sigmoid, bias=bias[:, 0:1],
                                   scale=HD ** -0.5)
                    act.activation(pass_on[:, (n + b) % 2, 0:size], z_ps[0:rows, 0:size], ACT.Sigmoid, bias=bias[:, 1:2],
                                   scale=-HD ** -0.5).then_inc(sigmoids, 1)

                def copy_weights(n):
                    act.wait_ge(w_turned, q * n_w + (n + 1))
                    m = 1 if n == 0 else 4
                    act.activation(wT[:, (n + b) % 2, 0:m * rows].rearrange("p (m n) -> p m n", n=rows),
                                   wT_ps[:, 0:m * P].rearrange("p (m n) -> p m n", n=P)[:, :, 0:rows],
                                   ACT.Copy).then_inc(wT_copied, 1)

                copy_keys(0)
                sigmoid(0)
                for n in range(n_w):
                    if n + 1 < n_w:
                        sigmoid(n + 1)
                    if n + 1 < groups:
                        copy_keys(n + 1)
                    copy_weights(n)
                act.wait_ge(v_used, q * n_pages + (n_pages + v_ring))
                act.wait_ge(folded, q + 2)
                act.activation(o[0:rows, :], o_ps[:, :], ACT.Copy).then_inc(o_copied, 1)
            over_sequences(act, step)

        @block.vector
        def _(dve):
            dve.sem_inc(dve_copied, 2)
            dve.sem_inc(scanned, 2)
            dve.sem_inc(gated, 1)

            def step(q, i, b):
                cols = ds(q * TSEQ, TSEQ)

                def queries():
                    dve.wait_ge(folded, q + 1)
                    view = q_rows[:, b, :].rearrange("p (h n) -> p h n", n=rows + 2 * TSEQ)
                    qT = newT[:, 2 * blocks:3 * blocks, :]
                    dve.tensor_scalar(view[0:HD, :, 0:TSEQ], qT[0:HD, :, cols], 1.0, None, ALU.mult).then_inc(q_made, 1)
                    dve.tensor_scalar(view[HD:P, :, TSEQ:2 * TSEQ], qT[HD:P, :, cols], 1.0, None,
                                      ALU.mult).then_inc(q_made, 1)
                    dve.tensor_scalar(mask[:, b, :], mask_all[:, ds(q, 1), :].rearrange("p o n -> p (o n)"), 1.0, None,
                                      ALU.mult).then_inc(q_made, 1)

                def copy_keys(g):
                    for p in range(4):
                        m = 4 * g + p
                        dve.wait_ge(k_turned, q * n_pages + (m + 1 + k_ring))
                        if p == 0:
                            dve.wait_ge(z_made, q * n_w + half_read(g))
                        dve.tensor_copy(kT[:, g % 2, half:blocks, p * P:(p + 1) * P],
                                        kT_ps[:, m % 2, BANK:D].rearrange("p (h n) -> p h n", n=P)
                                        ).then_inc(dve_copied, 1)

                def weights(n):
                    size = SMP if n == 0 else BANK
                    at = past if n == 0 else (groups - n) * BANK
                    dve.wait_ge(sigmoids, q * n_w + (n + 2))
                    if n > 0:
                        dve.wait_ge(w_made, q * n_w + n)
                    dve.tensor_tensor_scan(rest[:, at:at + size][:, ::-1], pass_on[:, (n + b) % 2, 0:size][:, ::-1],
                                           zeros[:, 0:size], rest[:, at + size:at + size + 1], ALU.mult,
                                           ALU.add).then_inc(scanned, 1)
                    dve.wait_ge(scanned, q * n_w + (n + 3))
                    dve.tensor_tensor(w[0:rows, at:at + size], w[0:rows, at:at + size], rest[:, at + 1:at + size + 1],
                                      ALU.mult).then_inc(w_made, 1)

                queries()
                copy_keys(0)
                weights(0)
                for n in range(n_w):
                    if n + 1 < n_w:
                        weights(n + 1)
                    if n + 1 < groups:
                        copy_keys(n + 1)
                dve.wait_ge(folded, q + 3)
                dve.tensor_tensor(out[:, :, cols], z_ps[:, 0:blocks * TSEQ].rearrange("p (h n) -> p h n", n=TSEQ), silu[:, :, cols],
                                  ALU.mult).then_inc(gated, 1)
            over_sequences(dve, step)


def trunk(nc, x_prompt, x_sample, state_gla, cache_k, cache_v, page_table, g_norm_a, w_in_a, w_alpha2, b_alpha,
          g_head_a, w_out_a, g_kv, w_kv, g_norm_b, w_in_b, b_sb, w_out_b, g_final, y_prompt, y_sample,
          state_prompt, state_sample, k_prompt, v_prompt, k_sample, v_sample):
    def rows(a):
        return a.rearrange("a b d -> (a b) d")

    def tile_of(prompt, sample):
        return lambda t: sample if is_sample(t) else prompt[ds(t * P, P), :]

    def heads(a):
        return a.rearrange("a t h d -> (a t) (h d)")

    xnT, oT = (nc.dram_tensor(n, (D, TOK), F32).ap() for n in ("xnT", "oT"))
    o_gla, h_mid = (nc.dram_tensor(n, (TOK, D), F32).ap() for n in ("o_gla", "h_mid"))
    proj_a = nc.dram_tensor("proj_a", (w_in_a.shape[2], TOK), F32).ap()
    proj_b = nc.dram_tensor("proj_b", (4 * D, TOK), F32).ap()
    x_of = tile_of(rows(x_prompt), rows(x_sample))
    h_of = tile_of(h_mid[0:SEQ, :], h_mid[SEQ:TOK, :])

    class Constants:
        pass

    with ExitStack() as stack:
        c = Constants()
        c.scope = Scope(nc, stack, "const")
        build_constants(nc, c)
        normalise(nc, c, x_of, xnT)
        full = w_in_a.shape[2] // P
        project(nc, c, "proja", xnT, [(w_in_a[0], g_norm_a[0], full, proj_a, 0)], tail=w_in_a.shape[2] - full * P)
        gla(nc, c, proj_a, w_alpha2[0], b_alpha[0], g_head_a[0], state_gla[0], state_prompt[0, 0], state_sample[0],
            o_gla)
        out_project(nc, c, "outa", o_gla, False, w_out_a[0], x_of, h_of, xnT=xnT)
        project(nc, c, "projb", xnT, [(w_kv, g_kv, 2 * D // P, proj_b, 0), (w_in_b[0], g_norm_b[0], 2 * D // P,
                                                                           proj_b, 2 * D)])
        prompt_attention(nc, c, proj_b, b_sb[0], heads(k_prompt), heads(v_prompt), oT)
        sample_attention(nc, c, proj_b, b_sb[0], cache_k, cache_v, page_table, heads(k_sample), heads(v_sample), oT)
        out_project(nc, c, "outb", oT, True, w_out_b[0], h_of, None, gain=g_final,
                    y_out=tile_of(rows(y_prompt), rows(y_sample)))


INPUTS = ("x_prompt", "x_sample", "state_gla", "cache_k", "cache_v", "page_table", "g_norm_a", "w_in_a", "w_alpha2",
          "b_alpha", "g_head_a", "w_out_a", "g_kv", "w_kv", "g_norm_b", "w_in_b", "b_sb", "w_out_b", "g_final")
OUTPUTS = (("y_prompt", (1, SEQ, D)), ("y_sample", (NSEQ, TSEQ, D)), ("state_gla_prompt", (1, 1, GH, DK, DV)),
           ("state_gla_sample", (1, NSEQ, GH, DK, DV)), ("k_prompt", (1, SEQ, NH, HD)), ("v_prompt", (1, SEQ, NH, HD)),
           ("k_sample", (NSEQ, TSEQ, NH, HD)), ("v_sample", (NSEQ, TSEQ, NH, HD)))


def kernel(**inputs):
    import concourse.bacc as bacc
    from concourse.bass_utils import run_bass_kernel_spmd

    nc = bacc.Bacc("TRN2", target_bir_lowering=False, num_devices=1)
    arrays, args = {}, []
    for name in INPUTS:
        a = np.ascontiguousarray(inputs[name])
        arrays[f"in_{name}"] = a
        args.append(nc.dram_tensor(f"in_{name}", a.shape, mybir.dt.from_np(a.dtype), kind="ExternalInput").ap())
    for name, shape in OUTPUTS:
        args.append(nc.dram_tensor(f"out_{name}", shape, F32, kind="ExternalOutput").ap())
    trunk(nc, *args)
    result = run_bass_kernel_spmd(nc, [arrays], core_ids=[0])
    return tuple(result.results[0][f"out_{name}"] for name, _ in OUTPUTS)
```

```python
from contextlib import ExitStack

import numpy as np

import concourse.bass as bass
from concourse import mybir

ALU = mybir.AluOpType
ACT = mybir.ActivationFunctionType
F32 = mybir.dt.float32
F32R = mybir.dt.float32r
BF16 = mybir.dt.bfloat16
I32 = mybir.dt.int32
ds = bass.ds

P = 128
D = 1024
KD = D // P
SEQ = 2048
NSEQ, TSEQ = 8, 4
SMP = NSEQ * TSEQ
TOK = SEQ + SMP
NT = SEQ // P
BANK = 512
NCH = SEQ // BANK
GH, DK, DV = 4, 128, 256
RANK = 16
CHUNK = 64
NCK = SEQ // CHUNK
TAU = 16.0
NH, HD = 16, 64
PAIRS = NH // 2
PAGE = 128
EPS = 1e-6
MASKED = -1e30


def over_tiles(engine, step, skip_first=False):
    if not skip_first:
        step(0, 0, 0)
    step(1, 0, 1)
    with engine.Fori(1, NT // 2) as i:
        step(i * 2, i, 0)
        step(i * 2 + 1, i, 1)
    step(NT, NT // 2, 0)


def is_sample(t):
    return isinstance(t, int) and t == NT


def rows_of(t):
    return SMP if is_sample(t) else P


def from_tile(t, n):
    return not isinstance(t, int) or t >= n


class Scope:

    def __init__(self, nc, stack, prefix):
        self.nc, self.stack, self.prefix, self.used = nc, stack, prefix, []
        stack.callback(self.close)

    def close(self):
        self.nc.clear_and_free_semaphores(self.used)
        self.nc.all_engine_barrier()

    def sb(self, name, shape, dt=F32):
        return self.stack.enter_context(self.nc.sbuf_tensor(f"{self.prefix}_{name}", shape, dt))

    def ps(self, name, shape, dt=F32):
        return self.stack.enter_context(self.nc.psum_tensor(f"{self.prefix}_{name}", shape, dt))

    def sem(self, name):
        sem = self.nc.alloc_semaphore(f"{self.prefix}_{name}")
        self.used.append(sem)
        return sem

    def sems(self, name, n):
        return [self.sem(f"{name}{i}") for i in range(n)]


def build_constants(nc, c):
    zeroed, c.consts_ready = c.scope.sem("zeroed"), c.scope.sem("consts_ready")
    c.ident = c.scope.sb("ident", [P, P])
    c.ident_bf = c.scope.sb("ident_bf", [P, P], BF16)
    c.diag_mask = c.scope.sb("diag_mask", [P, P], BF16)
    with nc.Block() as block:

        @block.gpsimd
        def _(pool):
            for t in (c.ident, c.ident_bf, c.diag_mask):
                pool.memset(t[:, :], 0.0).then_inc(zeroed, 1)
            pool.wait_ge(zeroed, 3)
            for t in (c.ident, c.ident_bf):
                pool.affine_select(out=t[:, :], in_=t[:, :], compare_op=ALU.not_equal, fill=1.0, base=0,
                                   pattern=[[-1, P]], channel_multiplier=1).then_inc(c.consts_ready, 1)
            pool.affine_select(out=c.diag_mask[:, :], in_=c.diag_mask[:, :], compare_op=ALU.is_gt, fill=MASKED,
                               base=0, pattern=[[-1, P]], channel_multiplier=1).then_inc(c.consts_ready, 1)


def normalise(nc, c, x_tile, xnT):
    with ExitStack() as stack:
        s = Scope(nc, stack, "norm")
        h = s.sb("h", [P, 2, D])
        square = s.sb("square", [P, D])
        xn = s.sb("xn", [P, 2, D])
        xT = s.sb("xT", [P, 2, KD, P])
        sumsq, root, rstd = (s.sb(n, [P, 2]) for n in ("sumsq", "root", "rstd"))
        eps = s.sb("eps", [P, 1])
        turned_ps = s.ps("turned", [P, 2, KD * P])
        h_in, xT_stored = s.sems("h_in", 2), s.sems("xT_stored", 2)
        eps_set, sumsq_made, root_made, rstd_made, xn_made, turned, act_copied, dve_copied = (
            s.sem(n) for n in ("eps_set", "sumsq_made", "root_made", "rstd_made", "xn_made", "turned",
                               "act_copied", "dve_copied"))
        block = stack.enter_context(nc.Block())
        half = KD // 2

        @block.sync
        def _(sp):
            def step(t, i, b):
                n = rows_of(t)
                if from_tile(t, 2):
                    sp.wait_ge(xn_made, t - 1)
                sp.dma_start(h[0:n, b, :], x_tile(t)).then_inc(h_in[b], 16)
            over_tiles(sp, step)

        @block.scalar
        def _(act):
            def copy(t, i, b):
                n = rows_of(t)
                act.wait_ge(turned, t + 1)
                if from_tile(t, 2):
                    act.wait_ge(xT_stored[b], 16 * i)
                act.activation(xT[:, b, 0:half, 0:n],
                               turned_ps[:, b, 0:half * P].rearrange("p (k n) -> p k n", n=P)[:, :, 0:n],
                               ACT.Copy).then_inc(act_copied, 1)

            def step(t, i, b):
                n = rows_of(t)
                act.wait_ge(h_in[b], 16 * i + 16)
                if from_tile(t, 2):
                    act.wait_ge(rstd_made, t - 1)
                act.activation(square[0:n, :], h[0:n, b, :], ACT.Square,
                               accum_out=sumsq[0:n, b:b + 1]).then_inc(sumsq_made, 1)
                act.wait_ge(sumsq_made, t + 1)
                act.activation(root[0:n, b:b + 1], sumsq[0:n, b:b + 1], ACT.Sqrt, scale=1.0 / D,
                               bias=eps[0:n, :]).then_inc(root_made, 1)
                if from_tile(t, 1):
                    copy(t - 1, i if b else i - 1, 1 - b)
            act.wait_ge(eps_set, 1)
            over_tiles(act, step)
            copy(NT, NT // 2, 0)

        @block.vector
        def _(dve):
            def copy(t, i, b):
                n = rows_of(t)
                dve.wait_ge(turned, t + 1)
                if from_tile(t, 2):
                    dve.wait_ge(xT_stored[b], 16 * i)
                dve.tensor_scalar(xT[:, b, half:KD, 0:n],
                                  turned_ps[:, b, half * P:].rearrange("p (k n) -> p k n", n=P)[:, :, 0:n],
                                  1.0, None, ALU.mult).then_inc(dve_copied, 1)

            def step(t, i, b):
                n = rows_of(t)
                dve.wait_ge(root_made, t + 1)
                dve.reciprocal(rstd[0:n, b:b + 1], root[0:n, b:b + 1]).then_inc(rstd_made, 1)
                dve.wait_ge(rstd_made, t + 1)
                if from_tile(t, 2):
                    dve.wait_ge(turned, t - 1)
                dve.tensor_scalar(xn[0:n, b, :], h[0:n, b, :], rstd[0:n, b:b + 1], None,
                                  ALU.mult).then_inc(xn_made, 1)
                if from_tile(t, 1):
                    copy(t - 1, i if b else i - 1, 1 - b)
            dve.memset(eps[:, :], EPS).then_inc(eps_set, 1)
            over_tiles(dve, step)
            copy(NT, NT // 2, 0)

        @block.tensor
        def _(pe):
            def step(t, i, b):
                n = rows_of(t)
                pe.wait_ge(xn_made, t + 1)
                if from_tile(t, 2):
                    pe.wait_ge(act_copied, t - 1)
                    pe.wait_ge(dve_copied, t - 1)
                for k in range(KD):
                    mm = pe.transpose(turned_ps[:, b, k * P:k * P + n], xn[0:n, b, k * P:(k + 1) * P],
                                      c.ident[0:n, 0:n])
                mm.then_inc(turned, 1)
            over_tiles(pe, step)

        @block.gpsimd
        def _(pool):
            def step(t, i, b):
                n = rows_of(t)
                pool.wait_ge(act_copied, t + 1)
                pool.wait_ge(dve_copied, t + 1)
                pool.wait_ge(eps_set, 1)
                col = ds(t * P, n)
                pool.dma_start(xnT.rearrange("(k p) n -> p k n", p=P)[:, :, col],
                               xT[:, b, :, 0:n]).then_inc(xT_stored[b], 16)
            over_tiles(pool, step)
            pool.wait_ge(xT_stored[0], 16 * (NT // 2 + 1))
            pool.wait_ge(xT_stored[1], 16 * (NT // 2))


def project(nc, c, name, xnT, jobs, tail=None):
    with ExitStack() as stack:
        s = Scope(nc, stack, name)
        slab = s.sb("slab", [P, 2, TOK])
        x_hi, x_lo = (s.sb(n, [P, KD, TOK], F32R) for n in ("x_hi", "x_lo"))
        w_raw = s.sb("w_raw", [P, 2, KD, P])
        w_scaled = s.sb("w_scaled", [P, KD, P])
        w_hi, w_lo = (s.sb(n, [P, 2, KD, P], F32R) for n in ("w_hi", "w_lo"))
        gain = s.sb("gain", [P, len(jobs), KD])
        out = s.sb("out", [P, 2, TOK])
        acc = s.ps("acc", [P, NCH + 1, BANK])
        slab_in, w_in, stored = s.sems("slab_in", 2), s.sems("w_in", 2), s.sems("stored", 2)
        gain_in = s.sem("gain_in")
        x_hi_made, x_lo_made, w_scaled_made, w_hi_made, w_lo_made, chunk_done, copied = (
            s.sem(n) for n in ("x_hi_made", "x_lo_made", "w_scaled_made", "w_hi_made", "w_lo_made",
                               "chunk_done", "copied"))
        block = stack.enter_context(nc.Block())
        spans = [(q * BANK, BANK) for q in range(NCH)] + [(SEQ, SMP)]
        n_spans = len(spans)

        def over_blocks(engine, step, skip_first=False):
            done = 0
            for j, (_, _, blocks, _, _) in enumerate(jobs):
                first = 0
                if done == 0:
                    if not skip_first:
                        step(j, 0, 0, 0, 0, P)
                    step(j, 1, 1, 0, 1, P)
                    first = 1
                with engine.Fori(first, blocks // 2) as i:
                    step(j, i * 2, i * 2 + done, i + done // 2, 0, P)
                    step(j, i * 2 + 1, i * 2 + 1 + done, i + done // 2, 1, P)
                done += blocks
            if tail:
                step(len(jobs) - 1, jobs[-1][2], done, done // 2, 0, tail)

        @block.sync
        def _(sp):
            for j, (_, g, _, _, _) in enumerate(jobs):
                sp.dma_start(gain[:, j, :], g.rearrange("(k p) -> p k", p=P), allow_slow_non_contiguous=True).then_inc(gain_in, 16)
            def step(j, jb, n, i, b, width):
                if from_tile(n, 2):
                    sp.wait_ge(w_scaled_made, n - 1)
                src = jobs[j][0].rearrange("(k p) n -> p k n", p=P)[:, :, ds(jb * P, width)]
                sp.dma_start(w_raw[:, b, :, 0:width], src).then_inc(w_in[b], 16)
            step(0, 0, 0, 0, 0, P)
            for k in range(KD):
                if k >= 2:
                    sp.wait_ge(x_lo_made, k - 1)
                sp.dma_start(slab[:, k % 2, :], xnT[k * P:(k + 1) * P, :]).then_inc(slab_in[k % 2], 16)
            over_blocks(sp, step, skip_first=True)

        @block.scalar
        def _(act):
            for k in range(KD):
                act.wait_ge(slab_in[k % 2], 16 * (k // 2 + 1))
                act.activation(x_hi[:, k, :], slab[:, k % 2, :], ACT.Copy).then_inc(x_hi_made, 1)

            def step(j, jb, n, i, b, width):
                for q, (at, size) in enumerate(spans):
                    act.wait_ge(chunk_done, n * n_spans + (q + 1))
                    if q == 0 and from_tile(n, 2):
                        act.wait_ge(stored[b], 16 * i)
                    act.activation(out[:, b, at:at + size], acc[:, q, 0:size], ACT.Copy).then_inc(copied, 1)
            over_blocks(act, step)

        @block.vector
        def _(dve):
            dve.wait_ge(gain_in, 16 * len(jobs))

            def step(j, jb, n, i, b, width):
                dve.wait_ge(w_in[b], 16 * i + 16)
                if from_tile(n, 1):
                    dve.wait_ge(w_lo_made, n)
                dve.tensor_tensor(w_scaled[:, :, 0:width], w_raw[:, b, :, 0:width],
                                  gain[:, j, :].unsqueeze(2).broadcast_to([P, KD, width]),
                                  ALU.mult).then_inc(w_scaled_made, 1)
                dve.wait_ge(w_scaled_made, n + 1)
                if from_tile(n, 2):
                    dve.wait_ge(chunk_done, (n - 1) * n_spans)
                dve.tensor_copy(w_hi[:, b, :, 0:width], w_scaled[:, :, 0:width]).then_inc(w_hi_made, 1)
                dve.wait_ge(w_hi_made, n + 1)
                dve.tensor_tensor(w_lo[:, b, :, 0:width], w_scaled[:, :, 0:width],
                                  w_hi[:, b, :, 0:width].bitcast(F32), ALU.subtract).then_inc(w_lo_made, 1)
            step(0, 0, 0, 0, 0, P)
            for k in range(KD):
                dve.wait_ge(x_hi_made, k + 1)
                dve.tensor_tensor(x_lo[:, k, :], slab[:, k % 2, :], x_hi[:, k, :].bitcast(F32),
                                  ALU.subtract).then_inc(x_lo_made, 1)
            over_blocks(dve, step, skip_first=True)

        @block.tensor
        def _(pe):
            def products(b, width, k, q):
                at, size = spans[q]
                for w, x in ((w_hi, x_hi), (w_lo, x_hi), (w_hi, x_lo)):
                    mm = pe.matmul(acc[:, q, 0:size], w[:, b, k, :], x[:, k, at:at + size],
                                   start=(k == 0 and w is w_hi and x is x_hi), stop=(k == KD - 1 and x is x_lo))
                return mm

            def step(j, jb, n, i, b, width):
                pe.wait_ge(w_lo_made, n + 1)
                if not from_tile(n, 1):
                    for k in range(KD):
                        pe.wait_ge(x_lo_made, k + 1)
                        for q in range(n_spans):
                            mm = products(b, width, k, q)
                            if k == KD - 1:
                                mm.then_inc(chunk_done, 1)
                    return
                for q, (at, size) in enumerate(spans):
                    if from_tile(n, 1):
                        pe.wait_ge(copied, (n - 1) * n_spans + (q + 1))
                    for k in range(KD):
                        mm = products(b, width, k, q)
                    mm.then_inc(chunk_done, 1)
            over_blocks(pe, step)

        @block.gpsimd
        def _(pool):
            def step(j, jb, n, i, b, width):
                pool.wait_ge(copied, n * n_spans + n_spans)
                pool.wait_ge(gain_in, 16 * len(jobs))
                _, _, _, dst, row = jobs[j]
                pool.dma_start(dst[ds(jb * P + row, width), :], out[0:width, b, :]).then_inc(stored[b], 16)
            over_blocks(pool, step)
            total = sum(j[2] for j in jobs)
            pool.wait_ge(stored[0], 16 * (total // 2 + (1 if tail else 0)))
            pool.wait_ge(stored[1], 16 * (total // 2))


def gla(nc, c, projT, w_alpha2, b_alpha, g_head, state_in, state_prompt, state_sample, o_out):
    q_rows, k_rows, v_rows, g_rows, r_rows = 0, GH * DK, 2 * GH * DK, 2 * GH * DK + GH * DV, 2 * GH * DK + 2 * GH * DV
    scale = float(np.float32(DK ** -0.5))
    wide = BANK + SMP
    n_tiles = NT + 1
    with ExitStack() as stack:
        s = Scope(nc, stack, "gla")
        qT, kT, ktT = (s.sb(n, [P, NCH, wide]) for n in ("qT", "kT", "ktT"))
        vgT = s.sb("vgT", [P, NCH, 4, wide])
        rT = s.sb("rT", [RANK, TOK])
        logit, work, b_sum, gap = (s.sb(n, [P, wide]) for n in ("logit", "work", "b_sum", "gap"))
        sigmoid_g = s.sb("sigmoid_g", [P, 2, wide])
        keep = s.sb("keep", [P, wide])
        w2, bias = s.sb("w2", [RANK, DK]), s.sb("bias", [P, 1])
        decay = s.sb("decay", [P, NCH, BANK // CHUNK])
        decay_smp = s.sb("decay_smp", [P, NSEQ])
        vg, vg_smp = s.sb("vg", [P, NCH, 4, 2 * DV]), s.sb("vg_smp", [SMP, 2 * DV])
        o, o_smp = s.sb("o", [P, NCH, 4, DV]), s.sb("o_smp", [SMP, DV])
        square = s.sb("square", [P, DV])
        ke = s.sb("ke", [P, 2, P])
        pT = s.sb("pT", [P, 2, P])
        S = s.sb("S", [P, 4, DV])
        s_in, s_new = s.sb("s_in", [P, NSEQ, DV]), s.sb("s_new", [P, NSEQ, DV])
        ke_smp, pT_smp = s.sb("ke_smp", [SMP, NSEQ, P]), s.sb("pT_smp", [SMP, SMP])
        q_smp = s.sb("q_smp", [P, NSEQ, SMP])
        tok_mask = s.sb("tok_mask", [P, NSEQ, SMP])
        row_mask = s.sb("row_mask", [SMP, NSEQ])
        may, may_smp = s.sb("may", [P, P], I32), s.sb("may_smp", [SMP, SMP], I32)
        mask_work = s.sb("mask_work", [P, P])
        g_gain = s.sb("g_gain", [P, DV])
        sumsq, root, rstd = (s.sb(n, [P, n_tiles]) for n in ("sumsq", "root", "rstd"))
        eps = s.sb("eps", [P, 1])
        kp_ps, o_ps, ds_ps = (s.ps(n, [P, 2, BANK]) for n in ("kp", "o_acc", "ds"))
        tok_ps = s.ps("tok", [P, BANK])
        logit_ps = s.ps("logit_acc", [P, BANK])
        ld = {n: s.sem(f"in_{n}") for n in ("w2", "b", "s0")}
        in_q, in_k, in_v, in_g = (s.sems(f"in_{n}", NCH) for n in "qkvg")
        once = s.sem("once_in")
        masks, logit_mm, logit_cp, prep, expd, tok_t, tok_cp, kp_t, ke_cp, pt_cp, ds_mm, s_made, o_mm, smp_made, \
            ds_smp, s_smp, sum_made, o_cp, root_made, rstd_made, normed, gated, s_zero, state_stored, smp_stored, o_smp_stored = (
                s.sem(n) for n in (
                    "masks", "logit_mm", "logit_cp", "prep", "expd", "tok_t", "tok_cp", "kp_t", "ke_cp", "pt_cp",
                    "ds_mm", "s_made", "o_mm", "smp_made", "ds_smp", "s_smp", "sum_made", "o_cp", "root_made", "rstd_made", "normed",
                    "gated", "s_zero", "state_stored", "smp_stored", "o_smp_stored"))
        o_stored = s.sems("o_stored", NCH)

        with nc.Block() as block:
            @block.gpsimd
            def _(pool):
                pool.memset(keep[:, :], 1.0).then_inc(masks, 1)
                pool.memset(tok_mask[:, :, :], 1.0).then_inc(masks, 1)
                pool.memset(row_mask[:, :], 1.0).then_inc(masks, 1)
                pool.memset(mask_work[:, :], 1.0).then_inc(masks, 1)
                pool.memset(may[:, :], 0).then_inc(masks, 1)
                pool.wait_ge(masks, 5)
                pool.affine_select(out=keep[:, 0:BANK], in_=keep[:, 0:BANK], compare_op=ALU.not_equal, fill=0.0, base=0,
                                   pattern=[[0, BANK // CHUNK], [1, CHUNK]], channel_multiplier=0).then_inc(masks, 1)
                pool.affine_select(out=keep[:, BANK:], in_=keep[:, BANK:], compare_op=ALU.not_equal, fill=0.0, base=0,
                                   pattern=[[0, NSEQ], [1, TSEQ]], channel_multiplier=0).then_inc(masks, 1)
                pool.affine_select(out=tok_mask[:, :, :], in_=tok_mask[:, :, :], compare_op=ALU.is_ge, fill=0.0,
                                   base=0, pattern=[[-TSEQ, NSEQ], [1, SMP]], channel_multiplier=0).then_inc(masks, 1)
                pool.affine_select(out=row_mask[:, :], in_=row_mask[:, :], compare_op=ALU.is_ge, fill=0.0,
                                   base=0, pattern=[[-TSEQ, NSEQ]], channel_multiplier=1).then_inc(masks, 1)
                pool.affine_select(out=mask_work[:, :], in_=mask_work[:, :], compare_op=ALU.is_ge, fill=0.0,
                                   base=0, pattern=[[1, P]], channel_multiplier=-1).then_inc(masks, 1)
                pool.wait_ge(masks, 10)
                pool.affine_select(out=tok_mask[:, :, :], in_=tok_mask[:, :, :], compare_op=ALU.is_gt, fill=0.0,
                                   base=TSEQ, pattern=[[TSEQ, NSEQ], [-1, SMP]], channel_multiplier=0).then_inc(masks, 1)
                pool.affine_select(out=row_mask[:, :], in_=row_mask[:, :], compare_op=ALU.is_gt, fill=0.0,
                                   base=TSEQ, pattern=[[TSEQ, NSEQ]], channel_multiplier=-1).then_inc(masks, 1)
                pool.memset(mask_work[0:CHUNK, CHUNK:], 0.0).then_inc(masks, 1)

            @block.vector
            def _(dve):
                dve.memset(pT[:, :, :], 0.0)
                dve.memset(pT_smp[:, :], 0.0)
                dve.memset(eps[:, :], EPS)
                dve.wait_ge(masks, 13)
                dve.tensor_copy(may[:, :], mask_work[:, :]).then_inc(prep, 1)
                dve.wait_ge(prep, 1)
                dve.tensor_tensor(ke_smp[:, :, 0:SMP], tok_mask[0:SMP, :, :],
                                  row_mask[:, :].unsqueeze(2).broadcast_to([SMP, NSEQ, SMP]), ALU.mult).then_inc(prep, 1)
                dve.wait_ge(prep, 2)
                dve.tensor_reduce(mask_work[0:SMP, 0:SMP], ke_smp[:, :, 0:SMP].rearrange("p s n -> p n s"),
                                  mybir.AxisListType.X, ALU.add).then_inc(prep, 1)
                dve.wait_ge(prep, 3)
                dve.tensor_tensor(mask_work[0:SMP, SMP:2 * SMP], mask_work[0:SMP, 0:SMP], may[0:SMP, 0:SMP],
                                  ALU.mult).then_inc(prep, 1)
                dve.wait_ge(prep, 4)
                dve.tensor_copy(may_smp[:, :], mask_work[0:SMP, SMP:2 * SMP]).then_inc(prep, 1)

            @block.sync
            def _(sp):
                sp.dma_start(rT[:, :], projT[r_rows:r_rows + RANK, :]).then_inc(once, 16)
                sp.dma_start(g_gain[:, :], g_head.unsqueeze(0).broadcast_to([P, DV])).then_inc(once, 16)
                sp.wait_ge(once, 32)
        PREP0 = 5
        START = -1
        ONE, TWO, FOUR = 1, 2, 4
        N_PREP, N_EXP = 8, 5

        STEPS = (((4, 1),), ((5, 1), (6, 1)), ((7, 1), (0, 2), (1, 2), (2, 2)), ((3, 2),))
        ROOTS, NORMS = (7, 11, 15, NT), (8, 12, NT, NT)
        order = []
        for t in range(n_tiles):
            steps = [("prep", (t // 4 + n) // NCH, (t // 4 + n) % NCH, k) for k, n in STEPS[t % 4] if t < NT]
            order += [x for x in steps if x[3] == 0] + [("tile", 0, t)] + [x for x in steps if x[3] > 0]
            order += [("root", 0, u) for u in range(NCH) if ROOTS[u] == t]
            order += [("norm", 0, u) for u in range(NCH) if NORMS[u] == t]
        first = [("prep", 1, 0, k) for k in range(8)] + [("prep", 1, 1, k) for k in range(4)]

        def over_heads(engine, run):
            run(START, first)
            with engine.Fori(0, GH - 1) as h:
                run(h, order)
            run(GH - 1, [x for x in order if x[1] == 0])

        def span_size(u):
            return wide if u == NCH - 1 else BANK

        def place(t):
            return (NCH - 1, BANK) if t == NT else (t // 4, t % 4 * P)

        block = stack.enter_context(nc.Block())

        @block.sync
        def _(sp):
            def span(h, u):
                at, n = u * BANK, span_size(u)
                sp.dma_start(qT[:, u, 0:n], projT[ds(h * DK + q_rows, DK), at:at + n]).then_inc(in_q[u], 16)
                sp.dma_start(kT[:, u, 0:n], projT[ds(h * DK + k_rows, DK), at:at + n]).then_inc(in_k[u], 16)
                for j, row, sem in ((2, g_rows, in_g[u]), (0, v_rows, in_v[u])):
                    sp.dma_start(vgT[:, u, j:j + 2, 0:n],
                                 projT[ds(h * DV + row, DV), at:at + n].rearrange("(b p) n -> p b n", p=P)
                                 ).then_inc(sem, 16)

            def gate_weights(h):
                sp.dma_start(w2[:, :], w_alpha2[:, ds(h * DK, DK)]).then_inc(ld["w2"], 16)
                sp.dma_start(bias[:, :], b_alpha.rearrange("(n o) -> n o", o=1)[ds(h * DK, DK), :]).then_inc(ld["b"], 16)

            def sample_states(h):
                sp.dma_start(s_in[:, :, :].unsqueeze(2),
                             state_in.rearrange("s h k v -> k s h v")[:, :, ds(h, 1), :]).then_inc(ld["s0"], 16)

            def store_o(h, u):
                sp.wait_ge(gated, h * NCH + (u + 1 + FOUR))
                sp.dma_start(o_out[u * BANK:(u + 1) * BANK, :].rearrange("(t p) n -> p t n", p=P)
                             [:, :, ds(h * DV, DV)], o[:, u, :, :]).then_inc(o_stored[u], 16)

            gate_weights(0)
            span(0, 0)
            span(0, 1)
            sample_states(0)
            span(0, 2)
            span(0, 3)

            def run(h, is_last):
                for u in range(NCH):
                    if not is_last:
                        sp.wait_ge(o_mm, h * n_tiles + ((n_tiles if u == NCH - 1 else 4 * u + 4) + TWO))
                        span(h + 1, u)
                        if u == 1:
                            gate_weights(h + 1)
                    if u < NCH - 1:
                        store_o(h, u)
                sp.wait_ge(s_made, h * NCK + (NCK + ONE))
                sp.dma_start(state_prompt.rearrange("h k v -> k h v")[:, ds(h, 1), :], S[:, 0:1, :]
                             ).then_inc(state_stored, 16)
                sp.wait_ge(s_smp, h * NSEQ + (NSEQ + ONE))
                sp.dma_start(state_sample.rearrange("s h k v -> k s h v")[:, :, ds(h, 1), :],
                             s_new[:, :, :].unsqueeze(2)).then_inc(smp_stored, 16)
                if not is_last:
                    sample_states(h + 1)
                store_o(h, 3)
                sp.dma_start(o_out[SEQ:TOK, ds(h * DV, DV)], o_smp[:, :]).then_inc(o_smp_stored, 16)
            with sp.Fori(0, GH - 1) as h:
                run(h, False)
            run(GH - 1, True)
            for stored in o_stored + [state_stored, smp_stored, o_smp_stored]:
                sp.wait_ge(stored, 16 * GH + ONE)

        @block.tensor
        def _(pe):
            pe.sem_inc(o_mm, TWO)
            pe.sem_inc(ds_smp, ONE)
            for stored in o_stored + [state_stored, smp_stored, o_smp_stored]:
                pe.sem_inc(stored, ONE)

            def run(h, items):
                def to_tokens(t):
                    n, b = rows_of(t), t % 2
                    u, at = place(t)
                    if t % 4 == 0 and t < NT:
                        pe.wait_ge(prep, h * (NCH * N_PREP) + (PREP0 + (u + 1) * N_PREP))
                        pe.wait_ge(in_v[u], h * 16 + 16)
                    pe.wait_ge(tok_cp, h * n_tiles + (t + ONE))
                    for j in range(4):
                        mm = pe.transpose(tok_ps[0:n, j * P:(j + 1) * P], vgT[:, u, j, at:at + n], c.ident[:, :])
                    mm.then_inc(tok_t, 1)
                    back = 0 if t == 0 else 1
                    pe.wait_ge(ke_cp, h * n_tiles + (t - back + ONE))
                    pe.wait_ge(pt_cp, h * n_tiles + (t - back + ONE))
                    pe.transpose(kp_ps[0:n, b, 0:P], kT[:, u, at:at + n], c.ident[:, :])
                    pe.matmul(kp_ps[0:n, b, P:P + n], ktT[:, u, at:at + n], qT[:, u, at:at + n],
                              start=True, stop=True).then_inc(kp_t, 1)

                def products(t):
                    b = t % 2
                    u, at = place(t)
                    pe.wait_ge(tok_cp, h * n_tiles + (t + 1 + ONE))
                    pe.wait_ge(ke_cp, h * n_tiles + (t + 1 + ONE))
                    pe.wait_ge(pt_cp, h * n_tiles + (t + 1 + ONE))
                    if t >= 1:
                        pe.wait_ge(s_made, h * NCK + (2 * t + ONE))
                    else:
                        pe.wait_ge(s_smp, h * NSEQ + ONE)
                    for half in range(2):
                        r = slice(half * CHUNK, (half + 1) * CHUNK)
                        pe.matmul(ds_ps[:, half, 0:DV], ke[r, b, :], vg[r, u, t % 4, 0:DV], start=True,
                                  stop=True).then_inc(ds_mm, 1)
                    pe.wait_ge(o_cp, h * n_tiles + (t - (1 if t else 0) + ONE))
                    pe.matmul(o_ps[:, b, 0:DV], pT[:, b, :], vg[:, u, t % 4, 0:DV], start=True, stop=True)
                    for half in range(2):
                        ck = 2 * t + half
                        if ck >= 1:
                            pe.wait_ge(s_made, h * NCK + (ck + ONE))
                        else:
                            pe.wait_ge(s_zero, h + 1)
                        r = slice(half * CHUNK, (half + 1) * CHUNK)
                        mm = pe.matmul(o_ps[r, b, 0:DV], qT[:, u, at + half * CHUNK:at + (half + 1) * CHUNK],
                                       S[:, ck % 4, :], start=False, stop=True, skip_group_check=True)
                    mm.then_inc(o_mm, 1)

                def sample_products():
                    t, b = NT, NT % 2
                    pe.wait_ge(tok_cp, h * n_tiles + (t + 1 + ONE))
                    pe.wait_ge(pt_cp, h * n_tiles + (t + 1 + ONE))
                    pe.wait_ge(o_cp, h * n_tiles + (t - 1 + ONE))
                    pe.wait_ge(smp_made, h * 2 + (2 + ONE))
                    pe.wait_ge(ld["s0"], h * 16 + 16)
                    for q in range(NSEQ):
                        pe.matmul(o_ps[0:SMP, b, 0:DV], q_smp[:, q, :], s_in[:, q, :], start=(q == 0), stop=False)
                    mm = pe.matmul(o_ps[0:SMP, b, 0:DV], pT_smp[:, :], vg_smp[:, 0:DV], start=False, stop=True)
                    mm.then_inc(o_mm, 1)
                    pe.wait_ge(s_made, h * NCK + (NCK + ONE))
                    for q in range(NSEQ):
                        if q >= 2:
                            pe.wait_ge(s_smp, h * NSEQ + (q - 1 + ONE))
                        pe.matmul(ds_ps[:, q % 2, 0:DV], ke_smp[:, q, :], vg_smp[:, 0:DV], start=True,
                                  stop=True).then_inc(ds_smp, 1)

                for kind, off, *x in items:
                    if kind == "prep":
                        u, k = x
                        if k == 0:
                            pe.wait_ge(ld["w2"], h * 16 + (16 * off + 16))
                            place_of = 5 * off + u
                            parts = [(u * BANK, BANK)] + ([(SEQ, SMP)] if u == NCH - 1 else [])
                            for i, (at, n) in enumerate(parts):
                                pe.wait_ge(logit_cp, h * 5 + (place_of + i + ONE))
                                pe.matmul(logit_ps[:, 0:n], w2[:, :], rT[:, at:at + n], start=True,
                                          stop=True).then_inc(logit_mm, 1)
                    elif kind == "tile":
                        t, = x
                        if t == 0:
                            to_tokens(0)
                        if t < NT:
                            to_tokens(t + 1)
                        if t < NT:
                            products(t)
                        else:
                            sample_products()
            over_heads(pe, run)

        @block.scalar
        def _(act):
            act.sem_inc(tok_cp, ONE)
            act.sem_inc(sum_made, ONE)
            act.sem_inc(o_cp, ONE)

            def run(h, items):
                def sum_squares(t):
                    n = rows_of(t)
                    act.wait_ge(o_mm, h * n_tiles + (t + 1 + TWO))
                    act.wait_ge(sum_made, h * n_tiles + (t + ONE))
                    act.activation(square[0:n, :], o_ps[0:n, t % 2, 0:DV], ACT.Square,
                                   accum_out=sumsq[0:n, t:t + 1]).then_inc(sum_made, 1)
                    if t == NT:
                        act.wait_ge(o_smp_stored, h * 16 + ONE)
                    elif t % 4 == 0:
                        act.wait_ge(o_stored[t // 4], h * 16 + ONE)
                    dst = o_smp[:, :] if t == NT else o[:, t // 4, t % 4, :]
                    act.activation(dst, o_ps[0:n, t % 2, 0:DV], ACT.Copy).then_inc(o_cp, 1)

                for kind, off, *x in items:
                    if kind == "tile":
                        t, = x
                        n = rows_of(t)
                        act.wait_ge(tok_t, h * n_tiles + (t + 1))
                        if t == NT:
                            act.wait_ge(gated, h * NCH + FOUR)
                            act.wait_ge(ds_smp, h * NSEQ + ONE)
                            dst = vg_smp[:, :]
                        else:
                            if t % 4 == 0:
                                act.wait_ge(gated, h * NCH + (t // 4 - 3 + FOUR))
                            dst = vg[:, t // 4, t % 4, :]
                        act.activation(dst, tok_ps[0:n, :], ACT.Copy).then_inc(tok_cp, 1)
                        if t >= 1:
                            sum_squares(t - 1)
                        if t == NT:
                            sum_squares(NT)
                        continue
                    if kind == "root":
                        u, = x
                        last_tile = NT if u == NCH - 1 else 4 * u + 3
                        act.wait_ge(sum_made, h * n_tiles + (last_tile + 1 + ONE))
                        last = act.activation(root[:, 4 * u:4 * u + 4], sumsq[:, 4 * u:4 * u + 4], ACT.Sqrt,
                                              scale=1.0 / DV, bias=eps[:, :])
                        if last_tile == NT:
                            last = act.activation(root[0:SMP, NT:], sumsq[0:SMP, NT:], ACT.Sqrt, scale=1.0 / DV,
                                                  bias=eps[0:SMP, :])
                        last.then_inc(root_made, 1)
                        continue
                    if kind == "norm":
                        continue
                    u, k = x
                    n = span_size(u)
                    p0 = PREP0 + (NCH * off + u) * N_PREP
                    e0 = (NCH * off + u) * N_EXP
                    hp, he = h * (NCH * N_PREP), h * (NCH * N_EXP)
                    if k == 2:
                        act.wait_ge(prep, hp + (p0 + 1))
                        act.activation(work[:, 0:n], work[:, 0:n], ACT.Exp, scale=-1.0).then_inc(expd, 1)
                        act.wait_ge(expd, he + (e0 + 1))
                        act.activation(work[:, 0:n], work[:, 0:n], ACT.Ln, bias=1.0).then_inc(expd, 1)
                    elif k == 4:
                        act.wait_ge(prep, hp + (p0 + 3))
                        act.activation(work[:, 0:n], b_sum[:, 0:n], ACT.Exp, scale=1.0 / TAU)
                        act.activation(logit[:, 0:n], b_sum[:, 0:n], ACT.Exp, scale=-1.0 / TAU)
                        if h is not START:
                            act.wait_ge(s_made, h * NCK + ((u + 1) * (BANK // CHUNK) * off + ONE))
                        last = act.activation(decay[:, u, :], b_sum[:, CHUNK - 1:BANK:CHUNK], ACT.Exp, scale=1.0 / TAU)
                        if u == NCH - 1:
                            act.wait_ge(s_smp, h * NSEQ + ONE)
                            last = act.activation(decay_smp[:, :], b_sum[:, BANK + TSEQ - 1:wide:TSEQ], ACT.Exp,
                                                  scale=1.0 / TAU)
                        last.then_inc(expd, 1)
                        act.wait_ge(prep, hp + (p0 + 4))
                        act.activation(gap[:, 0:n], gap[:, 0:n], ACT.Exp, scale=1.0 / TAU).then_inc(expd, 1)
                    elif k == 5:
                        act.wait_ge(in_g[u], h * 16 + (16 * off + 16))
                        act.activation(sigmoid_g[:, :, 0:n], vgT[:, u, 2:4, 0:n], ACT.Sigmoid).then_inc(expd, 1)
            over_heads(act, run)

        @block.vector
        def _(dve):
            for sem in (logit_cp, ke_cp, pt_cp, s_made, s_smp, smp_made):
                dve.sem_inc(sem, ONE)
            dve.sem_inc(gated, FOUR)

            def run(h, items):
                def states(t):
                    for half in range(2):
                        ck = 2 * t + half
                        dve.wait_ge(ds_mm, h * NCK + (ck + 1))
                        dve.wait_ge(o_mm, h * n_tiles + (t + TWO))
                        dve.wait_ge(s_made, h * NCK + (ck + ONE))
                        if ck == 0:
                            dve.wait_ge(s_zero, h + 1)
                        dve.scalar_tensor_tensor(
                            out=S[:, (ck + 1) % 4, :], in0=S[:, ck % 4, :],
                            scalar=decay[:, t // 4, ck % 8:ck % 8 + 1], in1=ds_ps[:, half, 0:DV], op0=ALU.mult,
                            op1=ALU.add).then_inc(s_made, 1)

                def norm(u):
                    dve.wait_ge(root_made, h * NCH + (u + 1))
                    last = dve.reciprocal(rstd[:, 4 * u:4 * u + 4], root[:, 4 * u:4 * u + 4])
                    if u == NCH - 1:
                        last = dve.reciprocal(rstd[0:SMP, NT:], root[0:SMP, NT:])
                    last.then_inc(rstd_made, 1)
                    dve.wait_ge(rstd_made, h * NCH + (u + 1))
                    dve.wait_ge(o_cp, h * n_tiles + ((n_tiles if u == NCH - 1 else 4 * u + 4) + ONE))
                    for t in range(4 * u, 4 * u + 4):
                        last = dve.scalar_tensor_tensor(out=o[:, u, t % 4, :], in0=o[:, u, t % 4, :],
                                                        scalar=rstd[:, t:t + 1], in1=g_gain[:, :], op0=ALU.mult,
                                                        op1=ALU.mult)
                    if u == NCH - 1:
                        last = dve.scalar_tensor_tensor(out=o_smp[:, :], in0=o_smp[:, :], scalar=rstd[0:SMP, NT:],
                                                        in1=g_gain[0:SMP, :], op0=ALU.mult, op1=ALU.mult)
                    last.then_inc(normed, 1)
                    dve.wait_ge(normed, h * NCH + (u + 1))
                    if u == NCH - 1:
                        dve.tensor_tensor(o_smp[:, :], o_smp[:, :], vg_smp[:, DV:], ALU.mult)
                    dve.tensor_tensor(o[:, u, :, :], o[:, u, :, :], vg[:, u, :, DV:], ALU.mult
                                      ).then_inc(gated, 1)

                def sample_operands():
                    dve.wait_ge(ke_cp, h * n_tiles + (n_tiles + ONE))
                    dve.tensor_tensor(ke_smp[:, :, :], ke[0:SMP, NT % 2, :].unsqueeze(1).broadcast_to([SMP, NSEQ, P]),
                                      row_mask[:, :].unsqueeze(2).broadcast_to([SMP, NSEQ, P]),
                                      ALU.mult).then_inc(smp_made, 1)
                    dve.tensor_tensor(q_smp[:, :, :], qT[:, NCH - 1, BANK:wide].unsqueeze(1).broadcast_to([P, NSEQ, SMP]),
                                      tok_mask[:, :, :], ALU.mult).then_inc(smp_made, 1)

                def sample_states():
                    dve.wait_ge(ld["s0"], h * 16 + 16)
                    dve.wait_ge(smp_stored, h * 16 + ONE)
                    for q in range(NSEQ):
                        dve.wait_ge(ds_smp, h * NSEQ + (q + 1 + ONE))
                        dve.scalar_tensor_tensor(out=s_new[:, q, :], in0=s_in[:, q, :], scalar=decay_smp[:, q:q + 1],
                                                 in1=ds_ps[:, q % 2, 0:DV], op0=ALU.mult, op1=ALU.add).then_inc(s_smp, 1)

                for kind, off, *x in items:
                    if kind == "tile":
                        t, = x
                        n, b = rows_of(t), t % 2
                        if t == 0:
                            dve.wait_ge(state_stored, h * 16 + ONE)
                            dve.wait_ge(o_mm, h * n_tiles + TWO)
                            dve.memset(S[:, 0, :], 0.0).then_inc(s_zero, 1)
                            dve.wait_ge(smp_made, h * 2 + ONE)
                        dve.wait_ge(kp_t, h * n_tiles + (t + 1))
                        dve.wait_ge(o_mm, h * n_tiles + (max(t - 1, 0) + TWO))
                        dve.tensor_copy(ke[0:n, b, :], kp_ps[0:n, b, 0:P]).then_inc(ke_cp, 1)
                        if t < NT:
                            dve.copy_predicated(pT[:, b, :], may[:, :], kp_ps[:, b, P:2 * P]).then_inc(pt_cp, 1)
                        else:
                            dve.copy_predicated(pT_smp[:, :], may_smp[:, :],
                                                kp_ps[0:SMP, b, P:P + SMP]).then_inc(pt_cp, 1)
                            sample_operands()
                        if t >= 1:
                            states(t - 1)
                        if t == NT:
                            sample_states()
                        continue
                    if kind == "norm":
                        norm(*x)
                        continue
                    if kind == "root":
                        continue
                    u, k = x
                    n = span_size(u)
                    p0 = PREP0 + (NCH * off + u) * N_PREP
                    e0 = (NCH * off + u) * N_EXP
                    hp, he, loads = h * (NCH * N_PREP), h * (NCH * N_EXP), h * 16 + (16 * off + 16)
                    if k == 1:
                        dve.wait_ge(ld["b"], h * 16 + (16 * off + 16))
                        dve.wait_ge(prep, hp + p0)
                        at_l = 5 * off + u
                        parts = [(0, BANK)] + ([(BANK, SMP)] if u == NCH - 1 else [])
                        for i, (at, m) in enumerate(parts):
                            dve.wait_ge(logit_mm, h * 5 + (at_l + i + 1))
                            dve.tensor_scalar(logit[:, at:at + m], logit_ps[:, 0:m], bias[:, 0:1], None,
                                              ALU.add).then_inc(logit_cp, 1)
                        dve.wait_ge(logit_cp, h * 5 + (at_l + len(parts) + ONE))
                        dve.scalar_tensor_tensor(out=work[:, 0:n], in0=logit[:, 0:n], scalar=-1.0, in1=logit[:, 0:n],
                                                 op0=ALU.mult, op1=ALU.max).then_inc(prep, 1)
                    elif k == 3:
                        dve.wait_ge(expd, he + (e0 + 2))
                        dve.wait_ge(prep, hp + (p0 + 1))
                        dve.scalar_tensor_tensor(out=logit[:, 0:n], in0=logit[:, 0:n], scalar=0.0, in1=work[:, 0:n],
                                                 op0=ALU.min, op1=ALU.subtract).then_inc(prep, 1)
                        dve.wait_ge(prep, hp + (p0 + 2))
                        dve.tensor_tensor_scan(b_sum[:, 0:n], keep[:, 0:n], logit[:, 0:n], 0.0, ALU.mult,
                                               ALU.add).then_inc(prep, 1)
                        dve.wait_ge(prep, hp + (p0 + 3))
                        pieces = [(0, BANK // CHUNK, CHUNK)]
                        if u == NCH - 1:
                            pieces = [(BANK, NSEQ, TSEQ)] + pieces
                        for lo, m, size in pieces:
                            v = b_sum[:, lo:lo + m * size].rearrange("p (c l) -> p c l", l=size)
                            last = dve.tensor_tensor(gap[:, lo:lo + m * size].rearrange("p (c l) -> p c l", l=size),
                                                     v[:, :, size - 1:size].broadcast_to([P, m, size]), v, ALU.subtract)
                        last.then_inc(prep, 1)
                    elif k == 6:
                        dve.wait_ge(in_q[u], loads)
                        dve.wait_ge(expd, he + (e0 + 3))
                        dve.scalar_tensor_tensor(out=qT[:, u, 0:n], in0=qT[:, u, 0:n], scalar=scale, in1=work[:, 0:n],
                                                 op0=ALU.mult, op1=ALU.mult).then_inc(prep, 1)
                        dve.wait_ge(in_k[u], loads)
                        dve.tensor_tensor(ktT[:, u, 0:n], kT[:, u, 0:n], logit[:, 0:n], ALU.mult).then_inc(prep, 1)
                        dve.wait_ge(expd, he + (e0 + 4))
                        dve.wait_ge(prep, hp + (p0 + 6))
                        dve.tensor_tensor(kT[:, u, 0:n], kT[:, u, 0:n], gap[:, 0:n], ALU.mult).then_inc(prep, 1)
                    elif k == 7:
                        dve.wait_ge(expd, he + (e0 + 5))
                        dve.tensor_tensor(vgT[:, u, 2:4, 0:n], vgT[:, u, 2:4, 0:n], sigmoid_g[:, :, 0:n],
                                          ALU.mult).then_inc(prep, 1)
            over_heads(dve, run)


def out_project(nc, c, name, o_in, transposed, w_out, residual, h_out, xnT=None, gain=None, y_out=None):
    with ExitStack() as stack:
        s = Scope(nc, stack, name)
        w_raw = s.sb("w_raw", [P, KD, D])
        w_hi, w_lo = (s.sb(n, [P, KD, D], F32R) for n in ("w_hi", "w_lo"))
        o = s.sb("o", [P, 2, D])
        oT_hi, oT_lo = (s.sb(n, [P, 2, KD, P], F32R) for n in ("oT_hi", "oT_lo"))
        res, h, xn = (s.sb(n, [P, 2, D]) for n in ("res", "h", "xn"))
        square = s.sb("square", [P, D])
        xT = s.sb("xT", [P, 2, KD, P])
        gains = s.sb("gains", [P, D])
        sumsq, root, rstd = (s.sb(n, [P, 2]) for n in ("sumsq", "root", "rstd"))
        eps = s.sb("eps", [P, 1])
        oT_ps, y_ps, t_ps = s.ps("oT", [P, KD * P]), s.ps("y", [P, 2, D]), s.ps("t", [P, KD * P])
        w_in, o_in_sem, res_in = s.sems("w_in", KD), s.sems("o_in", 2), s.sems("res_in", 2)
        h_stored, x_stored = s.sems("h_stored", 2), s.sems("x_stored", 2)
        gain_in, eps_set, w_hi_made, w_lo_made, o_turned, hi_made, lo_made, y_made, h_made, sumsq_made, root_made, \
            rstd_made, xn_made, x_turned, x_copied = (s.sem(n) for n in (
                "gain_in", "eps_set", "w_hi_made", "w_lo_made", "o_turned", "hi_made", "lo_made", "y_made", "h_made",
                "sumsq_made", "root_made", "rstd_made", "xn_made", "x_turned", "x_copied"))
        block = stack.enter_context(nc.Block())

        def lagged(i, b):
            return i if b else i - 1

        @block.sync
        def _(sp):
            if gain is not None:
                sp.dma_start(gains[:, :], gain.unsqueeze(0).broadcast_to([P, D])).then_inc(gain_in, 16)
            def step(t, i, b):
                n = rows_of(t)
                if from_tile(t, 2):
                    if transposed:
                        sp.wait_ge(lo_made, t - 1)
                    else:
                        sp.wait_ge(o_turned, t - 1)
                if transposed:
                    sp.dma_start(o[:, b, :].rearrange("p (k n) -> p k n", n=P)[:, :, 0:n],
                                 o_in.rearrange("(k p) n -> p k n", p=P)[:, :, ds(t * P, n)]).then_inc(o_in_sem[b], 16)
                else:
                    sp.dma_start(o[0:n, b, :], o_in[ds(t * P, n), :]).then_inc(o_in_sem[b], 16)
                if from_tile(t, 2):
                    sp.wait_ge(h_made, t - 1)
                sp.dma_start(res[0:n, b, :], residual(t)).then_inc(res_in[b], 16)
            step(0, 0, 0)
            for k in range(KD):
                sp.dma_start(w_raw[:, k, :], w_out[k * P:(k + 1) * P, :]).then_inc(w_in[k], 16)
            over_tiles(sp, step, skip_first=True)

        @block.scalar
        def _(act):
            act.wait_ge(eps_set, 1)

            def norm(t, i, b):
                n = rows_of(t)
                act.wait_ge(h_made, t + 1)
                if from_tile(t, 2):
                    act.wait_ge(rstd_made, t - 1)
                act.activation(square[0:n, :], h[0:n, b, :], ACT.Square,
                               accum_out=sumsq[0:n, b:b + 1]).then_inc(sumsq_made, 1)
                act.wait_ge(sumsq_made, t + 1)
                act.activation(root[0:n, b:b + 1], sumsq[0:n, b:b + 1], ACT.Sqrt, scale=1.0 / D,
                               bias=eps[0:n, :]).then_inc(root_made, 1)

            def step(t, i, b):
                n = rows_of(t)
                if from_tile(t, 2):
                    act.wait_ge(y_made, t - 1)
                if transposed:
                    act.wait_ge(o_in_sem[b], 16 * i + 16)
                    act.activation(oT_hi[:, b, :, 0:n], o[:, b, :].rearrange("p (k n) -> p k n", n=P)[:, :, 0:n],
                                   ACT.Copy).then_inc(hi_made, 1)
                else:
                    act.wait_ge(o_turned, t + 1)
                    act.activation(oT_hi[:, b, :, 0:n], oT_ps[:, :].rearrange("p (k n) -> p k n", n=P)[:, :, 0:n],
                                   ACT.Copy).then_inc(hi_made, 1)
                if from_tile(t, 1):
                    norm(t - 1, lagged(i, b), 1 - b)
            step(0, 0, 0)
            for k in range(KD):
                act.wait_ge(w_in[k], 16)
                act.activation(w_hi[:, k, :], w_raw[:, k, :], ACT.Copy).then_inc(w_hi_made, 1)
            over_tiles(act, step, skip_first=True)
            norm(NT, NT // 2, 0)

        @block.vector
        def _(dve):
            dve.memset(eps[:, :], EPS).then_inc(eps_set, 1)
            if gain is not None:
                dve.wait_ge(gain_in, 16)

            def after(t, i, b):
                n = rows_of(t)
                dve.wait_ge(y_made, t + 1)
                dve.wait_ge(res_in[b], 16 * i + 16)
                if from_tile(t, 2):
                    if h_out is not None:
                        dve.wait_ge(h_stored[b], 16 * i)
                    dve.wait_ge(xn_made, t - 1)
                dve.tensor_tensor(h[0:n, b, :], y_ps[0:n, b, :], res[0:n, b, :], ALU.add).then_inc(h_made, 1)

            def finish(t, i, b):
                n = rows_of(t)
                dve.wait_ge(root_made, t + 1)
                dve.reciprocal(rstd[0:n, b:b + 1], root[0:n, b:b + 1]).then_inc(rstd_made, 1)
                dve.wait_ge(rstd_made, t + 1)
                if xnT is not None:
                    if from_tile(t, 2):
                        dve.wait_ge(x_turned, t - 1)
                    dve.tensor_scalar(xn[0:n, b, :], h[0:n, b, :], rstd[0:n, b:b + 1], None,
                                      ALU.mult).then_inc(xn_made, 1)
                else:
                    if from_tile(t, 2):
                        dve.wait_ge(x_stored[b], 16 * i)
                    dve.scalar_tensor_tensor(out=xn[0:n, b, :], in0=h[0:n, b, :], scalar=rstd[0:n, b:b + 1],
                                             in1=gains[0:n, :], op0=ALU.mult, op1=ALU.mult).then_inc(xn_made, 1)

            def copy_x(t, i, b):
                n = rows_of(t)
                dve.wait_ge(x_turned, t + 1)
                if from_tile(t, 2):
                    dve.wait_ge(x_stored[b], 16 * i)
                dve.tensor_scalar(xT[:, b, :, 0:n], t_ps[:, :].rearrange("p (k n) -> p k n", n=P)[:, :, 0:n],
                                  1.0, None, ALU.mult).then_inc(x_copied, 1)

            def step(t, i, b):
                n = rows_of(t)
                dve.wait_ge(hi_made, t + 1)
                if from_tile(t, 2):
                    dve.wait_ge(y_made, t - 1)
                src = (o[:, b, :] if transposed else oT_ps[:, :]).rearrange("p (k n) -> p k n", n=P)[:, :, 0:n]
                dve.tensor_tensor(oT_lo[:, b, :, 0:n], src, oT_hi[:, b, :, 0:n].bitcast(F32),
                                  ALU.subtract).then_inc(lo_made, 1)
                if from_tile(t, 1):
                    after(t - 1, lagged(i, b), 1 - b)
                    finish(t - 1, lagged(i, b), 1 - b)
                if xnT is not None and from_tile(t, 2):
                    copy_x(t - 2, i - 1, b)
            step(0, 0, 0)
            for k in range(KD):
                dve.wait_ge(w_hi_made, k + 1)
                dve.tensor_tensor(w_lo[:, k, :], w_raw[:, k, :], w_hi[:, k, :].bitcast(F32),
                                  ALU.subtract).then_inc(w_lo_made, 1)
            over_tiles(dve, step, skip_first=True)
            after(NT, NT // 2, 0)
            finish(NT, NT // 2, 0)
            if xnT is not None:
                copy_x(NT - 1, NT // 2 - 1, 1)
                copy_x(NT, NT // 2, 0)

        @block.tensor
        def _(pe):
            def turn(t, i, b):
                n = rows_of(t)
                pe.wait_ge(o_in_sem[b], 16 * i + 16)
                if from_tile(t, 1):
                    pe.wait_ge(lo_made, t)
                for k in range(KD):
                    mm = pe.transpose(oT_ps[:, k * P:k * P + n], o[0:n, b, k * P:(k + 1) * P], c.ident[0:n, 0:n])
                mm.then_inc(o_turned, 1)

            def turn_x(t, i, b):
                n = rows_of(t)
                pe.wait_ge(xn_made, t + 1)
                if from_tile(t, 1):
                    pe.wait_ge(x_copied, t)
                for k in range(KD):
                    mm = pe.transpose(t_ps[:, k * P:k * P + n], xn[0:n, b, k * P:(k + 1) * P], c.ident[0:n, 0:n])
                mm.then_inc(x_turned, 1)

            def products(t, i, b):
                by_part = not from_tile(t, 1)
                pe.wait_ge(lo_made, t + 1)
                if from_tile(t, 2):
                    pe.wait_ge(h_made, t - 1)
                for j in range(D // BANK):
                    for k in range(KD):
                        if by_part and j == 0:
                            pe.wait_ge(w_lo_made, k + 1)
                        for w, x in ((w_hi, oT_hi), (w_lo, oT_hi), (w_hi, oT_lo)):
                            mm = pe.matmul(y_ps[:, b, j * BANK:(j + 1) * BANK], x[:, b, k, :],
                                           w[:, k, j * BANK:(j + 1) * BANK],
                                           start=(k == 0 and w is w_hi and x is oT_hi),
                                           stop=(k == KD - 1 and x is oT_lo))
                mm.then_inc(y_made, 1)

            def step(t, i, b):
                if not transposed:
                    turn(t, i, b)
                if from_tile(t, 1):
                    products(t - 1, lagged(i, b), 1 - b)
                if xnT is not None and from_tile(t, 2):
                    turn_x(t - 2, i - 1, b)
            over_tiles(pe, step)
            products(NT, NT // 2, 0)
            if xnT is not None:
                turn_x(NT - 1, NT // 2 - 1, 1)
                turn_x(NT, NT // 2, 0)

        @block.gpsimd
        def _(pool):
            def step(t, i, b):
                n = rows_of(t)
                if h_out is not None:
                    pool.wait_ge(h_made, t + 1)
                    pool.wait_ge(eps_set, 1)
                    pool.dma_start(h_out(t), h[0:n, b, :]).then_inc(h_stored[b], 16)
                pool.wait_ge(x_copied if xnT is not None else xn_made, t + 1)
                pool.wait_ge(eps_set, 1)
                if xnT is not None:
                    pool.dma_start(xnT.rearrange("(k p) n -> p k n", p=P)[:, :, ds(t * P, n)],
                                   xT[:, b, :, 0:n]).then_inc(x_stored[b], 16)
                else:
                    pool.dma_start(y_out(t), xn[0:n, b, :]).then_inc(x_stored[b], 16)
            over_tiles(pool, step)
            for stored in ([h_stored] if h_out is not None else []) + [x_stored]:
                pool.wait_ge(stored[0], 16 * (NT // 2 + 1))
                pool.wait_ge(stored[1], 16 * (NT // 2))


def chunks_of(tile):
    n, out = (tile + 1) * P, []
    while n > 0:
        out.append((max(0, n - 1024), n))
        n -= 1024
    return out


def attention_schedule():
    def logits(off, e, g):
        return [("z", off, e, t, j) for t in range(4 * g, 4 * g + 4) for j in range(len(chunks_of(t)))]

    def merge(main, beside):
        out, done = [], 0
        for m, v in enumerate(main):
            want = min(len(beside), -(-len(beside) * (m + 1) * 4 // (3 * len(main))))
            out += beside[done:want] + [v]
            done = want
        return out

    split = [[("split", 1, e, c) for c in range(NCH)] for e in range(2)]
    turn = [("turn", 1, m) for m in range(8)]
    silu = [("silu", 1, c) for c in range(NCH - 1)]
    extra = {(0, 0): [("silu", 0, NCH - 1)], (0, 3): split[0], (1, 1): turn[:4], (1, 2): turn[4:],
             (1, 3): split[1] + silu}
    groups = [(0, e, g) for e in range(2) for g in range(4)] + [(1, 0, 0)]
    order = []
    for n, (_, e, g) in enumerate(groups[:-1]):
        values = [("a", 0, e, g, j) for j in reversed(range(4 * g + 4))]
        order += merge(merge(values, logits(*groups[n + 1])), extra.get((e, g), []))
    return split[0] + logits(1, 0, 0) + turn + silu + split[1], order


def prompt_attention(nc, c, projT, b_sb, k_out, v_out, oT):
    k_rows, v_rows, q_rows, g_rows = 0, D, 2 * D, 3 * D
    first, order = attention_schedule()
    every_a = [x for x in order if x[0] == "a"]
    n_z, n_r = (sum(x[0] in kinds for x in order) for kinds in (("z",), ("a", "turn")))
    n_a = len(every_a)
    z_first, ring_first = (sum(x[0] in kinds for x in first) for kinds in (("z",), ("turn",)))
    z_place = {x[1:]: z_first + n for n, x in enumerate(x for x in order if x[0] == "z")}
    ring_place = {x: ring_first + n for n, x in enumerate(x for x in order if x[0] in ("a", "turn"))}
    ring_of_last = {x: ring_first + n for n, x in enumerate(every_a)}
    a_place = {x: n for n, x in enumerate(every_a)}
    LAST = PAIRS - 1
    START = -1
    CREDIT = 2
    last_of = {t: len(chunks_of(t)) - 1 for t in range(NT)}

    def z_at(off, e, t, j):
        if (off, e, t, j) in z_place:
            return z_place[(off, e, t, j)]
        return z_place[(off + 1, e, t, j)] - n_z

    def tile_before(off, e, t, by):
        n = (off * 2 + e) * NT + t - by
        return n // (2 * NT), n // NT % 2, n % NT

    def last_z(off, e, t):
        if off < 0:
            return last_z(off + 1, e, t) - n_z
        return z_at(off, e, t, last_of[t])

    def ring_at(pr, x):
        return (ring_of_last if pr is LAST else ring_place)[x]

    def last_ring(pr, off, e, g):
        return ring_at(None if off < 0 else pr, ("a", 0, e, g, 0)) + off * n_r

    with ExitStack() as stack:
        s = Scope(nc, stack, "att")
        raw_k, raw_v, raw_g, twice_k, twice_q = (s.sb(n, [P, SEQ]) for n in (
            "raw_k", "raw_v", "raw_g", "twice_k", "twice_q"))
        q_parts, k_hi, k_lo = (s.sb(n, [P, 2, SEQ], F32R) for n in ("q_parts", "k_hi", "k_lo"))
        silu = s.sb("silu", [P, SEQ])
        k_tok, v_tok = (s.sb(n, [P, NT, P]) for n in ("k_tok", "v_tok"))
        v_used = s.sb("v_used", [P, 2, NT, HD])
        w_even, w_odd = s.sb("w_even", [P, 4, SEQ - BANK]), s.sb("w_odd", [P, 4, SEQ])
        rest = s.sb("rest", [P, 2, SEQ + 1])
        zero, one = s.sb("zero", [P, 1]), s.sb("one", [P, 1])
        wT = s.sb("wT", [P, 2, BANK])
        out = s.sb("out", [P, SEQ])
        bias_all = s.sb("bias_all", [P, 2, NH])
        bias = s.sb("bias", [P, 2, 2])
        z_ps = s.ps("z", [P, 2, 1024])
        wT_ps = s.ps("wT_acc", [P, 2, BANK])
        o_ps = s.ps("o_acc", [P, 2, BANK])
        in_k, in_v, in_g, in_twice, bias_in, kv_stored = (s.sem(n) for n in (
            "in_k", "in_v", "in_g", "in_twice", "bias_in", "kv_stored"))
        out_stored, one_set = s.sems("out_stored", 2), s.sem("one_set")
        setup, bias_set, sig_made, silu_made, hi_made, lo_made, v_set, z_made, pass_made, sigmoids, scanned, w_made, ring_turned, \
            ring_copied, av_done, o_gated = (s.sem(n) for n in (
                "setup", "bias_set", "sig_made", "silu_made", "hi_made", "lo_made", "v_set", "z_made", "pass_made", "sigmoids",
                "scanned", "w_made", "ring_turned", "ring_copied", "av_done", "o_gated"))
        block = stack.enter_context(nc.Block())

        def group_no(e, g):
            return 4 * e + g

        def quarter(c):
            return slice(c * BANK, (c + 1) * BANK)

        def turn_at(pr, n):
            if pr is START:
                return n, n % 2
            place = ring_place[("turn", 1, n)]
            return pr * n_r + place, place % 2

        def weights(g, t, at, size):
            if g % 2:
                return w_odd[:, t % 4, at:at + size]
            return w_even[:, t % 4, at - BANK:at - BANK + size]

        def over_pairs(engine, run):
            run(START, first)
            with engine.Fori(0, PAIRS - 1) as pr:
                run(pr, order)
            run(LAST, [x for x in order if x[1] == 0])

        @block.sync
        def _(sp):
            sp.dma_start(bias_all[:, 0, :], b_sb.unsqueeze(0).broadcast_to([P, NH])).then_inc(bias_in, 16)

            def load_head(pair, e):
                for dst, row in ((twice_k, k_rows), (twice_q, q_rows)):
                    for half in range(2):
                        sp.dma_start(dst[half * HD:(half + 1) * HD, :],
                                     projT[ds(pair * P + (row + e * HD), HD), 0:SEQ]).then_inc(in_twice, 16)

            def load(dst, row, pair, sem):
                sp.dma_start(dst[:, :], projT[ds(pair * P + row, P), 0:SEQ]).then_inc(sem, 16)

            def store_out(pair, e):
                sp.wait_ge(o_gated, pair * 8 + (4 * e + 4 + CREDIT))
                sp.dma_start(oT[ds(pair * P + e * HD, HD), 0:SEQ], out[e * HD:(e + 1) * HD, :]
                             ).then_inc(out_stored[e], 16)

            def store_tokens(pair):
                for dst, src in ((k_out, k_tok), (v_out, v_tok)):
                    sp.dma_start(dst.rearrange("(t p) n -> p t n", p=P)[:, :, ds(pair * P, P)],
                                 src[:, :, :]).then_inc(kv_stored, 16)

            load_head(0, 0)
            load(raw_k, k_rows, 0, in_k)
            load(raw_v, v_rows, 0, in_v)
            load(raw_g, g_rows, 0, in_g)
            sp.wait_ge(lo_made, 2 * NCH)
            load_head(0, 1)
            sp.wait_ge(ring_copied, ring_first + CREDIT)
            store_tokens(0)
            with sp.Fori(0, PAIRS - 1) as pr:
                load(raw_k, k_rows + P, pr, in_k)
                load(raw_v, v_rows + P, pr, in_v)
                sp.wait_ge(silu_made, pr * NCH + NCH)
                load(raw_g, g_rows + P, pr, in_g)
                sp.wait_ge(lo_made, pr * (4 * NCH) + 4 * NCH)
                load_head(pr + 1, 0)
                store_out(pr, 0)
                sp.wait_ge(lo_made, pr * (4 * NCH) + 6 * NCH)
                load_head(pr + 1, 1)
                store_out(pr, 1)
                store_tokens(pr + 1)
            store_out(PAIRS - 1, 0)
            store_out(PAIRS - 1, 1)
            sp.wait_ge(kv_stored, 32 * PAIRS)
            for e in range(2):
                sp.wait_ge(out_stored[e], 16 * PAIRS + 1)

        @block.tensor
        def _(pe):
            pe.sem_inc(ring_turned, CREDIT)
            pe.sem_inc(av_done, CREDIT)

            def run(pr, items):
                def value_product(e, g, j):
                    x = ("a", 0, e, g, j)
                    a, lo, r = a_place[x], max(0, j - 4 * g) * P, slice(HD * e, HD * (e + 1))
                    pe.wait_ge(ring_copied, pr * n_r + (ring_at(pr, x) + 1 + CREDIT))
                    mm = pe.matmul(o_ps[r, group_no(e, g) % 2, lo:BANK], v_used[:, e, j, :], wT[:, a % 2, lo:BANK],
                                   start=(j == 4 * g + 3), stop=(j == 0), skip_group_check=True)
                    mm.then_inc(av_done, 1)

                for kind, off, *x in items:
                    if kind == "turn":
                        n, = x
                        ring, bank = turn_at(pr, n)
                        src = raw_k if n < 4 else raw_v
                        pe.wait_ge(in_k if n < 4 else in_v, pr * 16 + 32)
                        pe.wait_ge(ring_copied, ring + (CREDIT - 1))
                        for j in range(4):
                            at = ((n % 4) * 4 + j) * P
                            mm = pe.transpose(wT_ps[:, bank, j * P:(j + 1) * P], src[:, at:at + P], c.ident[:, :])
                        mm.then_inc(ring_turned, 1)
                    elif kind == "z":
                        e, t, j = x
                        lo, hi = chunks_of(t)[j]
                        n = z_at(off, e, t, j)
                        if t == 0:
                            pe.wait_ge(lo_made, pr * (4 * NCH) + (4 * off + 2 * e + 2) * NCH)
                        if not (pr is START and t < 2):
                            pe.wait_ge(sigmoids, pr * n_z + (n - 1))
                        for at in range(lo, hi, BANK):
                            size = min(BANK, hi - at)
                            dst = z_ps[:, n % 2, at - lo:at - lo + size]
                            diagonal = at + size == (t + 1) * P
                            if diagonal:
                                pe.matmul(dst[:, size - P:size], c.ident_bf[:, :], c.diag_mask[:, :], start=True,
                                          stop=False, skip_group_check=True)
                            q = q_parts[:, e, t * P:(t + 1) * P]
                            pe.matmul(dst, q, k_hi[:, e, at:at + size], start=not diagonal,
                                      stop=False, skip_group_check=True)
                            mm = pe.matmul(dst, q, k_lo[:, e, at:at + size], start=False,
                                           stop=True, skip_group_check=True)
                        mm.then_inc(z_made, 1)
                    elif kind == "a":
                        e, g, j = x
                        item = ("a", 0, e, g, j)
                        ring, gn = ring_at(pr, item), group_no(e, g)
                        is_first = j == 4 * g + 3
                        if is_first:
                            pe.wait_ge(w_made, pr * n_z + (last_z(0, e, j) + 1))
                            pe.wait_ge(o_gated, pr * 8 + (gn - 1 + CREDIT))
                            if g == 0:
                                pe.wait_ge(v_set, pr * 2 + (e + 1))
                        pe.wait_ge(ring_copied, pr * n_r + (ring - 1 + CREDIT))
                        for t in range(max(4 * g, j), 4 * g + 4):
                            at = SEQ - (t + 1) * P + j * P
                            mm = pe.transpose(wT_ps[:, ring % 2, (t % 4) * P:(t % 4 + 1) * P],
                                              weights(g, t, at, P), c.ident[:, :])
                        mm.then_inc(ring_turned, 1)
                        if not is_first:
                            value_product(e, g, j + 1)
                        if j == 0:
                            value_product(e, g, 0)
            over_pairs(pe, run)

        @block.scalar
        def _(act):
            act.sem_inc(ring_copied, CREDIT)

            def run(pr, items):
                before = pr is START
                for kind, off, *x in items:
                    if kind == "silu":
                        c, = x
                        act.wait_ge(in_g, pr * 16 + (16 * off + 16))
                        if not before:
                            act.wait_ge(o_gated, pr * 8 + (8 * off - 3 + c + CREDIT))
                        act.activation(silu[:, quarter(c)], raw_g[:, quarter(c)], ACT.Sigmoid).then_inc(sig_made, 1)
                    elif kind == "split":
                        e, c = x
                        if c == 0:
                            act.wait_ge(in_twice, pr * 128 + (128 * off + 64 * e + 64))
                            if not before:
                                act.wait_ge(z_made, pr * n_z + (last_z(0, e, NT - 1) + 1))
                        act.activation(k_hi[:, e, quarter(c)], twice_k[:, quarter(c)], ACT.Copy)
                        act.activation(q_parts[:, e, quarter(c)], twice_q[:, quarter(c)], ACT.Copy).then_inc(hi_made, 1)
                    elif kind == "turn":
                        n, = x
                        dst = k_tok if n < 4 else v_tok
                        ring, bank = turn_at(pr, n)
                        act.wait_ge(ring_turned, ring + (1 + CREDIT))
                        if not before and n == 0:
                            act.wait_ge(kv_stored, pr * 32 + 32)
                        if not before and n == 4:
                            act.wait_ge(v_set, pr * 2 + 2)
                        act.activation(dst[:, (n % 4) * 4:(n % 4) * 4 + 4, :],
                                       wT_ps[:, bank, :].rearrange("p (t n) -> p t n", n=P),
                                       ACT.Copy).then_inc(ring_copied, 1)
                    elif kind == "z":
                        e, t, j = x
                        lo, hi = chunks_of(t)[j]
                        n, at, g = z_at(off, e, t, j), SEQ - (t + 1) * P, t // 4
                        if t == 0:
                            act.wait_ge(bias_set, pr * 2 + (2 * off + e + 1))
                        if j == 0 and not before:
                            g_off, gn = divmod(off * 8 + group_no(e, g) - 2, 8)
                            act.wait_ge(ring_turned, pr * n_r + (last_ring(pr, g_off, gn // 4, gn % 4) + 1 + CREDIT))
                        if j == 0 and not (before and t < 2):
                            act.wait_ge(w_made, pr * n_z + (last_z(*tile_before(off, e, t, 2)) + 1))
                        act.wait_ge(z_made, pr * n_z + (n + 1))
                        act.activation(rest[:, t % 2, at + lo:at + hi], z_ps[:, n % 2, 0:hi - lo],
                                       ACT.Sigmoid, bias=bias[:, 1, e:e + 1], scale=-HD ** -0.5).then_inc(pass_made, 1)
                        act.activation(weights(g, t, at + lo, hi - lo), z_ps[:, n % 2, 0:hi - lo],
                                       ACT.Sigmoid, bias=bias[:, 0, e:e + 1], scale=HD ** -0.5).then_inc(sigmoids, 1)
                    else:
                        e, g, j = x
                        item = ("a", 0, e, g, j)
                        a, ring, lo = a_place[item], ring_at(pr, item), max(0, j - 4 * g) * P
                        act.wait_ge(ring_turned, pr * n_r + (ring + 1 + CREDIT))
                        act.wait_ge(av_done, pr * n_a + (a - 1 + CREDIT))
                        act.activation(wT[:, a % 2, lo:BANK], wT_ps[:, ring % 2, lo:BANK], ACT.Copy
                                       ).then_inc(ring_copied, 1)
            over_pairs(act, run)

        @block.vector
        def _(dve):
            dve.sem_inc(o_gated, CREDIT)
            for e in range(2):
                dve.sem_inc(out_stored[e], 1)
            dve.memset(zero[:, :], 0.0)
            dve.memset(rest[:, :, SEQ:], 1.0).then_inc(setup, 1)
            dve.wait_ge(bias_in, 16)
            dve.tensor_scalar(bias_all[:, 1, :], bias_all[:, 0, :], -1.0, None, ALU.mult).then_inc(setup, 1)
            dve.wait_ge(setup, 2)

            def run(pr, items):
                before = pr is START
                for kind, off, *x in items:
                    if kind == "silu":
                        c, = x
                        dve.wait_ge(sig_made, pr * NCH + (NCH * off + c + 1))
                        dve.tensor_tensor(silu[:, quarter(c)], silu[:, quarter(c)], raw_g[:, quarter(c)],
                                          ALU.mult).then_inc(silu_made, 1)
                    elif kind == "split":
                        e, c = x
                        if c == 0:
                            if not before:
                                dve.wait_ge(sigmoids, pr * n_z + (last_z(0, e, NT - 1) + 1))
                            dve.wait_ge(setup, 2)
                            dve.tensor_scalar(bias[:, :, e:e + 1], bias_all[:, :, ds(pr * 2 + (2 + e), 1)], 1.0, None,
                                              ALU.mult).then_inc(bias_set, 1)
                        dve.wait_ge(hi_made, pr * (2 * NCH) + ((2 + e) * NCH + c + 1))
                        dve.tensor_tensor(k_lo[:, e, quarter(c)], twice_k[:, quarter(c)],
                                          k_hi[:, e, quarter(c)].bitcast(F32), ALU.subtract).then_inc(lo_made, 1)
                        dve.tensor_tensor(q_parts[HD:P, e, quarter(c)], twice_q[HD:P, quarter(c)],
                                          q_parts[HD:P, e, quarter(c)].bitcast(F32), ALU.subtract).then_inc(lo_made, 1)
                    elif kind == "z":
                        e, t, j = x
                        lo, hi = chunks_of(t)[j]
                        n, at, b = z_at(off, e, t, j), SEQ - (t + 1) * P, t % 2
                        dve.wait_ge(pass_made, pr * n_z + (n + 1))
                        if not (before and t == 0):
                            dve.wait_ge(w_made, pr * n_z + n)
                        products = rest[:, b, at + lo:at + hi][:, ::-1]
                        dve.tensor_tensor_scan(products, products, zero[:, 0:1].broadcast_to([P, hi - lo]),
                                               rest[:, b, at + hi:at + hi + 1], ALU.mult, ALU.add).then_inc(scanned, 1)
                        dve.wait_ge(scanned, pr * n_z + (n + 1))
                        dve.wait_ge(sigmoids, pr * n_z + (n + 1))
                        these = weights(t // 4, t, at + lo, hi - lo)
                        dve.tensor_tensor(these, these, rest[:, b, at + lo + 1:at + hi + 1],
                                          ALU.mult).then_inc(w_made, 1)
                    elif kind == "a" and x[2] == 0:
                        e, g, _ = x
                        gn, r = group_no(e, g), slice(HD * e, HD * (e + 1))
                        if g == 0:
                            dve.wait_ge(out_stored[e], pr * 16 + 1)
                        dve.wait_ge(silu_made, pr * NCH + (g + 1))
                        dve.wait_ge(av_done, pr * n_a + (a_place[("a", 0, e, g, 0)] + 1 + CREDIT))
                        dve.tensor_tensor(out[r, g * BANK:(g + 1) * BANK], o_ps[r, gn % 2, :],
                                          silu[r, g * BANK:(g + 1) * BANK], ALU.mult).then_inc(o_gated, 1)
            over_pairs(dve, run)

        @block.gpsimd
        def _(pool):
            def use(pair, e, ring):
                pool.wait_ge(ring_copied, ring + (1 + CREDIT))
                pool.tensor_tensor(v_used[:, e, :, :], v_tok[:, :, e * HD:(e + 1) * HD],
                                   one[:, :].unsqueeze(2).broadcast_to([P, NT, HD]), ALU.mult).then_inc(v_set, 1)

            pool.memset(one[:, :], 1.0).then_inc(one_set, 1)
            pool.wait_ge(one_set, 1)
            use(0, 0, 7)
            use(0, 1, 7)
            with pool.Fori(0, PAIRS - 1) as pr:
                for e in range(2):
                    pool.wait_ge(av_done, pr * n_a + ((e + 1) * (n_a // 2) + CREDIT))
                    use(pr + 1, e, pr * n_r + ring_place[("turn", 1, 7)])


def sample_attention(nc, c, projT, b_sb, cache_k, cache_v, page_table, k_out, v_out, oT):
    n_phys = cache_k.shape[0]
    n_pages = page_table.shape[1]
    past = n_pages * PAGE
    groups = n_pages // 4
    rows = NH * TSEQ
    k_ring, v_ring, part_ring = 8, 8, 4
    blocks = D // P
    with ExitStack() as stack:
        s = Scope(nc, stack, "smp")
        newT = s.sb("newT", [P, 4 * blocks, SMP])
        silu = s.sb("silu", [P, blocks, SMP])
        new_k, new_v = s.sb("new_k", [SMP, D]), s.sb("new_v", [P, D])
        q_rows = s.sb("q_rows", [P, 2, 9 * rows])
        mask_all = s.sb("mask_all", [P, NSEQ, SMP], BF16)
        mask_tokens = s.sb("mask_tokens", [TSEQ, NSEQ, SMP], BF16)
        mask = s.sb("mask", [P, 2, SMP], BF16)
        mask_dram = nc.dram_tensor("mask_dram", (TSEQ, NSEQ * SMP), BF16).ap()
        table = s.sb("table", [1, NSEQ * n_pages], I32)
        k_pages, v_pages = s.sb("k_pages", [P, k_ring, D]), s.sb("v_pages", [P, v_ring, D])
        v_hi, v_lo = (s.sb(n, [P, part_ring, D], F32R) for n in ("v_hi", "v_lo"))
        new_v_hi, new_v_lo = (s.sb(n, [P, D], F32R) for n in ("new_v_hi", "new_v_lo"))
        kT = s.sb("kT", [P, 2, blocks, BANK])
        w = s.sb("w", [P, past + P])
        pass_on = s.sb("pass_on", [rows, 2, BANK])
        rest = s.sb("rest", [rows, past + SMP + 1])
        zeros = s.sb("zeros", [rows, BANK])
        wT = s.sb("wT", [P, 2, 4, 2 * rows], F32R)
        o = s.sb("o", [P, D])
        fold = s.sb("fold", [P, rows])
        out = s.sb("out", [P, blocks, SMP])
        bias = s.sb("bias", [rows, 2])
        kT_ps = s.ps("kT_acc", [P, 2, D])
        z_ps, wT_ps, o_ps = s.ps("z", [P, BANK]), s.ps("wT_acc", [P, BANK]), s.ps("o_acc", [P, D])
        once, table_in, mask_moved, kv_stored, out_stored = (s.sem(n) for n in (
            "once_in", "table_in", "mask_moved", "kv_stored", "out_stored"))
        k_in, v_in = s.sems("k_in", k_ring), s.sems("v_in", v_ring)
        v_hi_made, v_lo_made, w_lo_made = (s.sem(n) for n in ("v_hi_made", "v_lo_made", "w_lo_made"))
        new_parts, pass_made = s.sem("new_parts"), s.sem("pass_made")
        setup, masks, new_turned, new_copied, q_made, k_turned, act_copied, dve_copied, z_made, sigmoids, scanned, \
            w_made, w_turned, wT_copied, v_used, o_copied, folded, gated = (s.sem(n) for n in (
                "setup", "masks", "new_turned", "new_copied", "q_made", "k_turned", "act_copied", "dve_copied",
                "z_made", "sigmoids", "scanned", "w_made", "w_turned", "wT_copied", "v_used", "o_copied",
                "folded", "gated"))
        n_w = groups + 1
        half = blocks // 2

        with nc.Block() as block:
            @block.sync
            def _(sp):
                sp.dma_start(newT[:, :, :], projT.rearrange("(b p) n -> p b n", p=P)[:, :, SEQ:TOK]).then_inc(once, 16)
                sp.dma_start(bias[:, 0:1], b_sb.unsqueeze(1).unsqueeze(1).broadcast_to([NH, TSEQ, 1]),
                             allow_slow_non_contiguous=True).then_inc(once, 16)
                sp.dma_start(table[:, :], page_table.rearrange("(o s) n -> o (s n)", o=1)).then_inc(table_in, 16)
                sp.wait_ge(masks, 4)
                sp.dma_start(mask_dram, mask_tokens[:, :, :].rearrange("p s n -> p (s n)")).then_inc(mask_moved, 16)
                sp.wait_ge(mask_moved, 16)
                sp.dma_start(mask_all[0:rows, :, :].rearrange("p s n -> p (s n)"),
                             mask_dram.unsqueeze(0).broadcast_to([NH, TSEQ, NSEQ * SMP])).then_inc(mask_moved, 16)
                sp.wait_ge(new_copied, 4)
                sp.dma_start(k_out, new_k[:, :]).then_inc(kv_stored, 16)
                sp.dma_start(v_out, new_v[0:SMP, :]).then_inc(kv_stored, 16)
                sp.wait_ge(kv_stored, 32)
                sp.wait_ge(table_in, 16)
                sp.wait_ge(mask_moved, 32)

            @block.gpsimd
            def _(pool):
                pool.memset(mask_tokens[:, :, :], 0.0).then_inc(masks, 1)
                pool.memset(mask_all[:, :, :], 0.0).then_inc(masks, 1)
                pool.wait_ge(masks, 2)
                pool.affine_select(out=mask_tokens[:, :, :], in_=mask_tokens[:, :, :], compare_op=ALU.is_ge,
                                   fill=MASKED, base=0, pattern=[[-TSEQ, NSEQ], [1, SMP]],
                                   channel_multiplier=0).then_inc(masks, 1)
                pool.wait_ge(masks, 3)
                pool.affine_select(out=mask_tokens[:, :, :], in_=mask_tokens[:, :, :], compare_op=ALU.is_gt,
                                   fill=MASKED, base=0, pattern=[[TSEQ, NSEQ], [-1, SMP]],
                                   channel_multiplier=1).then_inc(masks, 1)

            @block.vector
            def _(dve):
                dve.memset(q_rows[:, :, :], 0.0)
                dve.memset(new_v[:, :], 0.0)
                dve.memset(w[:, :], 0.0)
                dve.memset(zeros[:, :], 0.0)
                dve.memset(rest[:, past + SMP:], 1.0).then_inc(setup, 1)
                dve.wait_ge(once, 32)
                dve.tensor_scalar(bias[:, 1:2], bias[:, 0:1], -1.0, None, ALU.mult).then_inc(setup, 1)
                dve.wait_ge(setup, 2)
                for n in range(4):
                    dve.wait_ge(new_turned, n + 1)
                    dst = (new_k if n < 2 else new_v)[0:SMP, (n % 2) * BANK:(n % 2 + 1) * BANK]
                    dve.tensor_copy(dst, kT_ps[0:SMP, n // 2, (n % 2) * BANK:(n % 2 + 1) * BANK]).then_inc(new_copied, 1)
                dve.wait_ge(new_copied, 4)
                dve.tensor_copy(new_v_hi[:, :], new_v[:, :]).then_inc(new_parts, 1)
                dve.wait_ge(new_parts, 1)
                dve.tensor_tensor(new_v_lo[:, :], new_v[:, :], new_v_hi[:, :].bitcast(F32), ALU.subtract)
                dve.tensor_tensor(fold[:, :], c.ident[:, 0:rows], c.ident[:, rows:P], ALU.add).then_inc(new_parts, 1)
                dve.wait_ge(setup, 3)
                dve.tensor_tensor(silu[:, :, :], silu[:, :, :], newT[:, 3 * blocks:, :], ALU.mult).then_inc(setup, 1)

            @block.scalar
            def _(act):
                act.wait_ge(once, 32)
                act.wait_ge(setup, 2)
                act.activation(silu[:, :, :], newT[:, 3 * blocks:, :], ACT.Sigmoid).then_inc(setup, 1)

            @block.tensor
            def _(pe):
                pe.wait_ge(once, 32)
                for n in range(4):
                    for j in range(4):
                        mm = pe.transpose(kT_ps[0:SMP, n // 2, (n % 2) * BANK + j * P:(n % 2) * BANK + (j + 1) * P],
                                          newT[:, 4 * n + j, :], c.ident[:, :])
                    mm.then_inc(new_turned, 1)

        block = stack.enter_context(nc.Block())

        def over_sequences(engine, step):
            with engine.Fori(0, NSEQ // 2 - 1) as i:
                step(i * 2, i, 0, True)
                step(i * 2 + 1, i, 1, True)
            step(NSEQ - 2, NSEQ // 2 - 1, 0, True)
            step(NSEQ - 1, NSEQ // 2 - 1, 1, False)

        def over_pages(q, n, follows, keys, values, in_turn):
            for turn in range(4 if in_turn else 1):
                pages = [turn] if in_turn else range(4)
                for p in pages:
                    if n + 1 < groups:
                        keys(q, 4 * (n + 1) + p)
                    elif n == groups and follows:
                        keys(q + 1, p)
                for p in pages:
                    values(p)

        def half_read(g):
            return g + 2 if g >= 2 else g + 1

        def page_of(m):
            return (groups - 1 - m // 4) * 4 + m % 4

        @block.sync
        def _(sp):
            def step(q, i, b, follows):
                for m in range(n_pages):
                    page = sp.value_load(table[0:1, ds(q * n_pages + page_of(m), 1)], min_val=0, max_val=n_phys - 1)
                    sp.wait_ge(k_turned, q * n_pages + (m + 1))
                    sp.wait_ge(table_in, 16)
                    sp.dma_start(k_pages[:, m % k_ring, :], cache_k.rearrange("g t h d -> (g t) (h d)")
                                 [ds(page * PAGE, PAGE), :]).then_inc(k_in[m % k_ring], 16)
                    sp.wait_ge(v_lo_made, q * n_pages + (m + 1))
                    sp.wait_ge(table_in, 16)
                    sp.dma_start(v_pages[:, m % v_ring, :], cache_v.rearrange("g t h d -> (g t) (h d)")
                                 [ds(page * PAGE, PAGE), :]).then_inc(v_in[m % v_ring], 16)
            over_sequences(sp, step)
            sp.wait_ge(gated, NSEQ + 1)
            sp.dma_start(oT.rearrange("(b p) n -> p b n", p=P)[:, :, SEQ:TOK], out[:, :, :]).then_inc(out_stored, 16)
            sp.wait_ge(out_stored, 16)

        @block.tensor
        def _(pe):
            pe.sem_inc(k_turned, k_ring)
            pe.sem_inc(v_used, part_ring)
            pe.sem_inc(z_made, 2)
            pe.sem_inc(folded, 2)
            per_lap = n_pages // k_ring

            def turn_keys(q, m):
                pe.wait_ge(k_in[m % k_ring], q * (16 * per_lap) + 16 * (m // k_ring + 1))
                pe.wait_ge(act_copied, q * n_pages + (m + 1))
                pe.wait_ge(dve_copied, q * n_pages + (m + 1))
                for hp in range(blocks):
                    mm = pe.transpose(kT_ps[:, m % 2, hp * P:(hp + 1) * P],
                                      k_pages[:, m % k_ring, hp * P:(hp + 1) * P], c.ident[:, :])
                mm.then_inc(k_turned, 1)

            for m in range(4):
                turn_keys(0, m)

            def step(q, i, b, follows):
                def logits(n):
                    pe.wait_ge(sigmoids, q * n_w + (n + 1))
                    if n == 0:
                        pe.wait_ge(gated, q + 1)
                        pe.wait_ge(q_made, q * 3 + 3)
                        pe.matmul(z_ps[0:rows, 0:SMP], c.ident_bf[:, 0:rows], mask[:, b, :], start=True, stop=False)
                        for hp in range(blocks):
                            mm = pe.matmul(z_ps[0:rows, 0:SMP], q_rows[:, b, hp * rows:(hp + 1) * rows], newT[:, hp, :],
                                           start=False, stop=(hp == blocks - 1))
                    else:
                        pe.wait_ge(act_copied, q * n_pages + (4 * n + 2))
                        pe.wait_ge(dve_copied, q * n_pages + (4 * n + 2))
                        for hp in range(blocks):
                            mm = pe.matmul(z_ps[0:rows, :], q_rows[:, b, hp * rows:(hp + 1) * rows],
                                           kT[:, (n - 1) % 2, hp, :], start=(hp == 0), stop=(hp == blocks - 1))
                    mm.then_inc(z_made, 1)

                def turn_weights(n):
                    pe.wait_ge(w_made, q * n_w + (n + 1))
                    pe.wait_ge(w_lo_made, q * n_w + (n + 1))
                    if n == 0:
                        mm = pe.transpose(wT_ps[:, 0:P], w[:, past:past + P], c.ident[:, :])
                    else:
                        for p in range(4):
                            at = page_of(4 * (n - 1) + p) * PAGE
                            mm = pe.transpose(wT_ps[:, p * P:(p + 1) * P], w[:, at:at + PAGE], c.ident[:, :])
                    mm.then_inc(w_turned, 1)

                def values(n, p):
                    if p == 0:
                        pe.wait_ge(w_lo_made, q * n_w + (n + 2))
                    if n == 0 and p > 0:
                        return
                    if n == 0:
                        pe.wait_ge(o_copied, q + 1)
                    m = 4 * (n - 1) + p
                    if n > 0:
                        pe.wait_ge(v_lo_made, q * n_pages + (m + 1 + v_ring))
                    for j in range(D // BANK):
                        for part, (new, page) in enumerate(((new_v_hi, v_hi), (new_v_lo, v_lo))):
                            src = new if n == 0 else page[:, m % part_ring, :]
                            mm = pe.matmul(o_ps[:, j * BANK:(j + 1) * BANK], wT[:, (n + b) % 2, p, :],
                                           src[:, j * BANK:(j + 1) * BANK], start=(n == 0 and part == 0),
                                           stop=(n == groups and p == 3 and part == 1))
                    if n > 0:
                        mm.then_inc(v_used, 1)

                logits(0)
                for n in range(n_w):
                    if n > 0:
                        turn_weights(n)
                    if n + 1 < n_w:
                        logits(n + 1)
                    if n == 0:
                        turn_weights(0)
                    over_pages(q, n, follows, turn_keys, lambda p: values(n, p), in_turn=True)
                pe.wait_ge(v_used, q * n_pages + (n_pages + part_ring))
                pe.wait_ge(o_copied, q + 2)
                for h in range(NH):
                    e, hp = h % 2, h // 2
                    mm = pe.matmul(z_ps[HD * e:HD * (e + 1), hp * TSEQ:(hp + 1) * TSEQ],
                                   o[:, h * HD:(h + 1) * HD], fold[:, h * TSEQ:(h + 1) * TSEQ],
                                   start=True, stop=True)
                mm.then_inc(folded, 1)
            over_sequences(pe, step)

        @block.scalar
        def _(act):
            act.sem_inc(act_copied, 2)
            act.sem_inc(sigmoids, 1)
            act.sem_inc(o_copied, 1)

            def copy_keys(q, m):
                act.wait_ge(k_turned, q * n_pages + (m + 1 + k_ring))
                if m % 4 == 0:
                    act.wait_ge(z_made, q * n_w + half_read(m // 4))
                act.activation(kT[:, m // 4 % 2, 0:half, m % 4 * P:(m % 4 + 1) * P],
                               kT_ps[:, m % 2, 0:BANK].rearrange("p (h n) -> p h n", n=P),
                               ACT.Copy).then_inc(act_copied, 1)

            for m in range(4):
                copy_keys(0, m)

            def step(q, i, b, follows):
                def sigmoid(n):
                    act.wait_ge(z_made, q * n_w + (n + 3))
                    size = SMP if n == 0 else BANK
                    at = past if n == 0 else (groups - n) * BANK
                    act.wait_ge(scanned, q * n_w + (n + 1))
                    act.wait_ge(v_used, q * n_pages + part_ring)
                    act.activation(pass_on[:, (n + b) % 2, 0:size], z_ps[0:rows, 0:size], ACT.Sigmoid, bias=bias[:, 1:2],
                                   scale=-HD ** -0.5).then_inc(pass_made, 1)
                    act.activation(w[0:rows, at:at + size], z_ps[0:rows, 0:size], ACT.Sigmoid, bias=bias[:, 0:1],
                                   scale=HD ** -0.5).then_inc(sigmoids, 1)

                def copy_weights(n):
                    act.wait_ge(w_turned, q * n_w + (n + 1))
                    m = 1 if n == 0 else 4
                    act.activation(wT[:, (n + b) % 2, 0:m, 0:rows],
                                   wT_ps[:, 0:m * P].rearrange("p (m n) -> p m n", n=P)[:, :, 0:rows],
                                   ACT.Copy).then_inc(wT_copied, 1)

                def split_values(n, p):
                    if n > groups:
                        return
                    m = 4 * (n - 1) + p
                    act.wait_ge(v_in[m % v_ring], q * (16 * (n_pages // v_ring)) + 16 * (m // v_ring + 1))
                    act.wait_ge(v_used, q * n_pages + (m + 1))
                    act.activation(v_hi[:, m % part_ring, :], v_pages[:, m % v_ring, :], ACT.Copy
                                   ).then_inc(v_hi_made, 1)

                sigmoid(0)
                for n in range(n_w):
                    if n > 0:
                        copy_weights(n)
                    if n + 1 < n_w:
                        sigmoid(n + 1)
                    if n == 0:
                        copy_weights(0)
                    over_pages(q, n, follows, copy_keys, lambda p: split_values(n + 1, p), in_turn=False)
                act.wait_ge(v_used, q * n_pages + (n_pages + part_ring))
                act.wait_ge(folded, q + 2)
                act.activation(o[:, :], o_ps[:, :], ACT.Copy).then_inc(o_copied, 1)
            over_sequences(act, step)

        @block.vector
        def _(dve):
            dve.sem_inc(dve_copied, 2)
            dve.sem_inc(scanned, 2)
            dve.sem_inc(gated, 1)
            dve.sem_inc(w_lo_made, 1)
            dve.sem_inc(v_lo_made, v_ring)

            def copy_keys(q, m):
                dve.wait_ge(k_turned, q * n_pages + (m + 1 + k_ring))
                if m % 4 == 0:
                    dve.wait_ge(z_made, q * n_w + half_read(m // 4))
                dve.tensor_copy(kT[:, m // 4 % 2, half:blocks, m % 4 * P:(m % 4 + 1) * P],
                                kT_ps[:, m % 2, BANK:D].rearrange("p (h n) -> p h n", n=P)).then_inc(dve_copied, 1)

            for m in range(4):
                copy_keys(0, m)

            def step(q, i, b, follows):
                cols = ds(q * TSEQ, TSEQ)

                def queries():
                    dve.wait_ge(folded, q + 1)
                    view = q_rows[:, b, :].rearrange("p (h n) -> p h n", n=rows + 2 * TSEQ)
                    qT = newT[:, 2 * blocks:3 * blocks, :]
                    dve.tensor_scalar(view[0:HD, :, 0:TSEQ], qT[0:HD, :, cols], 1.0, None, ALU.mult).then_inc(q_made, 1)
                    dve.tensor_scalar(view[HD:P, :, TSEQ:2 * TSEQ], qT[HD:P, :, cols], 1.0, None,
                                      ALU.mult).then_inc(q_made, 1)
                    dve.tensor_scalar(mask[:, b, :], mask_all[:, ds(q, 1), :].rearrange("p o n -> p (o n)"), 1.0, None,
                                      ALU.mult).then_inc(q_made, 1)

                def weights(n):
                    size = SMP if n == 0 else BANK
                    at = past if n == 0 else (groups - n) * BANK
                    dve.wait_ge(pass_made, q * n_w + (n + 1))
                    if n > 0:
                        dve.wait_ge(w_made, q * n_w + n)
                    dve.tensor_tensor_scan(rest[:, at:at + size][:, ::-1], pass_on[:, (n + b) % 2, 0:size][:, ::-1],
                                           zeros[:, 0:size], rest[:, at + size:at + size + 1], ALU.mult,
                                           ALU.add).then_inc(scanned, 1)
                    dve.wait_ge(scanned, q * n_w + (n + 3))
                    dve.wait_ge(sigmoids, q * n_w + (n + 2))
                    dve.tensor_tensor(w[0:rows, at:at + size], w[0:rows, at:at + size], rest[:, at + 1:at + size + 1],
                                      ALU.mult).then_inc(w_made, 1)

                def split_weights(n):
                    m = 1 if n == 0 else 4
                    dve.wait_ge(wT_copied, q * n_w + (n + 1))
                    dve.tensor_tensor(wT[:, (n + b) % 2, 0:m, rows:],
                                      wT_ps[:, 0:m * P].rearrange("p (m n) -> p m n", n=P)[:, :, 0:rows],
                                      wT[:, (n + b) % 2, 0:m, 0:rows].bitcast(F32), ALU.subtract).then_inc(w_lo_made, 1)

                def split_values(n, p):
                    if n > groups:
                        return
                    m = 4 * (n - 1) + p
                    dve.wait_ge(v_hi_made, q * n_pages + (m + 1))
                    dve.tensor_tensor(v_lo[:, m % part_ring, :], v_pages[:, m % v_ring, :],
                                      v_hi[:, m % part_ring, :].bitcast(F32), ALU.subtract).then_inc(v_lo_made, 1)

                queries()
                weights(0)
                for n in range(n_w):
                    if n > 0:
                        split_weights(n)
                    if n + 1 < n_w:
                        weights(n + 1)
                    if n == 0:
                        split_weights(0)
                    over_pages(q, n, follows, copy_keys, lambda p: split_values(n + 1, p), in_turn=False)
                dve.wait_ge(folded, q + 3)
                dve.tensor_tensor(out[:, :, cols], z_ps[:, 0:blocks * TSEQ].rearrange("p (h n) -> p h n", n=TSEQ), silu[:, :, cols],
                                  ALU.mult).then_inc(gated, 1)
            over_sequences(dve, step)


def trunk(nc, x_prompt, x_sample, state_gla, cache_k, cache_v, page_table, g_norm_a, w_in_a, w_alpha2, b_alpha,
          g_head_a, w_out_a, g_kv, w_kv, g_norm_b, w_in_b, b_sb, w_out_b, g_final, y_prompt, y_sample,
          state_prompt, state_sample, k_prompt, v_prompt, k_sample, v_sample):
    def rows(a):
        return a.rearrange("a b d -> (a b) d")

    def tile_of(prompt, sample):
        return lambda t: sample if is_sample(t) else prompt[ds(t * P, P), :]

    def heads(a):
        return a.rearrange("a t h d -> (a t) (h d)")

    xnT, oT = (nc.dram_tensor(n, (D, TOK), F32).ap() for n in ("xnT", "oT"))
    o_gla, h_mid = (nc.dram_tensor(n, (TOK, D), F32).ap() for n in ("o_gla", "h_mid"))
    proj_a = nc.dram_tensor("proj_a", (w_in_a.shape[2], TOK), F32).ap()
    proj_b = nc.dram_tensor("proj_b", (4 * D, TOK), F32).ap()
    x_of = tile_of(rows(x_prompt), rows(x_sample))
    h_of = tile_of(h_mid[0:SEQ, :], h_mid[SEQ:TOK, :])

    class Constants:
        pass

    with ExitStack() as stack:
        c = Constants()
        c.scope = Scope(nc, stack, "const")
        build_constants(nc, c)
        normalise(nc, c, x_of, xnT)
        full = w_in_a.shape[2] // P
        project(nc, c, "proja", xnT, [(w_in_a[0], g_norm_a[0], full, proj_a, 0)], tail=w_in_a.shape[2] - full * P)
        gla(nc, c, proj_a, w_alpha2[0], b_alpha[0], g_head_a[0], state_gla[0], state_prompt[0, 0], state_sample[0],
            o_gla)
        out_project(nc, c, "outa", o_gla, False, w_out_a[0], x_of, h_of, xnT=xnT)
        project(nc, c, "projb", xnT, [(w_kv, g_kv, 2 * D // P, proj_b, 0), (w_in_b[0], g_norm_b[0], 2 * D // P,
                                                                           proj_b, 2 * D)])
        prompt_attention(nc, c, proj_b, b_sb[0], heads(k_prompt), heads(v_prompt), oT)
        sample_attention(nc, c, proj_b, b_sb[0], cache_k, cache_v, page_table, heads(k_sample), heads(v_sample), oT)
        out_project(nc, c, "outb", oT, True, w_out_b[0], h_of, None, gain=g_final,
                    y_out=tile_of(rows(y_prompt), rows(y_sample)))


INPUTS = ("x_prompt", "x_sample", "state_gla", "cache_k", "cache_v", "page_table", "g_norm_a", "w_in_a", "w_alpha2",
          "b_alpha", "g_head_a", "w_out_a", "g_kv", "w_kv", "g_norm_b", "w_in_b", "b_sb", "w_out_b", "g_final")
OUTPUTS = (("y_prompt", (1, SEQ, D)), ("y_sample", (NSEQ, TSEQ, D)), ("state_gla_prompt", (1, 1, GH, DK, DV)),
           ("state_gla_sample", (1, NSEQ, GH, DK, DV)), ("k_prompt", (1, SEQ, NH, HD)), ("v_prompt", (1, SEQ, NH, HD)),
           ("k_sample", (NSEQ, TSEQ, NH, HD)), ("v_sample", (NSEQ, TSEQ, NH, HD)))


def kernel(**inputs):
    import concourse.bacc as bacc
    from concourse.bass_utils import run_bass_kernel_spmd

    nc = bacc.Bacc("TRN2", target_bir_lowering=False, num_devices=1)
    arrays, args = {}, []
    for name in INPUTS:
        a = np.ascontiguousarray(inputs[name])
        arrays[f"in_{name}"] = a
        args.append(nc.dram_tensor(f"in_{name}", a.shape, mybir.dt.from_np(a.dtype), kind="ExternalInput").ap())
    for name, shape in OUTPUTS:
        args.append(nc.dram_tensor(f"out_{name}", shape, F32, kind="ExternalOutput").ap())
    trunk(nc, *args)
    result = run_bass_kernel_spmd(nc, [arrays], core_ids=[0])
    return tuple(result.results[0][f"out_{name}"] for name, _ in OUTPUTS)
```
